# Optimizing a Trainium2 kernel written in Bass

```python
import math
import jax
import jax.numpy as jnp
from jax import lax
import numpy as np

D_MODEL = 1024
BATCH = 1
SEQ = 512
DEPTH = 2
DEC_BATCH = 8
DEC_SEQ = 4
PAST_LEN = 2048
PAGE_SIZE = 128

HG_HEADS = 4
HG_DK = 128
HG_DV = 128
HG_CHUNK = 64
DA_HEADS = 4
DA_DK = 64
DA_DV = 2 * DA_DK
Q_BLOCK = 128
ROPE_THETA = 500000.0
ROT_DIM = DA_DK // 4
N_GROUPS = 4
EXPERTS_PER_GROUP = 4
N_EXPERTS = N_GROUPS * EXPERTS_PER_GROUP
TOP_K_IN_GROUP = 2
EXPERT_FF = D_MODEL // 2
NORM_EPS = 1e-6
NEG = -1e30
F_MIN = 1e-30

HG_OUT = HG_HEADS * HG_DV
DA_OUT = DA_HEADS * DA_DV
MIX_WIDTH = HG_OUT + DA_OUT
_W = [HG_HEADS * HG_DK, HG_HEADS * HG_DK, HG_HEADS * HG_DV, HG_HEADS * HG_DV,
      DA_HEADS * 2 * DA_DK, DA_HEADS * 2 * DA_DK, DA_HEADS * DA_DV]
IN_SPLITS = [int(v) for v in np.cumsum(_W)[:-1]]
IN_WIDTH = int(sum(_W))

kernel_name = "hymba_hgrn2_diffattn_hmoe_step"

def rms_norm(x, w):
    xf = x.astype(jnp.float32)
    y = xf * lax.rsqrt(jnp.mean(xf * xf, axis=-1, keepdims=True) + NORM_EPS)
    return (y * w.astype(jnp.float32)).astype(x.dtype)

def rope(x, pos):
    half = ROT_DIM // 2
    inv = ROPE_THETA ** (-jnp.arange(0, ROT_DIM, 2, dtype=jnp.float32) / ROT_DIM)
    ang = pos.astype(jnp.float32)[:, None] * inv[None, :]
    cos = jnp.cos(ang)[:, None, None, :]
    sin = jnp.sin(ang)[:, None, None, :]
    xr = x[..., :ROT_DIM].astype(jnp.float32)
    x1, x2 = xr[..., :half], xr[..., half:]
    rot = jnp.concatenate([x1 * cos - x2 * sin, x2 * cos + x1 * sin], axis=-1)
    return jnp.concatenate([rot.astype(x.dtype), x[..., ROT_DIM:]], axis=-1)

def project(xn, w_in, lb, pos):
    b, t, _ = xn.shape
    z = xn @ w_in
    hq, hf, hi, hg, dq, dk, dv = jnp.split(z, IN_SPLITS, axis=-1)
    f32 = jnp.float32
    q_h = hq.reshape(b, t, HG_HEADS, HG_DK).astype(f32) * HG_DK ** -0.5
    f_raw = hf.reshape(b, t, HG_HEADS, HG_DK).astype(f32)
    f = lb + (1.0 - lb) * jax.nn.sigmoid(f_raw)
    log_f = jnp.log(jnp.maximum(f, F_MIN))
    k_h = (1.0 - lb) * jax.nn.sigmoid(-f_raw)
    i_h = hi.reshape(b, t, HG_HEADS, HG_DV).astype(f32)
    q_d = rope(dq.reshape(b, t, DA_HEADS, 2, DA_DK), pos)
    k_d = rope(dk.reshape(b, t, DA_HEADS, 2, DA_DK), pos)
    v_d = dv.reshape(b, t, DA_HEADS, DA_DV)
    return q_h, k_h, i_h, log_f, hg, q_d, k_d, v_d

def hgrn2_recurrence(q, k, v, log_f, s0):
    b, t = q.shape[:2]
    c = HG_CHUNK if t % HG_CHUNK == 0 else t
    n = t // c

    def to_chunks(a):
        return a.reshape((b, n, c) + a.shape[2:]).swapaxes(0, 1)

    tri = jnp.tril(jnp.ones((c, c), dtype=bool))[None, :, :, None, None]

    def step(s, inp):
        qc, kc, vc, gc = inp
        g = jnp.cumsum(gc, axis=1)
        o_inter = jnp.einsum('bthk,bhkv->bthv', qc * jnp.exp(g), s)
        diff = g[:, :, None] - g[:, None, :]
        decay = jnp.where(tri, jnp.exp(jnp.minimum(diff, 0.0)), 0.0)
        a = jnp.einsum('bthk,btshk,bshk->bths', qc, decay, kc)
        o_intra = jnp.einsum('bths,bshv->bthv', a, vc)
        g_last = g[:, -1]
        s_new = jnp.exp(g_last)[..., None] * s + jnp.einsum(
            'bshk,bshv->bhkv', kc * jnp.exp(g_last[:, None] - g), vc)
        return s_new, o_inter + o_intra

    xs = (to_chunks(q), to_chunks(k), to_chunks(v), to_chunks(log_f))
    s_fin, o = lax.scan(step, s0, xs)
    return o.swapaxes(0, 1).reshape(b, t, HG_HEADS, HG_DV), s_fin

def diff_attn_core(q, qpos, segs, lam):
    scale = DA_DK ** -0.5
    scores = []
    for k, v, kpos in segs:
        s = jnp.einsum('bqhcd,bkhcd->bhcqk', q, k).astype(jnp.float32) * scale
        scores.append(jnp.where(kpos[None, :] <= qpos[:, None], s, NEG))
    p = jax.nn.softmax(jnp.concatenate(scores, axis=-1), axis=-1)
    a = p[:, :, 0] - lam * p[:, :, 1]
    outs = []
    off = 0
    for k, v, kpos in segs:
        nk = k.shape[1]
        outs.append(jnp.einsum('bhqk,bkhd->bqhd', a[..., off:off + nk], v.astype(jnp.float32)))
        off += nk
    return sum(outs)

def diff_attn_prompt(q, k, v, pos, lam):
    b, s = q.shape[:2]
    nb = s // Q_BLOCK
    qb = q.reshape(b, nb, Q_BLOCK, DA_HEADS, 2, DA_DK).swapaxes(0, 1)
    starts = jnp.arange(nb, dtype=jnp.int32) * Q_BLOCK

    def blk(args):
        qblk, start = args
        qpos = start + jnp.arange(Q_BLOCK, dtype=jnp.int32)
        return diff_attn_core(qblk, qpos, [(k, v, pos)], lam)

    out = lax.map(blk, (qb, starts))
    return out.swapaxes(0, 1).reshape(b, s, DA_HEADS, DA_DV)

def hier_moe(xn, w_r1, b_r1, w_r2, b_r2, w_gate, w_up, w_down):
    b, t, d = xn.shape
    xt = xn.reshape(-1, d)
    n = xt.shape[0]
    lg1 = (xt @ w_r1 + b_r1).astype(jnp.float32)
    p1 = jax.nn.softmax(lg1, axis=-1)
    grp = jnp.argmax(lg1, axis=-1)
    p_grp = jnp.take_along_axis(p1, grp[:, None], axis=-1)[:, 0]
    lg2 = (xt @ w_r2 + b_r2).astype(jnp.float32).reshape(n, N_GROUPS, EXPERTS_PER_GROUP)
    lg2g = jnp.take_along_axis(lg2, grp[:, None, None], axis=1)[:, 0]
    top_v, top_i = lax.top_k(lg2g, TOP_K_IN_GROUP)
    w2 = jax.nn.softmax(top_v, axis=-1)
    within = jnp.einsum('nk,nke->ne', w2, jax.nn.one_hot(top_i, EXPERTS_PER_GROUP, dtype=jnp.float32))
    gates = (p_grp[:, None, None] * jax.nn.one_hot(grp, N_GROUPS, dtype=jnp.float32)[:, :, None]
             * within[:, None, :]).reshape(n, N_EXPERTS).astype(xt.dtype)
    y = jnp.zeros_like(xt)
    for e in range(N_EXPERTS):
        h = jax.nn.silu(xt @ w_gate[e]) * (xt @ w_up[e])
        y = y + (h * gates[:, e:e + 1]) @ w_down[e]
    return y.reshape(b, t, d)

def trunk_layer(h, pos, s0, past, lam, lam_init, lb, attn_norm_w, w_in, hgrn_norm_w,
                diff_norm_w, w_o, ffn_norm_w, w_r1, b_r1, w_r2, b_r2, w_gate, w_up, w_down):
    b, t, _ = h.shape
    xn = rms_norm(h, attn_norm_w)
    q_h, k_h, i_h, log_f, g_h, q_d, k_d, v_d = project(xn, w_in, lb, pos)
    o_h, s_fin = hgrn2_recurrence(q_h, k_h, i_h, log_f, s0)
    if past is None:
        o_d = diff_attn_prompt(q_d, k_d, v_d, pos, lam)
    else:
        k_past, v_past, kpos_past = past
        o_d = diff_attn_core(q_d, pos, [(k_past, v_past, kpos_past), (k_d, v_d, pos)], lam)
    g = jax.nn.sigmoid(g_h.astype(jnp.float32)).reshape(b, t, HG_HEADS, HG_DV)
    oh = rms_norm(o_h, hgrn_norm_w) * g
    od = rms_norm(o_d, diff_norm_w) * (1.0 - lam_init)
    o = jnp.concatenate([oh.reshape(b, t, HG_OUT), od.reshape(b, t, DA_OUT)], axis=-1).astype(h.dtype)
    h = h + o @ w_o
    h = h + hier_moe(rms_norm(h, ffn_norm_w), w_r1, b_r1, w_r2, b_r2, w_gate, w_up, w_down)
    k_rows = k_d.reshape(b, t, DA_HEADS, 2 * DA_DK)
    return h, k_rows, v_d, s_fin

def setup_inputs(seed: int = 0) -> dict:
    key = jax.random.key(seed)
    ks = jax.random.split(key, 24)
    f32 = jnp.float32
    n_pages = PAST_LEN // PAGE_SIZE
    n_used = DEC_BATCH * n_pages
    n_pool = n_used + n_used // 4

    def nrm(k, shape, s):
        return jax.random.normal(k, shape, f32) * s

    page_table = jax.random.permutation(ks[5], n_pool)[:n_used].reshape(DEC_BATCH, n_pages).astype(jnp.int32)
    return {
        "x_prompt": nrm(ks[0], (BATCH, SEQ, D_MODEL), 1.0),
        "x_sample": nrm(ks[1], (DEC_BATCH, DEC_SEQ, D_MODEL), 1.0),
        "cache_k": nrm(ks[2], (DEPTH, n_pool, PAGE_SIZE, DA_HEADS, 2 * DA_DK), 1.0),
        "cache_v": nrm(ks[3], (DEPTH, n_pool, PAGE_SIZE, DA_HEADS, DA_DV), 1.0),
        "state_hgrn": nrm(ks[4], (DEPTH, DEC_BATCH, HG_HEADS, HG_DK, HG_DV), 0.5),
        "page_table": page_table,
        "attn_norm_w": 1.0 + nrm(ks[6], (DEPTH, D_MODEL), 0.02),
        "w_in": nrm(ks[7], (DEPTH, D_MODEL, IN_WIDTH), D_MODEL ** -0.5),
        "hgrn_lb": nrm(ks[8], (DEPTH, HG_HEADS * HG_DK), 0.5),
        "hgrn_norm_w": 1.0 + nrm(ks[9], (DEPTH, HG_DV), 0.02),
        "diff_lambda": nrm(ks[10], (DEPTH, 4, DA_DK), 0.1),
        "diff_norm_w": 1.0 + nrm(ks[11], (DEPTH, DA_DV), 0.02),
        "w_o": nrm(ks[12], (DEPTH, MIX_WIDTH, D_MODEL), MIX_WIDTH ** -0.5),
        "ffn_norm_w": 1.0 + nrm(ks[13], (DEPTH, D_MODEL), 0.02),
        "w_r1": nrm(ks[14], (DEPTH, D_MODEL, N_GROUPS), D_MODEL ** -0.5),
        "b_r1": nrm(ks[15], (DEPTH, N_GROUPS), 0.01),
        "w_r2": nrm(ks[16], (DEPTH, D_MODEL, N_EXPERTS), D_MODEL ** -0.5),
        "b_r2": nrm(ks[17], (DEPTH, N_EXPERTS), 0.01),
        "w_gate": nrm(ks[18], (DEPTH, N_EXPERTS, D_MODEL, EXPERT_FF), D_MODEL ** -0.5),
        "w_up": nrm(ks[19], (DEPTH, N_EXPERTS, D_MODEL, EXPERT_FF), D_MODEL ** -0.5),
        "w_down": nrm(ks[20], (DEPTH, N_EXPERTS, EXPERT_FF, D_MODEL), EXPERT_FF ** -0.5),
        "final_norm_w": 1.0 + nrm(ks[21], (D_MODEL,), 0.02),
    }

def reference(x_prompt, x_sample, cache_k, cache_v, state_hgrn, page_table, attn_norm_w, w_in,
              hgrn_lb, hgrn_norm_w, diff_lambda, diff_norm_w, w_o, ffn_norm_w, w_r1, b_r1,
              w_r2, b_r2, w_gate, w_up, w_down, final_norm_w):
    b, s = x_prompt.shape[:2]
    bd, t = x_sample.shape[:2]
    n_pages = page_table.shape[1]
    past_len = n_pages * PAGE_SIZE
    pos_p = jnp.arange(s, dtype=jnp.int32)
    pos_s = past_len + jnp.arange(t, dtype=jnp.int32)
    pos_past = jnp.arange(past_len, dtype=jnp.int32)
    p_lb = jax.nn.softmax(hgrn_lb.astype(jnp.float32), axis=0)
    lb_all = jnp.cumsum(p_lb, axis=0) - p_lb[0:1]

    hp, hs = x_prompt, x_sample
    kp_l, vp_l, sp_l, ks_l, vs_l, ss_l = [], [], [], [], [], []
    for l in range(DEPTH):
        lam_init = 0.8 - 0.6 * math.exp(-0.3 * l)
        dl = diff_lambda[l].astype(jnp.float32)
        lam = jnp.exp(jnp.sum(dl[0] * dl[1])) - jnp.exp(jnp.sum(dl[2] * dl[3])) + lam_init
        lb = lb_all[l].reshape(HG_HEADS, HG_DK)
        wl = (attn_norm_w[l], w_in[l], hgrn_norm_w[l], diff_norm_w[l], w_o[l], ffn_norm_w[l],
              w_r1[l], b_r1[l], w_r2[l], b_r2[l], w_gate[l], w_up[l], w_down[l])
        s0_p = jnp.zeros((b, HG_HEADS, HG_DK, HG_DV), jnp.float32)
        hp, k_rows, v_rows, s_fin = trunk_layer(hp, pos_p, s0_p, None, lam, lam_init, lb, *wl)
        kp_l.append(k_rows)
        vp_l.append(v_rows)
        sp_l.append(s_fin)
        k_past = cache_k[l][page_table].reshape(bd, past_len, DA_HEADS, 2, DA_DK)
        v_past = cache_v[l][page_table].reshape(bd, past_len, DA_HEADS, DA_DV)
        s0_s = state_hgrn[l].astype(jnp.float32)
        hs, k_rows, v_rows, s_fin = trunk_layer(hs, pos_s, s0_s, (k_past, v_past, pos_past),
                                                lam, lam_init, lb, *wl)
        ks_l.append(k_rows)
        vs_l.append(v_rows)
        ss_l.append(s_fin)

    y_prompt = rms_norm(hp, final_norm_w)
    y_sample = rms_norm(hs, final_norm_w)
    return (y_prompt, y_sample, jnp.stack(kp_l), jnp.stack(vp_l), jnp.stack(sp_l),
            jnp.stack(ks_l), jnp.stack(vs_l), jnp.stack(ss_l))


_drawn_inputs = setup_inputs


def setup_inputs(seed=0):
    import zlib

    import numpy as np

    out = dict(_drawn_inputs(seed))
    spreads = {}
    factors = {'hgrn_norm_w': 2.831, 'b_r1': 3.037, 'b_r2': 7.903, 'final_norm_w': 2.739}
    for name, (base, spread) in spreads.items():
        noise = np.random.default_rng([zlib.crc32(name.encode()), seed]).standard_normal(out[name].shape)
        drawn = base * np.exp(spread * noise) if base else spread * noise
        out[name] = jnp.asarray(drawn.astype(out[name].dtype))
    for name, factor in factors.items():
        out[name] = (out[name] * factor).astype(out[name].dtype)
    return out
```

```python
import math
from contextlib import ExitStack

import concourse.bass as bass
from concourse import mybir
import numpy as np

ALU = mybir.AluOpType
ACT = mybir.ActivationFunctionType
F32 = mybir.dt.float32
U32 = mybir.dt.uint32
I32 = mybir.dt.int32
AX = mybir.AxisListType.X

L, D, S, DB, DT = 2, 1024, 512, 8, 4
H, DK, HD = 4, 64, 128
PAST, PAGE = 2048, 128
NPG = PAST // PAGE
P = 128
NS = DB * DT
TOK = S + NS
PT = S // P
NT = PT + 1
DC = D // P
W5 = 512
NE, NG, EG, FF = 16, 4, 4, 512
C = 16
NB = S // C
EPS = 1e-6
NEG = -1e30
F_MIN = 1e-30
YROWS = NE * P
THETA = 500000.0
ROT = DK // 4
HALF = TOK // 2
MAXX = 2 * TOK // P
XV = {"sel": 7, "ids": 10, "x": 12, "h": 13, "back": 18, "low": 23, "all": 28}
XP = {"ids": 1, "x": 2, "gate_up": 3, "h": 4, "y": 5, "low": 6, "all": 7}
XA = {"silu": 1, "h": 2, "y": 4}


def rows(i):
    return P if i < PT else NS


def tok(i):
    return slice(i * P, i * P + rows(i))


def constants():
    p = np.arange(P)[:, None]
    f = np.arange(P)[None, :]
    pos = np.zeros((P, NT), np.float32)
    for i in range(PT):
        pos[:, i] = np.arange(P) + i * P
    pos[:NS, PT] = PAST + np.arange(NS) % DT
    inv = (np.float32(THETA) ** (-np.arange(0, ROT, 2, dtype=np.float32) / np.float32(ROT))).astype(np.float32)
    ang = (pos[:, :, None] * inv[None, None, :]).astype(np.float32)
    cos, sin = np.cos(ang).astype(np.float32), np.sin(ang).astype(np.float32)
    row, key = np.arange(P)[:, None, None] % DT, np.arange(NS)[None, None, :]
    batch = np.arange(DB)[None, :, None]
    smask = np.where((key // DT == batch) & (key % DT <= row), 0.0, NEG)
    valid = np.ones((P, NT), np.float32)
    valid[NS:, PT] = 0.0
    blocks = {
        "ident": (p == f), "cmask": np.where(f <= p, 0.0, NEG), "ones": np.ones((P, P)),
        "tri": (p < f), "iota": np.broadcast_to(f, (P, P)),
        "cos": np.concatenate([cos, cos], -1).reshape(P, -1),
        "sin": np.concatenate([-sin, sin], -1).reshape(P, -1),
        "smask": smask.reshape(P, -1), "valid": valid,
        "even": (p // C % 2 == 0), "odd": (p // C % 2 == 1),
        "batch": (p // DT == np.arange(DB)[None, :]),
        "tokid": p + P * np.arange(NT)[None, :] * np.ones((P, 1)),
        "ebase": np.broadcast_to(P * np.arange(NE)[None, :], (P, NE)),
        "prio": np.broadcast_to(4.0 - np.arange(4)[None, :], (P, 4)),
        "eps": np.full((P, 1), EPS), "zero": np.zeros((P, 8)),
    }
    at, cols = {}, 0
    for name, a in blocks.items():
        n = a.shape[1]
        at[name] = (cols, n)
        cols += n
    return np.concatenate([np.asarray(a, np.float32) for a in blocks.values()], 1), at


def hgrn_items():
    items = []
    for h in range(H):
        items.append(("prep", h, 0))
        items += [("band", h, d) for d in range(C)]
        items.append(("keys", h, 0))
        items += [("round", h, r) for r in range(NB // 4)]
        items.append(("close", h, 0))
    return items


def weight_plan():
    plan = []
    for l in range(L):
        plan += [("in", l, j, (2, 3, 0, 1)[j % 4]) for j in range(7)]
        plan += [("out", l, n, n) for n in range(2)]
        for e in range(NE):
            for k in range(3):
                plan.append((("gate", "up", "down")[k], l, e, (2, 3, 4, 5, 0, 1)[(3 * e + k) % 6]))
    where, count = {}, [0] * 6
    for what, l, j, slot in plan:
        count[slot] += 1
        where[(what, l, j)] = (slot, count[slot])
    return plan, where


SPLITS = (4, 5, 6, 1, 2, 0, 3)


def build(nc, t_in, t_out):
    cst_np, at = constants()
    items = hgrn_items()
    plan, where = weight_plan()
    ctx = ExitStack()
    with ctx:
        def sb(name, n, dt=F32):
            return ctx.enter_context(nc.sbuf_tensor(name, [P, n], dt))

        def sem(name):
            return ctx.enter_context(nc.semaphore(name))

        bank = [ctx.enter_context(nc.psum_tensor(f"bank{i}", [P, 512], F32)) for i in range(8)]

        hid_a = sb("hid", NT * D)
        xT_a = sb("xT", DC * TOK)
        w_a = sb("wslots", 4 * 4096)
        h_a = sb("hgrn", 5 * H * TOK)
        t_a = sb("heads", 2 * H * S + NT * W5)
        m_a = sb("temps", 6400)
        cst = sb("cst", cst_np.shape[1])
        hid = hid_a[:, :].rearrange("p (i n) -> p i n", i=NT)
        xT = xT_a[:, :].rearrange("p (c n) -> p c n", c=DC)
        oT = xT

        def con(name, r=P):
            o, n = at[name]
            return cst[0:r, o:o + n]

        ident, ones, iota = con("ident"), con("ones"), con("iota")
        cosT = con("cos").rearrange("p (i n) -> p i n", i=NT)
        sinT = con("sin").rearrange("p (i n) -> p i n", i=NT)
        smask = con("smask").rearrange("p (b n) -> p b n", b=DB)

        def wslot(s):
            return w_a[:, 4096 * s:4096 * (s + 1)] if s < 4 else h_a[:, 4096 * (s - 4):4096 * (s - 3)]

        def weights(key, chunks):
            return wslot(where[key][0]).rearrange("p (c n) -> p c n", c=chunks)

        kpage = [w_a[:, 512 * s:512 * (s + 1)].rearrange("p (h n) -> p h n", h=H) for s in range(8)]
        vquad = [w_a[:, 4096 + 2048 * v:6144 + 2048 * v].rearrange("p (j h n) -> p j h n", j=4, h=H) for v in range(5)]
        NK, NV = len(kpage), len(vquad)

        hv = h_a[:, :].rearrange("p (k h n) -> p k h n", k=5, h=H)
        f_h, k_h, q_h, i_h, g_h = (hv[:, k] for k in range(5))

        def blk(a, h):
            return a[:, h, 0:S].rearrange("p (b c) -> p b c", c=C)

        qT = t_a[:, 0:2048].rearrange("p (h n) -> p h n", h=H)
        kT = t_a[:, 2048:4096].rearrange("p (h n) -> p h n", h=H)
        vtok = t_a[:, 4096:4096 + NT * W5].rearrange("p (i n) -> p i n", i=NT)
        xn = [m_a[:, 1024 * i:1024 * (i + 1)] for i in range(2)]
        junk = m_a[:, 2048:3072]
        qkt = [m_a[:, 3072 + 512 * i:3584 + 512 * i] for i in range(3)]
        e_p = [[m_a[:, 1024 * i + 512 * c:1024 * i + 512 * (c + 1)] for c in range(2)] for i in range(2)]
        aT = [m_a[:, 2048 + 512 * i:2560 + 512 * i] for i in range(2)]
        od = m_a[:, 3072:5120].rearrange("p (i n) -> p i n", i=PT)
        odsq = m_a[:, 5120:5248]
        ev = [m_a[:, 512 * i:512 * (i + 1)] for i in range(2)]
        pv_ = [m_a[:, 1024 + 512 * i:1536 + 512 * i] for i in range(2)]
        Fq = m_a[:, 2048:2560]
        khat = m_a[:, 2560:3072]
        itok = m_a[:, 3072:3584]
        ktok_m = [m_a[:, 3584 + 512 * i:4096 + 512 * i] for i in range(2)]
        sring = [m_a[:, 4608 + 128 * i:4736 + 128 * i] for i in range(8)]
        tmp = m_a[:, 5632:6144]
        f15 = m_a[:, 6144:6176]
        ktb = [a.rearrange("p (j h n) -> p j h n", j=4, h=H) for a in (w_a[:, 14336:16384], t_a[:, 0:2048])]
        scr = [t_a[:, 2048 + 512 * i:2560 + 512 * i] for i in range(6)]
        ptq = [t_a[:, 5120 + 512 * i:5632 + 512 * i].rearrange("p (j n) -> p j n", j=4) for i in range(2)]
        s0 = [t_a[:, 512 * i:512 * (i + 1)].rearrange("p (h n) -> p h n", h=H) for i in range(2)]
        s1 = [t_a[:, 1024 + 512 * i:1536 + 512 * i].rearrange("p (h n) -> p h n", h=H) for i in range(2)]
        sitok, sktok = t_a[0:NS, 2048:2560], t_a[0:NS, 2560:3072]
        smk = [t_a[0:NS, 3072 + 512 * i:3584 + 512 * i] for i in range(2)]
        xe = [t_a[:, 1024 * i:1024 * (i + 1)] for i in range(2)]
        xeT = [t_a[:, 2048 + 1024 * i:3072 + 1024 * i].rearrange("p (c n) -> p c n", c=DC) for i in range(2)]
        yt = [t_a[:, 4096 + 1024 * i:5120 + 1024 * i] for i in range(2)]
        silu = [m_a[:, 3072 + 512 * i:3584 + 512 * i] for i in range(2)]
        hgt = m_a[:, 4096:4608]
        hT = [m_a[:, 4608 + 512 * i:5120 + 512 * i].rearrange("p (c n) -> p c n", c=4) for i in range(2)]
        sel = m_a[:, 5632:6272].rearrange("p (i n) -> p i n", i=NT)
        yg = [m_a[:, 0:1024], m_a[:, 1024:2048], t_a[:, 4096:5120]]

        smalls = sb("smalls", 2304)
        used = [0]

        def shaped(a, shape):
            names = "abcd"[:len(shape)]
            if len(shape) == 1:
                return a
            return a.rearrange(f"p ({' '.join(names)}) -> p {' '.join(names)}", **dict(zip(names[:-1], shape)))

        def small(name, shape, dt=F32):
            n = int(np.prod(shape))
            a = smalls[:, used[0]:used[0] + n]
            used[0] += n
            return shaped(a if dt == F32 else a.bitcast(dt), shape)

        qTs = small("qTs", (H, NS))
        kTs = small("kTs", (H, NS))
        qz = [small(f"q_padded{i}", (H, 32)) for i in range(2)]
        nw = small("norm_cols", (2 * L, DC))
        hnw = small("hgrn_norm_col", (L,))
        dnw = small("diff_norm_col", (L,))
        lbr = small("lb_raw", (L, H))
        lbe = small("lb_exp", (L, H))
        lb = small("lb", (L, H))
        omlb = small("one_minus_lb", (L, H))
        lbt = small("lb_tmp", (2, H))
        dl = shaped(h_a[:, 0:512], (L, 4, DK))
        dlp = shaped(h_a[:, 512:768], (L, 2, DK))
        dls = small("diff_sum", (L, 2))
        nlam = small("minus_lambda", (L,))
        wr = small("router", (L, DC, NG + NE))
        brt = small("router_bias", (L, NG + NE))
        ptab = small("page_ids", (DB * NPG,), I32)
        ssq = small("ssq", (NT,))
        rt = small("root", (NT,))
        rs = small("rstd", (NT,))
        rope_t = shaped(m_a[:, 4608:4736], (2 * H, ROT))
        rope_u = shaped(m_a[:, 4736:4864], (2 * H, ROT))
        mx = small("row_max", (2, 2))
        rl = small("row_inv", (2, 2))
        ls = small("row_sum", (2, 2))
        ssq16 = small("od_ssq", (PT, H))
        rt16 = small("od_root", (PT, H))
        scn = [small(f"new_scores{i}", (NS,)) for i in range(2)]
        mx5 = small("sample_maxes", (5,))
        smx = small("sample_max", (1,))
        nmx = small("sample_minus_max", (2,))
        ls5 = small("sample_sums", (2, 5))
        sinv = small("sample_inv", (1,))
        sl = small("sample_sum", (1,))
        on = small("sample_o_rows", (HD,))
        so = small("sample_o", (H, 2, DT))
        sF = shaped(m_a[:, 2560:2688], (H, DB, DT))
        sE = shaped(m_a[:, 2688:2944], (2 * H, DB, DT))
        sP = shaped(m_a[:, 2944:3072], (H, DB, DT))
        sK = shaped(m_a[:, 3072:3200], (H, DB, DT))
        sA = shaped(m_a[:, 3200:3328], (H, DB, DT))
        lg = small("logits", (NT, NG + NE))
        r4 = shaped(m_a[:, 4608:4728], (6, NT, 4))
        r1 = small("route1", (8, NT))
        r16 = small("route16", (NT, 4, 4))
        msk = small("expert_mask", (NT, NE))
        m1 = shaped(m_a[:, 4728:4808], (NT, 4, 4))
        m2 = shaped(m_a[:, 4808:4888], (NT, 4, 4))
        pos = shaped(m_a[:, 4888:4968], (NT, NE))
        psel = small("slot_or_none", (NT, NE))
        tg = small("id_and_gate", (NT, NE, 2))
        rk = small("y_rows_f", (2, NT))
        rki = small("y_rows", (2, NT), U32)
        idx = small("slot_tokens", (NE,), U32)
        gate = small("slot_gates", (NE,))
        cntx = shaped(m_a[:, 5096:5144], (3, NE))
        ohx = small("extra_expert", (MAXX, NE))
        ohx2 = shaped(m_a[:, 4968:5096], (MAXX, NE))
        kx = small("extra_first_slot", (MAXX,))
        exf = small("extra_expert_f", (MAXX,))
        exi = small("extra_expert_i", (MAXX,), I32)
        nxi = small("extra_count", (1,), I32)
        psx = small("extra_slot_of", (NT,))
        tgx = small("extra_id_and_gate", (NT, 2))
        xid = small("extra_tokens", (1,), U32)
        xidf = small("extra_tokens_f", (1,))
        xgt = small("extra_gates", (1,))

        xn_d = nc.dram_tensor("xn_scratch", [TOK, D], F32, kind="Internal").ap()
        y_d = nc.dram_tensor("y_scratch", [YROWS + 1, D], F32, kind="Internal").ap()

        par = sem("params_loaded")
        xl = [sem(f"x_loaded{i}") for i in range(NT)]
        wl = [sem(f"w_loaded{i}") for i in range(6)]
        kl = [sem(f"k_loaded{i}") for i in range(NK)]
        vl = [sem(f"v_quad_loaded{i}") for i in range(NV)]
        prep_a, prep_v, prep_ok = sem("lb_exps"), sem("prep_steps"), sem("params_ready")
        dv, ac, pl = sem("dve_steps"), sem("act_steps"), sem("pool_steps")
        rt_ok, xn_ok, xt_ps, xt_ok, xn_st = (sem(x) for x in ("root_ready", "xn_ready", "xt_in_psum", "xt_ready", "xn_stored"))
        tp_ps, tp_ok, roped, qk_ps, qk_ok = (sem(x) for x in ("tok_proj_psum", "tok_proj_ready", "roped", "qk_t_psum", "qk_t_ready"))
        st_k = [sem(f"k_stored{i}") for i in range(3)]
        st_v = sem("v_stored")
        fp_ps, fp_ok, fk_ok = sem("feat_proj_psum"), sem("feat_proj_ready"), sem("gates_ready")
        pa_qk, pa_max, pa_exp, pa_comb, pa_at, pa_ate, pa_pv, pa_od = (
            sem(x) for x in ("p_scores", "p_max", "p_exp", "p_mixed", "p_t_psum", "p_t_ready", "p_o_psum", "p_o_ready"))
        od_sq, od_rt, od_n, od_t, od_ok = (sem(x) for x in ("od_sums", "od_roots", "od_normed", "od_t_psum", "od_t_ready"))
        kt_ps, kt_ok, qz_ok, sq_ps, sq_ok, s_neg, s_exp, pt_ps, pt_ok, pv_ps, s_on = (
            sem(x) for x in ("page_t_psum", "page_t_ready", "s_queries", "s_scores_psum", "s_scores_ready", "s_minus_max",
                             "s_exp", "s_p_t_psum", "s_p_t_ready", "s_values_psum", "s_o_rows"))
        hi_t, hi_ok, hE, hP, hbc, hacc = (sem(x) for x in ("i_t_psum", "i_t_ready", "h_keys", "h_prod", "h_band_psum", "h_band_added"))
        hF, hkt, hkt_ok, hU, hS, hO, hclose, s_stored = (
            sem(x) for x in ("h_decay", "h_kt_psum", "h_kt_ready", "h_update_psum", "h_state", "h_inter_psum", "h_closed", "s_stored"))
        sh_t, sh_m, sh_ps, sh_s, sh_bcp, sh_p = (
            sem(x) for x in ("sh_t_psum", "sh_masked", "sh_psum", "sh_state", "sh_band_psum", "sh_prod"))
        sh_in = [sem(f"sh_state_in{i}") for i in range(2)]
        sh_st = [sem(f"sh_stored{i}") for i in range(2)]
        nsq, nps, nrt, o_ok = (sem(x) for x in ("n_squares", "n_sums_psum", "n_roots", "o_ready"))
        wo_ps, wo_add = sem("wo_psum"), sem("wo_added")
        lg_ps, lg_ok, rexp, msk_ok, pos_ps, psel_ok, sel_ok, id_ps, id_ok, rk_ok = (
            sem(x) for x in ("logits_psum", "logits_ready", "route_exps", "masks_ready", "slots_psum", "slots_ready", "sel_ready", "ids_psum", "ids_ready", "rows_ready"))
        xe_in = [sem(f"xe_gathered{i}") for i in range(2)]
        xe_ps, xe_ok, gu_ps, si_ok, hg_ok, ht_ps, ht_ok, y_ps, y_ok = (
            sem(x) for x in ("xe_t_psum", "xe_t_ready", "gate_up_psum", "silu_ready", "h_ready", "h_t_psum", "h_t_ready", "y_psum", "y_ready"))
        y_st = [sem(f"y_stored{i}") for i in range(2)]
        yg_in = [sem(f"y_gathered{i}") for i in range(3)]
        xw, xg, xv, xp, xa = ([sem(f"extra_{w}{l}") for l in range(L)] for w in ("weights", "gathered", "dve", "pe", "act"))
        passed = sem("extra_waits_passed")
        zero_st = sem("zero_row_stored")
        moe_add, out_ok, out_st = sem("moe_added"), sem("out_ready"), sem("out_stored")
        fw_in = sem("final_w_loaded")

        NPAR = 13
        NQ = DB * NPG // 4
        SLOTS = DB * NPG + 12

        def qn(g):
            return 5 * (g // 4) + g % 4


        def used(key):
            what, l, j = key
            if what == "in":
                return (tp_ps, 15 * l + NT * (j + 1)) if j < 3 else (fp_ps, 32 * l + 8 * (j - 2))
            if what == "out":
                return wo_ps, 10 * l + NT * (j + 1)
            if what == "down":
                return y_ps, 2 * (NE * l + j) + 2
            return gu_ps, 2 * (NE * l + j) + (1 if what == "gate" else 2)

        def extra_tiles(eng, ready, body):
            eng.wait_ge(rk_ok, ready)
            n = eng.value_load(nxi[0:1, 0:1], min_val=0, max_val=MAXX)
            with eng.Fori(0, MAXX) as t:
                with eng.If(t < n):
                    body(t)
                    eng.sem_inc(passed, 1)

        def wwait(eng, key):
            slot, n = where[key]
            eng.wait_ge(wl[slot], 16 * n)

        block = ctx.enter_context(nc.Block())

        @block.sync
        def _(sp):
            with nc.allow_non_contiguous_dma(reason="small parameter columns"):
                sp.dma_start(cst[:, :], t_in["constants"]).then_inc(par, 16)
                for i in range(NT):
                    src = t_in["x_prompt"][0, tok(i), :] if i < PT else t_in["x_sample"].rearrange("b t d -> (b t) d")
                    sp.dma_start(hid[0:rows(i), i, :], src).then_inc(xl[i], 16)

                def load_w(n):
                    what, l, j, slot = plan[n]
                    cnt = where[(what, l, j)][1]
                    if cnt > 1:
                        before = next(k for k, v in where.items() if v == (slot, cnt - 1))
                        sp.wait_ge(*used(before))
                    if what == "in":
                        src = t_in["w_in"][l, :, SPLITS[j] * W5:(SPLITS[j] + 1) * W5]
                    elif what == "out":
                        src = t_in["w_o"][l, :, j * W5:(j + 1) * W5]
                    else:
                        src = t_in["w_" + what][l, j]
                    ch = 4 if what == "down" else DC
                    sp.dma_start(wslot(slot).rearrange("p (c n) -> p c n", c=ch),
                                 src.rearrange("(c p) n -> p c n", p=P)).then_inc(wl[slot], 16)

                load_w(0)
                sp.dma_start(nw[:, 0:L, :], t_in["attn_norm_w"].rearrange("l (c p) -> p l c", p=P)).then_inc(par, 16)
                sp.dma_start(nw[:, L:2 * L, :], t_in["ffn_norm_w"].rearrange("l (c p) -> p l c", p=P)).then_inc(par, 16)
                sp.dma_start(hnw[:, :], t_in["hgrn_norm_w"].rearrange("l p -> p l")).then_inc(par, 16)
                sp.dma_start(dnw[:, :], t_in["diff_norm_w"].rearrange("l p -> p l")).then_inc(par, 16)
                sp.dma_start(lbr[:, :, :], t_in["hgrn_lb"].rearrange("l (h p) -> p l h", p=P)).then_inc(par, 16)
                sp.dma_start(dl[:, :, :, :].rearrange("p a b c -> p (a b c)"),
                             t_in["diff_lambda"].rearrange("(o a) b c -> o (a b c)", o=1).to_broadcast([P, L * 4 * DK])).then_inc(par, 16)
                for l in range(L):
                    sp.dma_start(wr[:, l, :, 0:NG], t_in["w_r1"][l].rearrange("(c p) n -> p c n", p=P)).then_inc(par, 16)
                    sp.dma_start(wr[:, l, :, NG:], t_in["w_r2"][l].rearrange("(c p) n -> p c n", p=P)).then_inc(par, 16)
                sp.dma_start(brt[:, :, 0:NG], t_in["b_r1"].rearrange("(o l) n -> o l n", o=1).to_broadcast([P, L, NG])).then_inc(par, 16)
                sp.dma_start(brt[:, :, NG:], t_in["b_r2"].rearrange("(o l) n -> o l n", o=1).to_broadcast([P, L, NE])).then_inc(par, 16)
                sp.dma_start(ptab[0:1, :], t_in["page_table"].rearrange("(o b) j -> o (b j)", o=1)).then_inc(par, 16)
                for n in range(1, 4):
                    load_w(n)
                sp.wait_ge(par, 16 * (NPAR + 1))
                per = len(plan) // L
                for l in range(L):
                    for j in range(4 if l == 0 else 0, 7):
                        load_w(l * per + j)
                    sp.wait_ge(*used(("in", l, 6)))

                    def load_page(p, dst, cache, done):
                        page = sp.value_load(ptab[0:1, p:p + 1], min_val=0, max_val=t_in["cache_k"].shape[1] - 1)
                        sp.dma_start(dst.rearrange("p h n -> p (h n)"),
                                     cache[l, bass.ds(page, 1)].rearrange("o p h n -> (o p) (h n)")).then_inc(done, 16)

                    for g in range(NQ + 1):
                        for p in range(4 * g, min(4 * g + 4, DB * NPG)):
                            if p >= NK:
                                sp.wait_ge(kt_ps, l * DB * NPG + p - NK + 1)
                            load_page(p, kpage[p % NK], t_in["cache_k"], kl[p % NK])
                        if g:
                            v = l * NQ + g - 1
                            if g - 1 >= NV:
                                sp.wait_ge(pv_ps, qn(v - NV) + 1)
                            for j in range(4):
                                load_page(4 * (g - 1) + j, vquad[v % NV][:, j], t_in["cache_v"], vl[v % NV])
                    sp.wait_ge(kt_ps, (l + 1) * DB * NPG)
                    load_w(l * per + 7)
                    sp.wait_ge(pv_ps, (l + 1) * 5 * DB)
                    load_w(l * per + 8)
                    for q in range(3 * NE):
                        if q == 2:
                            sp.wait_ge(o_ok, 6 * (l + 1))
                        load_w(l * per + 9 + q)

                    def extra(t):
                        e = sp.value_load(exi[0:1, bass.ds(t, 1)], min_val=0, max_val=NE - 1)
                        for slot, what, ch in ((2, "gate", DC), (3, "up", DC), (4, "down", 4)):
                            sp.dma_start(wslot(slot).rearrange("p (c n) -> p c n", c=ch),
                                         t_in["w_" + what][l, bass.ds(e, 1)].rearrange("o (c p) n -> p (o c) n", p=P)).then_inc(xw[l], 16)
                        sp.wait_ge(xp[l], t * XP["all"] + XP["y"])
                    sp.wait_ge(*used(("down", l, NE - 2)))
                    extra_tiles(sp, l + 1, extra)
                sp.wait_ge(moe_add, 10 * L)
                sp.dma_start(xT_a[:, 0:D], t_in["final_norm_w"].rearrange("(o n) -> o n", o=1).to_broadcast([P, D])).then_inc(fw_in, 16)

        @block.tensor
        def _(pe):
            mm, tr = nc.tensor.matmul, nc.tensor.transpose

            def norm_turn(m, i):
                pe.wait_ge(xn_ok, NT * m + i + 1)
                r = rows(i)
                for j in range(2):
                    n = 2 * (NT * m + i) + j
                    if n >= 2:
                        pe.wait_ge(xt_ok, n - 1)
                    for c in range(4):
                        k = 4 * j + c
                        x = tr(bank[j][:, c * P:c * P + r], xn[i % 2][0:r, k * P:(k + 1) * P], ident[0:r, 0:r])
                    x.then_inc(xt_ps, 1)

            def proj_tok(l, n):
                s, i = n // NT, n % NT
                r = rows(i)
                g = 15 * l + n
                if i == 0:
                    wwait(pe, ("in", l, s))
                pe.wait_ge(xt_ok, 10 * 2 * l + 2 * (i + 1))
                if g >= 2:
                    pe.wait_ge(tp_ok, g - 1)
                w = weights(("in", l, s), DC)
                for c in range(DC):
                    x = mm(bank[2 + n % 2][0:r, :], xT[:, c, tok(i)], w[:, c, :], start=(c == 0), stop=(c == DC - 1))
                x.then_inc(tp_ps, 1)

            def turn_qk(l, n):
                i = n % NT
                r = rows(i)
                g = 10 * l + n
                pe.wait_ge(roped, g + 1)
                if g >= 2:
                    pe.wait_ge(qk_ok, g - 1)
                for h in range(H):
                    x = tr(bank[4 + n % 2][:, h * P:h * P + r], qkt[n % 3][0:r, h * P:(h + 1) * P], ident[0:r, 0:r])
                x.then_inc(qk_ps, 1)

            def proj_feat(l, g):
                s, h, half = 3 + g // 8, g // 2 % 4, g % 2
                n = 32 * l + g
                if g % 8 == 0:
                    wwait(pe, ("in", l, s))
                if n >= 2:
                    pe.wait_ge(fp_ok, n - 1)
                w = weights(("in", l, s), DC)
                for c in range(DC):
                    x = mm(bank[6 + g % 2][:, 0:HALF], w[:, c, h * P:(h + 1) * P], xT[:, c, half * HALF:(half + 1) * HALF],
                           start=(c == 0), stop=(c == DC - 1))
                x.then_inc(fp_ps, 1)

            def scores(l, u):
                i, h, U = u // H, u % H, 16 * l + u
                if U >= 2:
                    pe.wait_ge(pa_exp, U - 1)
                for c in range(2):
                    o = bank[c + 2 * (u % 2)]
                    a, z = 64 * c, 64 * (c + 1)
                    q = qT[a:z, h, tok(i)]
                    if i > 0:
                        mm(o[:, 0:i * P], q, kT[a:z, h, 0:i * P], start=True, stop=True)
                    mm(o[:, i * P:(i + 1) * P], q, kT[a:z, h, tok(i)], start=True, stop=False)
                    x = mm(o[:, i * P:(i + 1) * P], ident, con("cmask"), start=False, stop=True)
                x.then_inc(pa_qk, 1)

            def turn_a(l, u):
                i, U = u // H, 16 * l + u
                pe.wait_ge(pa_comb, U + 1)
                if U >= 2:
                    pe.wait_ge(pa_ate, U - 1)
                for j in range(i + 1):
                    x = tr(bank[4 + u % 2][:, j * P:(j + 1) * P], e_p[u % 2][1][:, j * P:(j + 1) * P], ident)
                x.then_inc(pa_at, 1)

            def values(l, u):
                i, h, U = u // H, u % H, 16 * l + u
                pe.wait_ge(pa_ate, U + 1)
                if U >= 2:
                    pe.wait_ge(pa_od, U - 1)
                for j in range(i + 1):
                    x = mm(bank[6 + u % 2][:, 0:HD], aT[u % 2][:, j * P:(j + 1) * P], vtok[:, j, h * HD:(h + 1) * HD],
                           start=(j == 0), stop=(j == i))
                x.then_inc(pa_pv, 1)

            def page_turn(l, s):
                g = l * DB * NPG + s
                pe.wait_ge(kl[s % NK], 16 * (l * (DB * NPG // NK) + s // NK + 1))
                if g >= 2:
                    pe.wait_ge(kt_ok, g - 1)
                for h in range(H):
                    x = tr(bank[s % 2][:, h * P:(h + 1) * P], kpage[s % NK][:, h, :], ident)
                x.then_inc(kt_ps, 1)

            def quad_scores(l, g):
                G_ = l * NQ + g
                Q = qn(G_)
                pe.wait_ge(kt_ok, 4 * G_ + 4)
                pe.wait_ge(qz_ok, G_ // 4 + 1)
                if Q >= 2:
                    pe.wait_ge(sq_ok, Q - 1)
                for h in range(H):
                    x = mm(bank[2 + Q % 2][32 * h:32 * h + 32, :], qz[g // 4 % 2][:, h, :], ktb[g % 2][:, :, h, :], start=True, stop=True)
                x.then_inc(sq_ps, 1)

            def new_scores(l, b):
                Q = 5 * (l * DB + b) + 4
                pe.wait_ge(sq_ok, Q - 1)
                for h in range(H):
                    x = mm(bank[2 + Q % 2][32 * h:32 * h + 32, 0:NS], qz[b % 2][:, h, :], kTs[:, h, :], start=True, stop=True)
                x.then_inc(sq_ps, 1)

            def turn_p(l, b, q):
                B = l * DB + b
                pe.wait_ge(s_exp, 5 * B + q + 1)
                if 6 * B + q:
                    pe.wait_ge(pt_ok, 6 * B + q)
                if q < 4:
                    for j in range(4):
                        x = tr(bank[4][:, j * P:(j + 1) * P], scr[(4 * B + q) % 6][:, j * P:(j + 1) * P], ident)
                else:
                    x = tr(bank[4][0:NS, 0:P], scn[b % 2], ident)
                x.then_inc(pt_ps, 1)

            def quad_values(l, b, q):
                B = l * DB + b
                pe.wait_ge(pt_ok, 6 * B + q + 1)
                if q == 0 and B:
                    pe.wait_ge(s_on, B)
                par = (5 * B + q) % 2
                if q < 4:
                    v = l * NQ + 4 * b + q
                    pe.wait_ge(vl[v % NV], 64 * (v // NV + 1))
                    for j in range(4):
                        for h in range(H):
                            x = mm(bank[5][32 * h:32 * h + 32, 0:HD], ptq[par][:, j, 32 * h:32 * h + 32], vquad[v % NV][:, j, h, :],
                                   start=(q == 0 and j == 0), stop=False)
                else:
                    for h in range(H):
                        x = mm(bank[5][32 * h:32 * h + 32, 0:HD], ptq[par][0:NS, 0, 32 * h:32 * h + 32],
                               vtok[0:NS, PT, h * HD:(h + 1) * HD], start=False, stop=True)
                x.then_inc(pv_ps, 1)

            def turn_o(l, b):
                B = l * DB + b
                pe.wait_ge(s_on, B + 1)
                pe.wait_ge(pt_ok, 6 * B + 5)
                tr(bank[4][:, 0:P], on, ident).then_inc(pt_ps, 1)

            def hgrn(l, item):
                kind, h, n = item
                hh = l * H + h
                if kind == "prep":
                    if hh >= 1:
                        pe.wait_ge(hclose, hh)
                    for i in range(PT):
                        x = tr(bank[6][:, i * P:(i + 1) * P], i_h[:, h, tok(i)], ident)
                    x.then_inc(hi_t, 1)
                elif kind == "band":
                    g = C * hh + n
                    pe.wait_ge(hP, g + 1)
                    if g >= 1:
                        pe.wait_ge(hacc, g)
                    mm(bank[7][:, 0:NB * (C - n)], ones, pv_[n % 2][:, 0:NB * (C - n)], start=True, stop=True).then_inc(hbc, 1)
                elif kind == "keys":
                    pe.wait_ge(hi_ok, hh + 1)
                    pe.wait_ge(hE, C * hh + C)
                    for i in range(PT):
                        x = tr(bank[6][:, i * P:(i + 1) * P], khat[:, i * P:(i + 1) * P], ident)
                    x.then_inc(hkt, 1)
                elif kind == "round":
                    if n == 0:
                        pe.wait_ge(hkt_ok, hh + 1)
                    else:
                        pe.wait_ge(hS, NB * hh + 4 * n)
                    for k in range(4):
                        b = 4 * n + k
                        rr = slice(32 * (b // 2 % 4), 32 * (b // 2 % 4) + 32)
                        tile_ = b // 8
                        x = mm(bank[6][:, k * P:(k + 1) * P], ktok_m[b % 2][rr, tile_ * P:(tile_ + 1) * P],
                               itok[rr, tile_ * P:(tile_ + 1) * P], start=True, stop=True)
                        if k % 2:
                            x.then_inc(hU, 1)
                        if k == 1:
                            pe.wait_ge(hU, 2 * ((NB // 4) * hh + n) + 1)
                    if n >= 1:
                        inter(l, h, n - 1)
                elif kind == "close":
                    inter(l, h, NB // 4 - 1)

            def inter(l, h, n):
                hh = l * H + h
                pe.wait_ge(hF, hh + 1)
                if n == 0:
                    pe.wait_ge(hacc, C * (hh + 1))
                for b in range(4 * n, 4 * n + 4):
                    if b == 0:
                        continue
                    pe.wait_ge(hS, NB * hh + b)
                    x = mm(bank[7][:, b * C:(b + 1) * C], sring[b % 8], Fq[:, b * C:(b + 1) * C], start=True, stop=True)
                x.then_inc(hO, 1)

            def hgrn_sample(l):
                pe.wait_ge(hclose, (l + 1) * H)
                pe.wait_ge(sh_p, 1 + 2 * l)
                for h in range(H):
                    tr(bank[0][0:NS, h * P:(h + 1) * P], i_h[:, h, S:TOK], ident)
                for h in range(H):
                    x = tr(bank[1][0:NS, h * P:(h + 1) * P], sK[:, h].rearrange("p b t -> p (b t)"), ident)
                x.then_inc(sh_t, 1)
                pe.wait_ge(sh_p, 2 + 2 * l)
                x = mm(bank[2][:, 0:H * DB * 10], ones, pv_[0][:, 0:H * DB * 10], start=True, stop=True)
                x.then_inc(sh_bcp, 1)
                for b in range(DB):
                    B = l * DB + b
                    pe.wait_ge(sh_m, B + 1)
                    if b >= 2:
                        pe.wait_ge(sh_s, B - 1)
                    for h in range(H):
                        mm(bank[4 + b % 2][:, h * P:(h + 1) * P], smk[b % 2][:, h * P:(h + 1) * P], sitok[:, h * P:(h + 1) * P],
                           start=True, stop=True)
                    pe.wait_ge(sh_in[b % 2], 16 * (l * (DB // 2) + b // 2 + 1))
                    for h in range(H):
                        x = mm(bank[3][:, (b * H + h) * DT:(b * H + h + 1) * DT], s0[b % 2][:, h, :], sF[:, h, b, :],
                               start=True, stop=True)
                    x.then_inc(sh_ps, 1)

            def feature_sums(l, n):
                g = 6 * l + n
                pe.wait_ge(nsq, g + 1)
                if g >= 2:
                    pe.wait_ge(nrt, g - 1)
                w = S if n < 4 else H * NS
                mm(bank[6 + n % 2][:, 0:w], ones, pv_[n % 2][:, 0:w], start=True, stop=True).then_inc(nps, 1)

            def out_proj(l, n):
                s, i = n // NT, n % NT
                r, g = rows(i), 10 * l + n
                if i == 0:
                    wwait(pe, ("out", l, s))
                if g >= 2:
                    pe.wait_ge(wo_add, g - 1)
                w = weights(("out", l, s), DC)
                for c in range(DC):
                    x = mm(bank[2 + n % 2][0:r, :], oT[:, c, tok(i)], w[:, c, :], start=(c == 0), stop=(c == DC - 1))
                x.then_inc(wo_ps, 1)

            def x_turn(l, e):
                E_ = l * NE + e
                pe.wait_ge(xe_in[e % 2], 16 * (l * (NE // 2) + e // 2 + 1))
                if E_ >= 1:
                    pe.wait_ge(xe_ok, 2 * E_)
                for j in range(2):
                    for c in range(4):
                        k = 4 * j + c
                        x = tr(bank[j][:, c * P:(c + 1) * P], xe[e % 2][:, k * P:(k + 1) * P], ident)
                    x.then_inc(xe_ps, 1)

            def gate_up(l, e):
                E_ = l * NE + e
                pe.wait_ge(xe_ok, 2 * E_ + 2)
                if E_ >= 1:
                    pe.wait_ge(hg_ok, E_)
                for k, what in enumerate(("gate", "up")):
                    wwait(pe, (what, l, e))
                    w = weights((what, l, e), DC)
                    for c in range(DC):
                        x = mm(bank[2 + k][:, :], xeT[e % 2][:, c, :], w[:, c, :], start=(c == 0), stop=(c == DC - 1))
                    x.then_inc(gu_ps, 1)

            def h_turn(l, e):
                E_ = l * NE + e
                pe.wait_ge(hg_ok, E_ + 1)
                if E_ >= 1:
                    pe.wait_ge(ht_ok, E_)
                for c in range(4):
                    x = tr(bank[4][:, c * P:(c + 1) * P], hgt[:, c * P:(c + 1) * P], ident)
                x.then_inc(ht_ps, 1)

            def down(l, e):
                E_ = l * NE + e
                pe.wait_ge(ht_ok, E_ + 1)
                wwait(pe, ("down", l, e))
                w = weights(("down", l, e), 4)
                for n in range(2):
                    if E_ >= 1:
                        pe.wait_ge(y_ok, 2 * E_ - 1 + n)
                    for c in range(4):
                        x = mm(bank[5 + n][:, :], hT[e % 2][:, c, :], w[:, c, n * W5:(n + 1) * W5], start=(c == 0), stop=(c == 3))
                    x.then_inc(y_ps, 1)

            pe.wait_ge(par, 16 * (NPAR + 1))
            for l in range(L):
                if l:
                    pe.wait_ge(y_ok, 2 * NE * l)
                for i in range(NT):
                    norm_turn(2 * l, i)
                for n in range(15):
                    proj_tok(l, n)
                    if 1 <= n <= 10:
                        turn_qk(l, n - 1)
                for g in range(32):
                    proj_feat(l, g)
                pe.wait_ge(tp_ok, 15 * (l + 1))
                pe.wait_ge(fp_ok, 32 * (l + 1))
                pe.wait_ge(qk_ok, 10 * (l + 1))
                for v in range(16 + 3):
                    if v < 16:
                        scores(l, v)
                    if 2 <= v < 18:
                        turn_a(l, v - 2)
                    if 3 <= v:
                        values(l, v - 3)
                pe.wait_ge(pa_ate, 16 * (l + 1))
                for i in range(PT):
                    n = PT * l + i
                    pe.wait_ge(od_n, n + 1)
                    if n >= 2:
                        pe.wait_ge(od_ok, n - 1)
                    for h in range(H):
                        x = tr(bank[4 + i % 2][:, h * P:(h + 1) * P], od[:, i, h * P:(h + 1) * P], ident)
                    x.then_inc(od_t, 1)
                pe.wait_ge(od_ok, PT * (l + 1))
                pe.wait_ge(pa_od, 16 * (l + 1))
                pe.wait_ge(pa_exp, 16 * (l + 1))
                for s in range(SLOTS):
                    if s < DB * NPG:
                        page_turn(l, s)
                    if s % 4 == 0 and 1 <= s // 4 <= NQ:
                        quad_scores(l, s // 4 - 1)
                        if s % NPG == 0:
                            new_scores(l, s // NPG - 1)
                    b, k = s // NPG - 1, s % NPG
                    if b >= 0:
                        if 3 <= k < 8:
                            turn_p(l, b, k - 3)
                        if 4 <= k < 9:
                            quad_values(l, b, k - 4)
                        if k == 10:
                            turn_o(l, b)
                    if s < len(items):
                        hgrn(l, items[s])
                pe.wait_ge(pt_ok, 6 * DB * (l + 1))
                hgrn_sample(l)
                pe.wait_ge(hclose, (l + 1) * H)
                for n in range(6):
                    feature_sums(l, n)
                pe.wait_ge(o_ok, 6 * (l + 1))
                for n in range(10):
                    out_proj(l, n)
                pe.wait_ge(sh_s, DB * (l + 1))
                for i in range(NT):
                    norm_turn(2 * l + 1, i)
                for i in range(NT):
                    n = NT * l + i
                    pe.wait_ge(xt_ok, 10 * (2 * l + 1) + 2 * (i + 1))
                    if i >= 2:
                        pe.wait_ge(lg_ok, n - 1 + l)
                    for c in range(DC):
                        x = mm(bank[4 + i % 2][0:rows(i), 0:NG + NE], xT[:, c, tok(i)], wr[:, l, c, :], start=(c == 0), stop=(c == DC - 1))
                    x.then_inc(lg_ps, 1)
                pe.wait_ge(msk_ok, l + 1)
                for i in range(NT):
                    for j in range(i + 1):
                        x = mm(bank[6][:, i * NE:(i + 1) * NE], ones if j < i else con("tri"), msk[:, j, :], start=(j == 0), stop=(j == i))
                for j in range(NT):
                    x = mm(bank[6][:, NT * NE:(NT + 1) * NE], ones, msk[:, j, :], start=(j == 0), stop=(j == NT - 1))
                x.then_inc(pos_ps, 1)
                pe.wait_ge(psel_ok, l + 1)
                for e in range(NE):
                    E_ = l * NE + e
                    pe.wait_ge(sel_ok, E_ + 1)
                    if e >= 1:
                        pe.wait_ge(id_ok, E_)
                    for i in range(NT):
                        x = mm(bank[7][:, 0:2], sel[:, i, :], tg[:, i, e, :], start=(i == 0), stop=(i == NT - 1))
                    x.then_inc(id_ps, 1)
                pe.wait_ge(xt_ok, 10 * (2 * l + 2))
                pe.wait_ge(wo_add, 10 * (l + 1))
                x_turn(l, 0)
                for e in range(NE):
                    gate_up(l, e)
                    if e >= 1:
                        down(l, e - 1)
                    if e + 1 < NE:
                        x_turn(l, e + 1)
                    h_turn(l, e)
                down(l, NE - 1)

                def extra(t):
                    V_, A_ = t * XV["all"], t * XA["y"]
                    pe.wait_ge(xv[l], V_ + XV["sel"])
                    for i in range(NT):
                        x = mm(bank[7][:, 0:2], sel[:, i, :], tgx[:, i, :], start=(i == 0), stop=(i == NT - 1))
                    x.then_inc(xp[l], 1)
                    pe.wait_ge(xg[l], t * 16 + 16)
                    for k in range(DC):
                        x = tr(bank[k // 4][:, k % 4 * P:(k % 4 + 1) * P], xe[0][:, k * P:(k + 1) * P], ident)
                    x.then_inc(xp[l], 1)
                    pe.wait_ge(xv[l], V_ + XV["x"])
                    pe.wait_ge(xw[l], t * 48 + 48)
                    for k in range(2):
                        w = wslot(2 + k).rearrange("p (c n) -> p c n", c=DC)
                        for c in range(DC):
                            x = mm(bank[2 + k][:, :], xeT[0][:, c, :], w[:, c, :], start=(c == 0), stop=(c == DC - 1))
                    x.then_inc(xp[l], 1)
                    pe.wait_ge(xv[l], V_ + XV["h"])
                    for c in range(4):
                        x = tr(bank[4][:, c * P:(c + 1) * P], hgt[:, c * P:(c + 1) * P], ident)
                    x.then_inc(xp[l], 1)
                    pe.wait_ge(xa[l], A_ + XA["h"])
                    w = wslot(4).rearrange("p (c n) -> p c n", c=4)
                    for n in range(2):
                        for c in range(4):
                            x = mm(bank[5 + n][:, :], hT[0][:, c, :], w[:, c, n * W5:(n + 1) * W5], start=(c == 0), stop=(c == 3))
                    x.then_inc(xp[l], 1)
                    pe.wait_ge(xa[l], A_ + XA["y"])
                    pe.wait_ge(xv[l], V_ + XV["back"])
                    for n in range(2):
                        if n:
                            pe.wait_ge(xv[l], V_ + XV["low"])
                        for i in range(NT):
                            x = mm(bank[i][0:rows(i), :], sel[:, i, 0:rows(i)], yt[0][:, n * W5:(n + 1) * W5], start=True, stop=True)
                        x.then_inc(xp[l], 1)
                    pe.wait_ge(xv[l], V_ + XV["all"])

                pe.wait_ge(y_ok, 2 * NE * (l + 1))
                extra_tiles(pe, l + 1, extra)

        @block.scalar
        def _(act):
            A = nc.scalar.activation
            steps = [0]

            def link(ins):
                steps[0] += 1
                ins.then_inc(ac, 1)
                act.wait_ge(ac, steps[0])

            def norm_roots(m):
                for i in range(NT):
                    r = rows(i)
                    if m == 0:
                        act.wait_ge(xl[i], 16)
                    elif m % 2:
                        act.wait_ge(wo_add, 10 * (m // 2) + 5 + i + 1)
                    else:
                        act.wait_ge(moe_add, 10 * (m // 2 - 1) + 2 * i + 2)
                    link(A(junk[0:r, :], hid[0:r, i, :], ACT.Square, accum_out=ssq[0:r, i:i + 1]))
                    A(rt[0:r, i:i + 1], ssq[0:r, i:i + 1], ACT.Sqrt, bias=con("eps")[0:r, :], scale=1.0 / D).then_inc(rt_ok, 1)

            act.wait_ge(prep_v, 1)
            A(lbe[:, :, :], lbe[:, :, :], ACT.Exp).then_inc(prep_a, 1)
            A(dls[:, :, :], dls[:, :, :], ACT.Exp).then_inc(prep_a, 1)
            for l in range(L):
                norm_roots(2 * l)
                for n in range(15):
                    s, i, g = n // NT, n % NT, 15 * l + n
                    r = rows(i)
                    act.wait_ge(tp_ps, g + 1)
                    if s < 2:
                        if n >= 3:
                            act.wait_ge(qk_ps, 10 * l + n - 2)
                        if l or n >= 8:
                            per = [sum(1 for x in range(5, 10) if x % 3 == k) for k in range(3)]
                            done = per[n % 3] * l + sum(1 for x in range(5, n) if x % 3 == n % 3)
                            if done:
                                act.wait_ge(st_k[n % 3], 16 * done)
                        dst = qkt[n % 3][0:r, :]
                    else:
                        dst = vtok[0:r, i, :]
                    A(dst, bank[2 + n % 2][0:r, :], ACT.Copy).then_inc(tp_ok, 1)
                for g in range(32):
                    s, h, half = g // 8, g // 2 % 4, g % 2
                    cols = slice(half * HALF, (half + 1) * HALF)
                    act.wait_ge(fp_ps, 32 * l + g + 1)
                    src = bank[6 + g % 2][:, 0:HALF]
                    if s == 0:
                        A(f_h[:, h, cols], src, ACT.Sigmoid)
                        x = A(k_h[:, h, cols], src, ACT.Sigmoid, scale=-1.0)
                    elif s == 1:
                        x = A(i_h[:, h, cols], src, ACT.Copy)
                    elif s == 2:
                        x = A(q_h[:, h, cols], src, ACT.Copy, scale=float(HD) ** -0.5)
                    else:
                        x = A(g_h[:, h, cols], src, ACT.Sigmoid)
                    x.then_inc(fp_ok, 1)
                for v in range(16 + 3):
                    if v < 16:
                        u, U = v, 16 * l + v
                        w = (u // H + 1) * P
                        act.wait_ge(pa_max, U + 1)
                        if v >= 2:
                            act.wait_ge(pa_at, U - 1)
                        for c in range(2):
                            x = A(e_p[u % 2][c][:, 0:w], bank[c + 2 * (u % 2)][:, 0:w], ACT.Exp,
                                  bias=mx[:, u % 2, c:c + 1], accum_out=ls[:, u % 2, c:c + 1])
                        x.then_inc(pa_exp, 1)
                    if 2 <= v < 18:
                        u, U = v - 2, 16 * l + v - 2
                        w = (u // H + 1) * P
                        act.wait_ge(pa_at, U + 1)
                        if v >= 4:
                            act.wait_ge(pa_pv, U - 1)
                        A(aT[u % 2][:, 0:w], bank[4 + u % 2][:, 0:w], ACT.Copy).then_inc(pa_ate, 1)
                act.wait_ge(od_sq, l + 1)
                A(rt16[:, :, :], ssq16[:, :, :], ACT.Sqrt, bias=con("eps"), scale=1.0 / HD).then_inc(od_rt, 1)
                act.wait_ge(od_t, PT * (l + 1))
                for s in range(SLOTS):
                    if s < DB * NPG:
                        G_ = l * NQ + s // 4
                        act.wait_ge(kt_ps, l * DB * NPG + s + 1)
                        if G_ >= 2:
                            act.wait_ge(sq_ps, qn(G_ - 2) + 1)
                        A(ktb[s // 4 % 2][:, s % 4].rearrange("p h n -> p (h n)"), bank[s % 2][:, :], ACT.Copy).then_inc(kt_ok, 1)
                    b, k = s // NPG - 1, s % NPG
                    if b >= 0 and 1 <= k < 4:
                        B = l * DB + b
                        act.wait_ge(s_neg, B + 1)
                        for q in range(2 * (k - 1), min(2 * k, 5)):
                            x = scr[(4 * B + q) % 6] if q < 4 else scn[b % 2]
                            A(x, x, ACT.Exp, bias=nmx[:, b % 2:b % 2 + 1], accum_out=ls5[:, b % 2, q:q + 1]).then_inc(s_exp, 1)
                for n in range(6):
                    g = 6 * l + n
                    w = S if n < 4 else H * NS
                    act.wait_ge(nps, g + 1)
                    if n >= 2:
                        act.wait_ge(o_ok, g - 1)
                    A(ev[n % 2][:, 0:w], bank[6 + n % 2][:, 0:w], ACT.Sqrt, bias=con("eps"), scale=1.0 / HD).then_inc(nrt, 1)
                norm_roots(2 * l + 1)
                act.wait_ge(lg_ok, NT * (l + 1) + l + 1)
                A(r4[:, 0], r4[:, 0], ACT.Exp).then_inc(rexp, 1)
                A(r1[:, 2], r1[:, 2], ACT.Exp).then_inc(rexp, 1)
                for e in range(NE + 1):
                    if e < NE:
                        E_ = l * NE + e
                        act.wait_ge(gu_ps, 2 * E_ + 1)
                        if E_ >= 2:
                            act.wait_ge(hg_ok, E_ - 1)
                        A(silu[e % 2], bank[2][:, :], ACT.Silu).then_inc(si_ok, 1)
                    if e >= 1:
                        E_ = l * NE + e - 1
                        act.wait_ge(y_ps, 2 * E_ + 1)
                        if E_ >= 2:
                            act.wait_ge(y_st[(e - 1) % 2], 16 * (E_ // 2))
                        A(yt[(e - 1) % 2][:, 0:W5], bank[5][:, :], ACT.Copy).then_inc(y_ok, 1)
                        act.wait_ge(y_ps, 2 * E_ + 2)
                        A(yt[(e - 1) % 2][:, W5:D], bank[6][:, :], ACT.Copy).then_inc(y_ok, 1)
                    if e < NE:
                        E_ = l * NE + e
                        act.wait_ge(ht_ps, E_ + 1)
                        A(hT[e % 2].rearrange("p c n -> p (c n)"), bank[4][:, :], ACT.Copy).then_inc(ht_ok, 1)

                def extra(t):
                    P_, A_ = t * XP["all"], t * XA["y"]
                    act.wait_ge(xp[l], P_ + XP["gate_up"])
                    A(silu[0], bank[2][:, :], ACT.Silu).then_inc(xa[l], 1)
                    act.wait_ge(xp[l], P_ + XP["h"])
                    A(hT[0].rearrange("p c n -> p (c n)"), bank[4][:, :], ACT.Copy).then_inc(xa[l], 1)
                    act.wait_ge(xp[l], P_ + XP["y"])
                    for n in range(2):
                        A(yt[0][:, n * W5:(n + 1) * W5], bank[5 + n][:, :], ACT.Copy).then_inc(xa[l], 1)
                for b in range(2):
                    act.wait_ge(y_st[b], 16 * (NE // 2) * (l + 1))
                extra_tiles(act, l + 1, extra)
            norm_roots(2 * L)

        @block.vector
        def _(dve):
            V = nc.vector
            made = {}

            def link(ins, signal=dv):
                made[signal.name] = made.get(signal.name, 0) + 1
                ins.then_inc(signal, 1)
                dve.wait_ge(signal, made[signal.name])

            def norm_tile(m, i):
                r = rows(i)
                dve.wait_ge(rt_ok, NT * m + i + 1)
                link(V.reciprocal(rs[0:r, i:i + 1], rt[0:r, i:i + 1]))
                if m < 2 * L:
                    if i >= 2:
                        dve.wait_ge(xt_ps, 2 * (NT * m + i - 2) + 2)
                        if m % 2:
                            dve.wait_ge(xn_st, 16 * (NT * (m // 2) + i - 1))
                    link(V.tensor_scalar(xn[i % 2][0:r, :], hid[0:r, i, :], rs[0:r, i:i + 1], None, ALU.mult), xn_ok)

            def norm_out(m, i):
                r = rows(i)
                wcol = (m // 2) if m % 2 == 0 else L + m // 2
                for j in range(2):
                    dve.wait_ge(xt_ps, 2 * (NT * m + i) + j + 1)
                    link(V.tensor_tensor(xT[:, 4 * j:4 * j + 4, tok(i)], bank[j][:, :].rearrange("p (c n) -> p c n", c=4)[:, :, 0:r],
                                    nw[:, wcol, 4 * j:4 * j + 4].unsqueeze(2).to_broadcast([P, 4, r]), ALU.mult), xt_ok)

            def norm(m):
                for i in range(NT):
                    norm_tile(m, i)
                    if i >= 1:
                        norm_out(m, i - 1)
                norm_out(m, NT - 1)

            link(V.memset(ssq[:, :], 1.0))
            for i in range(2):
                V.memset(qz[i], 0.0)
            V.memset(lg[:, :, :].rearrange("p a b -> p (a b)"), 0.0)
            dve.wait_ge(par, 16 * (NPAR + 1))
            link(V.tensor_tensor(lbt[:, 0], lbr[:, 0], lbr[:, 1], ALU.max))
            for l in range(L):
                link(V.tensor_tensor(lbe[:, l], lbr[:, l], lbt[:, 0], ALU.subtract))
                link(V.tensor_tensor(dlp[:, l], dl[:, l, 0:4:2, :], dl[:, l, 1:4:2, :], ALU.mult))
                link(V.tensor_reduce(dls[:, l, :], dlp[:, l], AX, ALU.add))
            link(V.tensor_copy(lbt[:, 1], lbt[:, 0]), prep_v)
            dve.wait_ge(prep_a, 2)
            link(V.tensor_tensor(lbt[:, 0], lbe[:, 0], lbe[:, 1], ALU.add))
            link(V.reciprocal(lbt[:, 0], lbt[:, 0]))
            for l in range(L):
                link(V.tensor_tensor(lbe[:, l], lbe[:, l], lbt[:, 0], ALU.mult))
            link(V.tensor_tensor(lb[:, 0], lbe[:, 0], lbe[:, 0], ALU.subtract))
            link(V.tensor_tensor(lb[:, 1], lbe[:, 0], lbe[:, 1], ALU.add))
            link(V.tensor_tensor(lb[:, 1], lb[:, 1], lbe[:, 0], ALU.subtract))
            for l in range(L):
                lam_init = 0.8 - 0.6 * math.exp(-0.3 * l)
                link(V.tensor_scalar(omlb[:, l], lb[:, l], -1.0, 1.0, ALU.mult, ALU.add))
                link(V.tensor_tensor(nlam[:, l:l + 1], dls[:, l, 1:2], dls[:, l, 0:1], ALU.subtract))
                link(V.tensor_scalar(nlam[:, l:l + 1], nlam[:, l:l + 1], lam_init, None, ALU.subtract))
                link(V.tensor_scalar(dnw[:, l:l + 1], dnw[:, l:l + 1], 1.0 - lam_init, None, ALU.mult))

            def rope(l, n):
                i = n % NT
                r = rows(i)
                dve.wait_ge(tp_ok, 15 * l + n + 1)
                x = qkt[n % 3][0:r, :].rearrange("p (g n) -> p g n", n=DK)
                hr = ROT // 2
                cb = cosT[0:r, i, :].unsqueeze(1).to_broadcast([r, 2 * H, ROT])
                V.tensor_tensor(rope_t[0:r], x[:, :, 0:ROT], cb, ALU.mult)
                V.tensor_tensor(rope_u[0:r, :, 0:hr], x[:, :, hr:ROT], sinT[0:r, i, 0:hr].unsqueeze(1).to_broadcast([r, 2 * H, hr]), ALU.mult)
                link(V.tensor_tensor(rope_u[0:r, :, hr:ROT], x[:, :, 0:hr], sinT[0:r, i, hr:ROT].unsqueeze(1).to_broadcast([r, 2 * H, hr]), ALU.mult))
                link(V.tensor_tensor(x[:, :, 0:ROT], rope_t[0:r], rope_u[0:r], ALU.add), roped)

            def qk_out(l, n):
                i = n % NT
                r = rows(i)
                dve.wait_ge(qk_ps, 10 * l + n + 1)
                src = bank[4 + n % 2][:, :].rearrange("p (h n) -> p h n", h=H)[:, :, 0:r]
                if n < NT:
                    dst = qT[:, :, tok(i)] if i < PT else qTs[:, :, :]
                    link(V.tensor_scalar(dst, src, DK ** -0.5, None, ALU.mult), qk_ok)
                else:
                    dst = kT[:, :, tok(i)] if i < PT else kTs[:, :, :]
                    link(V.tensor_copy(dst, src), qk_ok)

            def hgrn(l, item):
                kind, h, n = item
                hh = l * H + h
                E0 = blk(k_h, h)
                if kind == "prep":
                    dve.wait_ge(hi_t, hh + 1)
                    link(V.tensor_copy(itok, bank[6][:, :]), hi_ok)
                    band_prod(l, h, 0)
                elif kind == "band":
                    if n + 1 < C:
                        band_prod(l, h, n + 1)
                    w = C - n
                    dve.wait_ge(hbc, C * hh + n + 1)
                    src = bank[7][:, 0:NB * w].rearrange("p (b c) -> p b c", c=w)
                    o = oT[:, h, 0:S].rearrange("p (b c) -> p b c", c=C)
                    if n == 0:
                        link(V.tensor_tensor(o, src, blk(i_h, h), ALU.mult), hacc)
                    else:
                        t = tmp[:, 0:NB * w].rearrange("p (b c) -> p b c", c=w)
                        x = V.tensor_tensor(t, src, blk(i_h, h)[:, :, 0:w], ALU.mult)
                        link(x, hacc)
                        dve.wait_ge(hacc, C * hh + n + 1)
                        link(V.tensor_tensor(o[:, :, n:C], o[:, :, n:C], t, ALU.add))
                elif kind == "keys":
                    dve.wait_ge(hkt, hh + 1)
                    V.tensor_scalar(ktok_m[0], bank[6][:, :], con("even"), None, ALU.mult)
                    link(V.tensor_scalar(ktok_m[1], bank[6][:, :], con("odd"), None, ALU.mult), hkt_ok)
                elif kind == "round":
                    dve.wait_ge(hU, 2 * ((NB // 4) * hh + n + 1))
                    if n == 0:
                        dve.wait_ge(hF, hh + 1)
                        if hh:
                            dve.wait_ge(s_stored, 16 * hh)
                    elif n >= 2:
                        dve.wait_ge(hO, (NB // 4) * hh + n - 1)
                    for k in range(4):
                        b = 4 * n + k
                        u = bank[6][:, k * P:(k + 1) * P]
                        if k == 3 and n:
                            dve.wait_ge(hO, (NB // 4) * hh + n)
                        if b == 0:
                            x = V.tensor_copy(sring[1], u)
                        else:
                            x = V.scalar_tensor_tensor(sring[(b + 1) % 8], sring[b % 8], f15[:, b:b + 1], u, ALU.mult, ALU.add)
                        link(x, hS)
                        dve.wait_ge(hS, NB * hh + b + 1)
                elif kind == "close":
                    dve.wait_ge(hO, (NB // 4) * (hh + 1))
                    link(V.tensor_tensor(oT[:, h, C:S], oT[:, h, C:S], bank[7][:, C:S], ALU.add), hclose)

            def band_prod(l, h, n):
                hh = l * H + h
                g = C * hh + n
                dve.wait_ge(hE, g + 1)
                if n >= 2:
                    dve.wait_ge(hbc, g - 1)
                w = C - n
                e = blk(k_h, h) if n == 0 else ev[n % 2].rearrange("p (b c) -> p b c", c=C)[:, :, n:C]
                link(V.tensor_tensor(pv_[n % 2][:, 0:NB * w].rearrange("p (b c) -> p b c", c=w), e, blk(q_h, h)[:, :, n:C], ALU.mult), hP)

            def queries(l, b):
                if b >= 2:
                    dve.wait_ge(sq_ps, 5 * (l * DB + b - 1))
                for c in range(2):
                    a, z = 64 * c, 64 * (c + 1)
                    x = V.tensor_copy(qz[b % 2][a:z, :, DT * c:DT * (c + 1)], qTs[a:z, :, b * DT:(b + 1) * DT])
                link(x, qz_ok)

            def scores_out(l, g):
                G_ = l * NQ + g
                dve.wait_ge(sq_ps, qn(G_) + 1)
                if G_ >= 6:
                    dve.wait_ge(pt_ps, 6 * ((G_ - 6) // 4) + (G_ - 6) % 4 + 1)
                link(V.tensor_scalar(scr[G_ % 6], bank[2 + qn(G_) % 2][:, :], 1.0, None, ALU.mult, ALU.max,
                                     accum_out=mx5[:, g % 4:g % 4 + 1]), sq_ok)

            def new_out(l, b):
                B = l * DB + b
                dve.wait_ge(sq_ps, 5 * B + 5)
                if b >= 2:
                    dve.wait_ge(pt_ps, 6 * (B - 2) + 5)
                link(V.tensor_tensor(scn[b % 2], bank[2 + (5 * B + 4) % 2][:, 0:NS], smask[:, b, :], ALU.add), sq_ok)
                link(V.tensor_reduce(mx5[:, 4:5], scn[b % 2], AX, ALU.max))
                link(V.tensor_reduce(smx, mx5, AX, ALU.max))
                link(V.tensor_scalar(nmx[:, b % 2:b % 2 + 1], smx, -1.0, None, ALU.mult), s_neg)

            def p_out(l, b, q):
                B = l * DB + b
                dve.wait_ge(pt_ps, 6 * B + q + 1)
                n = 5 * B + q
                if n >= 2:
                    dve.wait_ge(pv_ps, n - 1)
                if q < 4:
                    link(V.tensor_copy(ptq[n % 2], bank[4][:, :].rearrange("p (j n) -> p j n", j=4)), pt_ok)
                else:
                    link(V.tensor_copy(ptq[n % 2][0:NS, 0, :], bank[4][0:NS, 0:P]), pt_ok)

            def o_rows(l, b):
                B = l * DB + b
                dve.wait_ge(s_exp, 5 * B + 5)
                link(V.tensor_reduce(sl, ls5[:, b % 2, :], AX, ALU.add))
                link(V.reciprocal(sinv, sl))
                dve.wait_ge(pv_ps, 5 * B + 5)
                link(V.tensor_scalar(on, bank[5][:, 0:HD], sinv, None, ALU.mult), s_on)

            def o_out(l, b):
                B = l * DB + b
                dve.wait_ge(pt_ps, 6 * B + 6)
                link(V.tensor_copy(so.rearrange("p h c t -> p h (c t)"), bank[4][:, 0:P].rearrange("p (h r) -> p h r", h=H)[:, :, 0:2 * DT]))
                link(V.scalar_tensor_tensor(oT[:, H:2 * H, S + b * DT:S + (b + 1) * DT], so[:, :, 1, :], nlam[:, l:l + 1], so[:, :, 0, :],
                                            ALU.mult, ALU.add), pt_ok)

            def hgrn_sample(l):
                sv = [a[:, :, S:TOK].rearrange("p h (b t) -> p h b t", t=DT) for a in (f_h, k_h, q_h, i_h)]
                f, k, q, i_ = sv
                link(V.tensor_copy(sF[:, :, :, 0], f[:, :, :, 0]))
                for t in range(1, DT):
                    link(V.tensor_tensor(sF[:, :, :, t], sF[:, :, :, t - 1], f[:, :, :, t], ALU.mult))
                at_ = 0
                for d in range(DT):
                    src = k if d == 0 else sE[:, H * (d % 2):H * (d % 2) + H]
                    if d:
                        prev = k if d == 1 else sE[:, H * ((d - 1) % 2):H * ((d - 1) % 2) + H]
                        link(V.tensor_tensor(src[:, :, :, d:DT], f[:, :, :, d:DT], prev[:, :, :, d - 1:DT - 1], ALU.mult))
                    V.tensor_copy(sK[:, :, :, DT - 1 - d], src[:, :, :, DT - 1])
                    w = DT - d
                    dst = pv_[0][:, at_:at_ + H * DB * w].rearrange("p (h b t) -> p h b t", h=H, t=w)
                    x = V.tensor_tensor(dst, src[:, :, :, d:DT], q[:, :, :, d:DT], ALU.mult)
                    if d < DT - 1:
                        link(x)
                    at_ += H * DB * w
                link(x, sh_p)
                dve.wait_ge(sh_p, 2 * l + 1)
                link(V.tensor_copy(f15.rearrange("p (h b) -> p h b", h=H), sF[:, :, :, DT - 1]))
                link(V.tensor_tensor(sF[:, :, :, :], sF[:, :, :, :], q, ALU.mult), sh_p)
                dve.wait_ge(sh_t, l + 1)
                V.tensor_copy(sitok, bank[0][0:NS, :])
                link(V.tensor_copy(sktok, bank[1][0:NS, :]))
                dve.wait_ge(sh_bcp, l + 1)
                at_ = 0
                for d in range(DT):
                    w = DT - d
                    src = bank[2][:, at_:at_ + H * DB * w].rearrange("p (h b t) -> p h b t", h=H, t=w)
                    if d == 0:
                        link(V.tensor_tensor(sA[:, :, :, :], src, i_, ALU.mult))
                    else:
                        link(V.tensor_tensor(sP[:, :, :, 0:w], src, i_[:, :, :, 0:w], ALU.mult))
                        link(V.tensor_tensor(sA[:, :, :, d:DT], sA[:, :, :, d:DT], sP[:, :, :, 0:w], ALU.add))
                    at_ += H * DB * w
                for b in range(DB):
                    B = l * DB + b
                    if b >= 2:
                        dve.wait_ge(sh_ps, B - 1)
                        dve.wait_ge(sh_st[b % 2], 16 * (l * (DB // 2) + b // 2))
                    elif l:
                        dve.wait_ge(sh_st[b % 2], 16 * (l * (DB // 2)))
                    link(V.tensor_scalar(smk[b % 2], sktok, con("batch", NS)[:, b:b + 1], None, ALU.mult), sh_m)
                    dve.wait_ge(sh_ps, B + 1)
                    for h in range(H):
                        x = V.scalar_tensor_tensor(s1[b % 2][:, h, :], s0[b % 2][:, h, :], f15[:, h * DB + b:h * DB + b + 1],
                                                   bank[4 + b % 2][:, h * P:(h + 1) * P], ALU.mult, ALU.add)
                    link(x, sh_s)
                o = oT[:, 0:H, S:TOK].rearrange("p h (b t) -> p h b t", t=DT)
                link(V.tensor_tensor(o, sA[:, :, :, :], bank[3][:, 0:DB * H * DT].rearrange("p (b h t) -> p h b t", b=DB, h=H), ALU.add))

            def parts(n):
                if n < 4:
                    return oT[:, n, 0:S], g_h[:, n, 0:S]
                if n == 4:
                    return oT[:, 0:H, S:TOK], g_h[:, :, S:TOK]
                return oT[:, H:2 * H, S:TOK], None

            def flat(a, n):
                w = S if n < 4 else H * NS
                return a[:, 0:w] if n < 4 else a[:, 0:w].rearrange("p (h n) -> p h n", h=H)

            def feature_norms(l):
                def square(n):
                    g = 6 * l + n
                    o, _ = parts(n)
                    if n >= 2:
                        dve.wait_ge(nps, g - 1)
                    link(V.tensor_tensor(flat(pv_[n % 2], n), o, o, ALU.mult), nsq)
                square(0)
                square(1)
                for n in range(6):
                    g = 6 * l + n
                    o, gt = parts(n)
                    dve.wait_ge(nrt, g + 1)
                    if n + 2 < 6:
                        square(n + 2)
                    e = flat(ev[n % 2], n)
                    link(V.reciprocal(e, e))
                    if n < 5:
                        link(V.scalar_tensor_tensor(o, o, hnw[:, l:l + 1], e, ALU.mult, ALU.mult))
                        link(V.tensor_tensor(o, o, gt, ALU.mult), o_ok)
                    else:
                        link(V.scalar_tensor_tensor(o, o, dnw[:, l:l + 1], e, ALU.mult, ALU.mult), o_ok)

            def first_of(dst, x, m, t):
                b = lambda a: a.unsqueeze(2).to_broadcast([P, NT, 4])
                link(V.tensor_reduce(m, x, AX, ALU.max))
                link(V.tensor_tensor(dst, x, b(m), ALU.is_equal))
                link(V.tensor_tensor(dst, dst, con("prio").unsqueeze(1).to_broadcast([P, NT, 4]), ALU.mult))
                link(V.tensor_reduce(t, dst, AX, ALU.max))
                link(V.tensor_tensor(dst, dst, b(t), ALU.is_equal))

            def route(l):
                b = lambda a: a.unsqueeze(2).to_broadcast([P, NT, 4])
                for i in range(NT):
                    r = rows(i)
                    n = NT * l + i
                    dve.wait_ge(lg_ps, n + 1)
                    link(V.tensor_tensor(lg[0:r, i, :], bank[4 + i % 2][0:r, 0:NG + NE], brt[0:r, l, :], ALU.add), lg_ok)
                    dve.wait_ge(lg_ok, n + 1 + l)
                lg1 = lg[:, :, 0:NG]
                lg2 = lg[:, :, NG:].rearrange("p i (g j) -> p i g j", g=NG)
                grp, o1, o2, lgg = r4[:, 1], r4[:, 2], r4[:, 3], r4[:, 4]
                first_of(grp, lg1, r1[:, 0], r1[:, 1])
                link(V.tensor_tensor(r4[:, 0], lg1, b(r1[:, 0]), ALU.subtract))
                for i in range(NT):
                    link(V.tensor_tensor(r16[:, i], lg2[:, i], grp[:, i].unsqueeze(2).to_broadcast([P, 4, 4]), ALU.mult))
                    link(V.tensor_reduce(lgg[:, i], r16[:, i].rearrange("p g j -> p j g"), AX, ALU.add))
                first_of(o1, lgg, r1[:, 3], r1[:, 1])
                link(V.scalar_tensor_tensor(r4[:, 5], o1, NEG, lgg, ALU.mult, ALU.add))
                first_of(o2, r4[:, 5], r1[:, 4], r1[:, 1])
                link(V.tensor_tensor(r1[:, 2], r1[:, 4], r1[:, 3], ALU.subtract))
                link(V.tensor_copy(r1[:, 5], r1[:, 4]), lg_ok)
                for i in range(NT):
                    for m, o in ((m1, o1), (m2, o2)):
                        link(V.tensor_tensor(m[:, i], grp[:, i].unsqueeze(2).to_broadcast([P, 4, 4]), o[:, i].unsqueeze(1).to_broadcast([P, 4, 4]), ALU.mult))
                        link(V.tensor_scalar(m[:, i], m[:, i], con("valid")[:, i:i + 1], None, ALU.mult))
                f1, f2 = (m.rearrange("p i g j -> p i (g j)") for m in (m1, m2))
                link(V.tensor_tensor(msk[:, :, :], f1, f2, ALU.add), msk_ok)
                dve.wait_ge(rexp, 2 * l + 2)
                link(V.tensor_reduce(r1[:, 0], r4[:, 0], AX, ALU.add))
                link(V.tensor_scalar(r1[:, 5], r1[:, 2], 1.0, None, ALU.add))
                link(V.tensor_tensor(r1[:, 0], r1[:, 0], r1[:, 5], ALU.mult))
                link(V.reciprocal(r1[:, 6], r1[:, 0]))
                link(V.tensor_tensor(r1[:, 7], r1[:, 6], r1[:, 2], ALU.mult))
                b16 = lambda a: a.unsqueeze(2).to_broadcast([P, NT, NE])
                t16 = r16.rearrange("p i g j -> p i (g j)")
                link(V.tensor_tensor(t16, f1, b16(r1[:, 6]), ALU.mult))
                link(V.tensor_tensor(psel[:, :, :], f2, b16(r1[:, 7]), ALU.mult))
                V.tensor_copy(tg[:, :, :, 0], b16(con("tokid")))
                link(V.tensor_tensor(tg[:, :, :, 1], t16, psel[:, :, :], ALU.add))
                dve.wait_ge(pos_ps, l + 1)
                link(V.tensor_copy(pos.rearrange("p i e -> p (i e)"), bank[6][:, 0:NT * NE]))
                link(V.scalar_tensor_tensor(psel[:, :, :], pos[:, :, :], 1.0, msk[:, :, :], ALU.add, ALU.mult))
                link(V.tensor_scalar(psel[:, :, :], psel[:, :, :], 1.0, None, ALU.subtract))
                link(V.tensor_copy(r1[:, 0], r1[:, 1]), psel_ok)
                cnt = bank[6][:, NT * NE:(NT + 1) * NE]
                link(V.tensor_scalar(cntx[:, 0], cnt, float(P), None, ALU.is_gt))
                for k in range(2, NT):
                    link(V.scalar_tensor_tensor(cntx[:, 0], cnt, float(P * k), cntx[:, 0], ALU.is_gt, ALU.add))
                link(V.tensor_tensor_scan(cntx[:, 1], ones[:, 0:NE], cntx[:, 0], 0.0, ALU.mult, ALU.add))
                link(V.tensor_tensor(cntx[:, 2], cntx[:, 1], cntx[:, 0], ALU.subtract))
                it = iota[:, 0:MAXX].unsqueeze(2).to_broadcast([P, MAXX, NE])
                be = lambda a: a.unsqueeze(1).to_broadcast([P, MAXX, NE])
                link(V.tensor_tensor(ohx[:, :, :], it, be(cntx[:, 2]), ALU.is_ge))
                link(V.tensor_tensor(ohx2[:, :, :], it, be(cntx[:, 1]), ALU.is_lt))
                link(V.tensor_tensor(ohx[:, :, :], ohx[:, :, :], ohx2[:, :, :], ALU.mult))
                link(V.tensor_tensor(ohx2[:, :, :], ohx[:, :, :], be(cntx[:, 2]), ALU.mult))
                link(V.tensor_reduce(kx[:, :], ohx2[:, :, :], AX, ALU.add))
                link(V.tensor_tensor(kx[:, :], iota[:, 0:MAXX], kx[:, :], ALU.subtract))
                link(V.tensor_scalar(kx[:, :], kx[:, :], 1.0, float(P), ALU.add, ALU.mult))
                link(V.tensor_tensor(ohx2[:, :, :], ohx[:, :, :], be(iota[:, 0:NE]), ALU.mult))
                link(V.tensor_reduce(exf[:, :], ohx2[:, :, :], AX, ALU.add))
                link(V.tensor_copy(exi[:, :], exf[:, :]))
                link(V.tensor_copy(nxi[:, :], cntx[:, 1, NE - 1:NE]))
                for k, f in enumerate((f1, f2)):
                    link(V.tensor_tensor(t16, f, pos[:, :, :], ALU.mult))
                    link(V.tensor_reduce(r1[:, 1], t16, AX, ALU.add))
                    link(V.tensor_tensor(t16, f, con("ebase").unsqueeze(1).to_broadcast([P, NT, NE]), ALU.mult))
                    link(V.tensor_reduce(rk[:, k], t16, AX, ALU.add))
                    link(V.tensor_tensor(rk[:, k], rk[:, k], r1[:, 1], ALU.add))
                    link(V.tensor_scalar(r1[:, 1], r1[:, 1], float(P), None, ALU.is_lt))
                    link(V.tensor_scalar(rk[:, k], rk[:, k], float(YROWS), None, ALU.subtract))
                    link(V.tensor_tensor(rk[:, k], rk[:, k], r1[:, 1], ALU.mult))
                    link(V.tensor_scalar(rk[:, k], rk[:, k], float(YROWS), None, ALU.add))
                link(V.tensor_copy(rki[:, :, :], rk[:, :, :]), rk_ok)

            def sel_build(l, e):
                E_ = l * NE + e
                if E_:
                    dve.wait_ge(id_ps, E_)
                link(V.tensor_tensor(sel, iota.unsqueeze(1).to_broadcast([P, NT, P]), psel[:, :, e].unsqueeze(2).to_broadcast([P, NT, P]),
                                ALU.is_equal), sel_ok)

            def ids_out(l, e):
                E_ = l * NE + e
                dve.wait_ge(id_ps, E_ + 1)
                V.tensor_copy(idx[:, e:e + 1], bank[7][:, 0:1])
                link(V.tensor_copy(gate[:, e:e + 1], bank[7][:, 1:2]), id_ok)

            for l in range(L):
                norm(2 * l)
                for n in range(15):
                    if n < 10:
                        rope(l, n)
                    if 1 <= n <= 10:
                        qk_out(l, n - 1)
                dve.wait_ge(fp_ok, 32 * l + 8)
                for h in range(H):
                    link(V.tensor_scalar(f_h[:, h, :], f_h[:, h, :], omlb[:, l, h:h + 1], lb[:, l, h:h + 1], ALU.mult, ALU.add))
                    V.tensor_scalar(k_h[:, h, :], k_h[:, h, :], omlb[:, l, h:h + 1], None, ALU.mult)
                    link(V.tensor_scalar(f_h[:, h, :], f_h[:, h, :], F_MIN, None, ALU.max), fk_ok)
                dve.wait_ge(fk_ok, H * (l + 1))
                for v in range(16 + 3):
                    if v < 16:
                        u, U = v, 16 * l + v
                        w = (u // H + 1) * P
                        dve.wait_ge(pa_qk, U + 1)
                        for c in range(2):
                            x = V.tensor_reduce(mx[:, u % 2, c:c + 1], bank[c + 2 * (u % 2)][:, 0:w], AX, ALU.max)
                        link(x)
                        link(V.tensor_scalar(mx[:, u % 2, :], mx[:, u % 2, :], -1.0, None, ALU.mult), pa_max)
                    if 1 <= v < 17:
                        u, U = v - 1, 16 * l + v - 1
                        w = (u // H + 1) * P
                        e0, e1 = (e_p[u % 2][c][:, 0:w] for c in range(2))
                        dve.wait_ge(pa_exp, U + 1)
                        link(V.reciprocal(rl[:, u % 2, :], ls[:, u % 2, :]))
                        link(V.tensor_tensor(rl[:, u % 2, 1:2], rl[:, u % 2, 1:2], nlam[:, l:l + 1], ALU.mult))
                        link(V.tensor_scalar(e1, e1, rl[:, u % 2, 1:2], None, ALU.mult))
                        link(V.scalar_tensor_tensor(e1, e0, rl[:, u % 2, 0:1], e1, ALU.mult, ALU.add), pa_comb)
                    if 3 <= v:
                        u, U = v - 3, 16 * l + v - 3
                        i, h = u // H, u % H
                        dve.wait_ge(pa_pv, U + 1)
                        if v == 3:
                            for k in range(3):
                                dve.wait_ge(st_k[k], 16 * (l + 1) * sum(1 for x_ in range(5, 10) if x_ % 3 == k))
                        link(V.tensor_copy(od[:, i, h * HD:(h + 1) * HD], bank[6 + u % 2][:, 0:HD]), pa_od)
                        dve.wait_ge(pa_od, U + 1)
                        o = od[:, i, h * HD:(h + 1) * HD]
                        x = V.tensor_tensor_reduce(odsq, o, o, 1.0, 0.0, ALU.mult, ALU.add, ssq16[:, i, h:h + 1])
                link(x, od_sq)
                dve.wait_ge(od_rt, l + 1)
                link(V.reciprocal(rt16[:, :, :], rt16[:, :, :]))
                for i in range(PT):
                    o = od[:, i, :].rearrange("p (h n) -> p h n", h=H)
                    link(V.tensor_tensor(o, o, rt16[:, i, :].unsqueeze(2).to_broadcast([P, H, HD]), ALU.mult), od_n)
                for i in range(PT):
                    dve.wait_ge(od_t, PT * l + i + 1)
                    link(V.tensor_scalar(oT[:, H:2 * H, tok(i)], bank[4 + i % 2][:, :].rearrange("p (h n) -> p h n", h=H),
                                    dnw[:, l:l + 1], None, ALU.mult), od_ok)
                queries(l, 0)
                dve.wait_ge(st_v, 16 * NT * (l + 1))
                for s in range(SLOTS):
                    if s % 4 == 0 and 1 <= s // 4 <= NQ:
                        scores_out(l, s // 4 - 1)
                        if s % NPG == 0:
                            new_out(l, s // NPG - 1)
                    b, k = s // NPG - 1, s % NPG
                    if k == 8 and b + 2 < DB:
                        queries(l, b + 2)
                    if b >= 0:
                        if 3 <= k < 8:
                            p_out(l, b, k - 3)
                        if k == 9:
                            o_rows(l, b)
                        if k == 10:
                            o_out(l, b)
                    if s < len(items):
                        hgrn(l, items[s])
                hgrn_sample(l)
                feature_norms(l)
                for n in range(10):
                    s, i = n // NT, n % NT
                    r = rows(i)
                    dve.wait_ge(wo_ps, 10 * l + n + 1)
                    hh_ = hid[0:r, i, s * W5:(s + 1) * W5]
                    link(V.tensor_tensor(hh_, hh_, bank[2 + n % 2][0:r, :], ALU.add), wo_add)
                norm(2 * l + 1)
                route(l)
                for e in range(NE):
                    sel_build(l, e)
                    ids_out(l, e)
                for e in range(NE + 1):
                    if e < NE:
                        E_ = l * NE + e
                        for j in range(2):
                            dve.wait_ge(xe_ps, 2 * E_ + j + 1)
                            link(V.tensor_tensor(xeT[e % 2][:, 4 * j:4 * j + 4, :], bank[j][:, :].rearrange("p (c n) -> p c n", c=4),
                                            nw[:, L + l, 4 * j:4 * j + 4].unsqueeze(2).to_broadcast([P, 4, P]), ALU.mult), xe_ok)
                    if e >= 1:
                        E_ = l * NE + e - 1
                        dve.wait_ge(si_ok, E_ + 1)
                        dve.wait_ge(gu_ps, 2 * E_ + 2)
                        if E_ >= 1:
                            dve.wait_ge(ht_ps, E_)
                        link(V.scalar_tensor_tensor(hgt, silu[(e - 1) % 2], gate[:, e - 1:e], bank[3][:, :], ALU.mult, ALU.mult), hg_ok)
                def extra(t):
                    P_, A_, V_ = t * XP["all"], t * XA["y"], t * XV["all"]
                    k = [0]

                    def step(ins):
                        k[0] += 1
                        ins.then_inc(xv[l], 1)
                        dve.wait_ge(xv[l], V_ + k[0])

                    t16 = r16.rearrange("p i g j -> p i (g j)")
                    oh = ohx[:, bass.ds(t, 1), :].to_broadcast([P, NT, NE])
                    step(V.tensor_tensor(t16, psel[:, :, :], oh, ALU.mult))
                    step(V.tensor_reduce(psx[:, :], t16, AX, ALU.add))
                    step(V.tensor_tensor(t16, tg[:, :, :, 1], oh, ALU.mult))
                    step(V.tensor_reduce(tgx[:, :, 1], t16, AX, ALU.add))
                    step(V.tensor_copy(tgx[:, :, 0], con("tokid")))
                    step(V.tensor_tensor(psx[:, :], psx[:, :], kx[:, bass.ds(t, 1)].to_broadcast([P, NT]), ALU.subtract))
                    step(V.tensor_tensor(sel, iota.unsqueeze(1).to_broadcast([P, NT, P]), psx[:, :].unsqueeze(2).to_broadcast([P, NT, P]), ALU.is_equal))
                    assert k[0] == XV["sel"]
                    dve.wait_ge(xp[l], P_ + XP["ids"])
                    step(V.tensor_copy(xid[:, :], bank[7][:, 0:1]))
                    step(V.tensor_copy(xidf[:, :], bank[7][:, 0:1]))
                    step(V.tensor_copy(xgt[:, :], bank[7][:, 1:2]))
                    assert k[0] == XV["ids"]
                    dve.wait_ge(xp[l], P_ + XP["x"])
                    for j in range(2):
                        step(V.tensor_tensor(xeT[0][:, 4 * j:4 * j + 4, :], bank[j][:, :].rearrange("p (c n) -> p c n", c=4),
                                             nw[:, L + l, 4 * j:4 * j + 4].unsqueeze(2).to_broadcast([P, 4, P]), ALU.mult))
                    assert k[0] == XV["x"]
                    dve.wait_ge(xa[l], A_ + XA["silu"])
                    step(V.scalar_tensor_tensor(hgt, silu[0], xgt[:, 0:1], bank[3][:, :], ALU.mult, ALU.mult))
                    assert k[0] == XV["h"]
                    for i in range(NT):
                        step(V.tensor_scalar(sel[:, i, :], iota, float(P * i), xidf[:, 0:1], ALU.add, ALU.is_equal))
                    assert k[0] == XV["back"]
                    for n in range(2):
                        dve.wait_ge(xp[l], P_ + XP["all"] - 1 + n)
                        for i in range(NT):
                            hh_ = hid[0:rows(i), i, n * W5:(n + 1) * W5]
                            step(V.tensor_tensor(hh_, hh_, bank[i][0:rows(i), :], ALU.add))
                    assert k[0] == XV["all"]
                extra_tiles(dve, l + 1, extra)

                for q in range(2 * NT):
                    i, k = q // 2, q % 2
                    r = rows(i)
                    n = 2 * NT * l + q
                    dve.wait_ge(yg_in[n % 3], 16 * (n // 3 + 1))
                    link_v = V.tensor_tensor(hid[0:r, i, :], hid[0:r, i, :], yg[n % 3][0:r, :], ALU.add)
                    link(link_v, moe_add)
                    dve.wait_ge(moe_add, n + 1)
            dve.wait_ge(fw_in, 16)
            for i in range(NT):
                r = rows(i)
                norm_tile(2 * L, i)
                link(V.scalar_tensor_tensor(hid[0:r, i, :], hid[0:r, i, :], rs[0:r, i:i + 1], xT_a[0:r, 0:D], ALU.mult, ALU.mult), out_ok)

        @block.gpsimd
        def _(pool):
            G = nc.gpsimd
            made = {}

            def link(ins, signal=pl):
                made[signal.name] = made.get(signal.name, 0) + 1
                ins.then_inc(signal, 1)
                pool.wait_ge(signal, made[signal.name])

            def hgrn(l, h):
                hh = l * H + h
                f, k, q = blk(f_h, h), blk(k_h, h), blk(q_h, h)
                kh = khat.rearrange("p (b c) -> p b c", c=C)
                Fb = Fq.rearrange("p (b c) -> p b c", c=C)
                if hh:
                    pool.wait_ge(hclose, hh)
                else:
                    pool.wait_ge(od_ok, PT)
                for d in range(C):
                    g = C * hh + d
                    src = k if d == 0 else ev[d % 2].rearrange("p (b c) -> p b c", c=C)
                    if d:
                        prev = k if d == 1 else ev[(d - 1) % 2].rearrange("p (b c) -> p b c", c=C)
                        if d >= 3:
                            pool.wait_ge(hP, g - 1)
                        link(G.tensor_tensor(src[:, :, d:C], f[:, :, d:C], prev[:, :, d - 1:C - 1], ALU.mult))
                    link(G.tensor_copy(kh[:, :, C - 1 - d], src[:, :, C - 1]), hE)
                link(G.tensor_copy(Fb[:, :, 0], f[:, :, 0]))
                for t in range(1, C):
                    link(G.tensor_tensor(Fb[:, :, t], Fb[:, :, t - 1], f[:, :, t], ALU.mult))
                link(G.tensor_copy(f15, Fb[:, :, C - 1]))
                link(G.tensor_tensor(Fb, Fb, q, ALU.mult), hF)
                pool.wait_ge(hS, NB * (hh + 1))
                G.dma_start(t_out["s_prompt"][l, 0, h], sring[NB % 8]).then_inc(s_stored, 16)

            def y_store(l, e):
                E_ = l * NE + e
                pool.wait_ge(y_ok, 2 * E_ + 2)
                G.dma_start(y_d[e * P:(e + 1) * P, :], yt[e % 2]).then_inc(y_st[e % 2], 16)

            pool.wait_ge(par, 16 * (NPAR + 1))
            G.dma_start(y_d[YROWS, :].rearrange("(p n) -> p n", n=8), con("zero")).then_inc(zero_st, 16)
            for l in range(L):
                for n in range(5, 10):
                    i = n % NT
                    r = rows(i)
                    pool.wait_ge(roped, 10 * l + n + 1)
                    dst = (t_out["k_prompt"][l, 0, tok(i)] if i < PT else t_out["k_sample"][l].rearrange("b t h n -> (b t) h n"))
                    G.dma_start(dst.rearrange("t h n -> t (h n)"), qkt[n % 3][0:r, :]).then_inc(st_k[n % 3], 16)
                for i in range(NT):
                    r = rows(i)
                    pool.wait_ge(tp_ok, 15 * l + 10 + i + 1)
                    dst = (t_out["v_prompt"][l, 0, tok(i)] if i < PT else t_out["v_sample"][l].rearrange("b t h n -> (b t) h n"))
                    G.dma_start(dst.rearrange("t h n -> t (h n)"), vtok[0:r, i, :]).then_inc(st_v, 16)
                if l:
                    pool.wait_ge(od_ok, PT * (l + 1))
                for h in range(H):
                    hgrn(l, h)
                pool.wait_ge(pt_ok, 6 * DB * (l + 1))
                for b in range(DB):
                    B = l * DB + b
                    if b >= 2:
                        pool.wait_ge(sh_s, B - 1)
                    G.dma_start(s0[b % 2], t_in["state_hgrn"][l, b].rearrange("h k v -> k h v")).then_inc(sh_in[b % 2], 16)
                    if b >= 1:
                        pool.wait_ge(sh_s, B)
                        G.dma_start(t_out["s_sample"][l, b - 1].rearrange("h k v -> k h v"), s1[(b - 1) % 2]).then_inc(sh_st[(b - 1) % 2], 16)
                pool.wait_ge(sh_s, (l + 1) * DB)
                G.dma_start(t_out["s_sample"][l, DB - 1].rearrange("h k v -> k h v"), s1[(DB - 1) % 2]).then_inc(sh_st[(DB - 1) % 2], 16)
                for i in range(NT):
                    r = rows(i)
                    pool.wait_ge(xn_ok, NT * (2 * l + 1) + i + 1)
                    if i:
                        pool.wait_ge(xn_st, 16 * (NT * l + i))
                    G.dma_start(xn_d[tok(i), :], xn[i % 2][0:r, :]).then_inc(xn_st, 16)
                pool.wait_ge(xn_st, 16 * NT * (l + 1))
                pool.wait_ge(st_v, 16 * NT * (l + 1))
                for b in range(2):
                    pool.wait_ge(sh_st[b], 16 * (DB // 2) * (l + 1))
                for e in range(NE):
                    E_ = l * NE + e
                    pool.wait_ge(id_ok, E_ + 1)
                    if e >= 2:
                        pool.wait_ge(xe_ps, 2 * (E_ - 1))
                    G.indirect_dma_start(out=xe[e % 2], out_offset=None, in_=xn_d,
                                         in_offset=bass.IndirectOffsetOnAxis(ap=idx[:, e:e + 1], axis=0)).then_inc(xe_in[e % 2], 16)
                    if e >= 2:
                        y_store(l, e - 2)
                for e in range(NE - 2, NE):
                    y_store(l, e)
                for b in range(2):
                    pool.wait_ge(y_st[b], 16 * (NE // 2) * (l + 1))

                def extra(t):
                    pool.wait_ge(xv[l], t * XV["all"] + XV["ids"])
                    pool.sem_inc(passed, 1)
                    G.indirect_dma_start(out=xe[0], out_offset=None, in_=xn_d,
                                         in_offset=bass.IndirectOffsetOnAxis(ap=xid[:, 0:1], axis=0)).then_inc(xg[l], 16)
                    pool.wait_ge(xv[l], t * XV["all"] + XV["all"])
                extra_tiles(pool, l + 1, extra)
                pool.wait_ge(zero_st, 16)
                for q in range(2 * NT):
                    i, k = q // 2, q % 2
                    r = rows(i)
                    n = 2 * NT * l + q
                    if q >= 3:
                        pool.wait_ge(moe_add, n - 2)
                    G.indirect_dma_start(out=yg[n % 3][0:r, :], out_offset=None, in_=y_d,
                                         in_offset=bass.IndirectOffsetOnAxis(ap=rki[0:r, k, i:i + 1], axis=0)).then_inc(yg_in[n % 3], 16)
            for i in range(NT):
                r = rows(i)
                pool.wait_ge(out_ok, i + 1)
                dst = t_out["y_prompt"][0, tok(i), :] if i < PT else t_out["y_sample"].rearrange("b t d -> (b t) d")
                G.dma_start(dst, hid[0:r, i, :]).then_inc(out_st, 16)
            pool.wait_ge(out_st, 16 * NT)
            pool.wait_ge(st_v, 16 * NT * L)
            pool.wait_ge(s_stored, 16 * H * L)
            for k in range(3):
                pool.wait_ge(st_k[k], 16 * L * sum(1 for x in range(5, 10) if x % 3 == k))
            for b in range(2):
                pool.wait_ge(sh_st[b], 16 * (DB // 2) * L)


_INS = ["x_prompt", "x_sample", "cache_k", "cache_v", "state_hgrn", "page_table", "attn_norm_w", "w_in", "hgrn_lb",
        "hgrn_norm_w", "diff_lambda", "diff_norm_w", "w_o", "ffn_norm_w", "w_r1", "b_r1", "w_r2", "b_r2",
        "w_gate", "w_up", "w_down", "final_norm_w"]
_OUTS = {"y_prompt": (1, S, D), "y_sample": (DB, DT, D), "k_prompt": (L, 1, S, H, HD), "v_prompt": (L, 1, S, H, HD),
         "s_prompt": (L, 1, H, HD, HD), "k_sample": (L, DB, DT, H, HD), "v_sample": (L, DB, DT, H, HD),
         "s_sample": (L, DB, H, HD, HD)}


def kernel(**inputs):
    import concourse.bacc as bacc
    from concourse.bass_utils import run_bass_kernel_spmd

    nc = bacc.Bacc("TRN2", target_bir_lowering=False, num_devices=1)
    arrays, t_in, t_out = {}, {}, {}
    for name in _INS:
        a = np.ascontiguousarray(inputs[name])
        arrays[f"in_{name}"] = a
        t_in[name] = nc.dram_tensor(f"in_{name}", a.shape, mybir.dt.from_np(a.dtype), kind="ExternalInput").ap()
    c = constants()[0]
    arrays["in_constants"] = c
    t_in["constants"] = nc.dram_tensor("in_constants", c.shape, F32, kind="ExternalInput").ap()
    for name, shape in _OUTS.items():
        t_out[name] = nc.dram_tensor(f"out_{name}", shape, F32, kind="ExternalOutput").ap()
    build(nc, t_in, t_out)
    r = run_bass_kernel_spmd(nc, [arrays], core_ids=[0])
    return tuple(r.results[0][f"out_{name}"] for name in _OUTS)
```

```python
import math
from contextlib import ExitStack

import concourse.bass as bass
from concourse import mybir
import numpy as np

ALU = mybir.AluOpType
ACT = mybir.ActivationFunctionType
F32 = mybir.dt.float32
U32 = mybir.dt.uint32
I32 = mybir.dt.int32
AX = mybir.AxisListType.X

L, D, S, DB, DT = 2, 1024, 512, 8, 4
H, DK, HD = 4, 64, 128
PAST, PAGE = 2048, 128
NPG = PAST // PAGE
P = 128
NS = DB * DT
TOK = S + NS
PT = S // P
NT = PT + 1
DC = D // P
WB = 512
NE, NG, EG, FF = 16, 4, 4, 512
C = 16
NB = S // C
EPS = 1e-6
NEG = -1e30
F_MIN = 1e-30
YROWS = NE * P
THETA = 500000.0
ROT = DK // 4
HALF = TOK // 2
MAXX = 2 * TOK // P
XV = {"sel": 7, "ids": 10, "x": 12, "h": 13, "back": 18, "low": 23, "all": 28}
XP = {"ids": 1, "x": 2, "gate_up": 3, "h": 4, "y": 5, "low": 6, "all": 7}
XA = {"silu": 1, "h": 2, "y": 4}


def rows(i):
    return P if i < PT else NS


def tok(i):
    return slice(i * P, i * P + rows(i))


def constants():
    p = np.arange(P)[:, None]
    f = np.arange(P)[None, :]
    pos = np.zeros((P, NT), np.float32)
    for i in range(PT):
        pos[:, i] = np.arange(P) + i * P
    pos[:NS, PT] = PAST + np.arange(NS) % DT
    inv = (np.float32(THETA) ** (-np.arange(0, ROT, 2, dtype=np.float32) / np.float32(ROT))).astype(np.float32)
    ang = (pos[:, :, None] * inv[None, None, :]).astype(np.float32)
    cos, sin = np.cos(ang).astype(np.float32), np.sin(ang).astype(np.float32)
    row, key = np.arange(P)[:, None, None] % DT, np.arange(NS)[None, None, :]
    batch = np.arange(DB)[None, :, None]
    smask = np.where((key // DT == batch) & (key % DT <= row), 0.0, NEG)
    valid = np.ones((P, NT), np.float32)
    valid[NS:, PT] = 0.0
    blocks = {
        "ident": (p == f), "cmask": np.where(f <= p, 0.0, NEG), "ones": np.ones((P, P)),
        "tri": (p < f), "iota": np.broadcast_to(f, (P, P)),
        "cos": np.concatenate([cos, cos], -1).reshape(P, -1),
        "sin": np.concatenate([-sin, sin], -1).reshape(P, -1),
        "smask": smask.reshape(P, -1), "valid": valid,
        "even": (p // C % 2 == 0), "odd": (p // C % 2 == 1),
        "batch": (p // DT == np.arange(DB)[None, :]),
        "tokid": p + P * np.arange(NT)[None, :] * np.ones((P, 1)),
        "ebase": np.broadcast_to(P * np.arange(NE)[None, :], (P, NE)),
        "prio": np.broadcast_to(4.0 - np.arange(4)[None, :], (P, 4)),
        "eps": np.full((P, 1), EPS), "zero": np.zeros((P, 8)),
    }
    at, cols = {}, 0
    for name, a in blocks.items():
        n = a.shape[1]
        at[name] = (cols, n)
        cols += n
    return np.concatenate([np.asarray(a, np.float32) for a in blocks.values()], 1), at


def hgrn_items():
    items = []
    for h in range(H):
        items.append(("prep", h, 0))
        items += [("band", h, d) for d in range(C)]
        items.append(("keys", h, 0))
        items += [("round", h, r) for r in range(NB // 4)]
        items += [("close", h, 0), ("merge", h, 0)]
    items += [("s_keys", 0, 0), ("s_turn", 0, 0)] + [("s_batch", 0, b) for b in range(DB)]
    items += [("norm", 0, n) for n in range(H + 1)]
    return items


def weight_plan():
    plan = []
    for l in range(L):
        plan += [("in", l, j, (2, 3, 0, 1)[j % 4]) for j in range(7)]
        plan += [("out", l, n, n) for n in range(2)]
        for e in range(NE):
            for k in range(3):
                plan.append((("gate", "up", "down")[k], l, e, (2, 3, 4, 5, 0, 1)[(3 * e + k) % 6]))
    where, count = {}, [0] * 6
    for what, l, j, slot in plan:
        count[slot] += 1
        where[(what, l, j)] = (slot, count[slot])
    return plan, where


SPLITS = (4, 5, 6, 1, 2, 0, 3)


def build(nc, t_in, t_out):
    cst_np, at = constants()
    items = hgrn_items()
    plan, where = weight_plan()
    ctx = ExitStack()
    with ctx:
        def sb(name, n, dt=F32):
            return ctx.enter_context(nc.sbuf_tensor(name, [P, n], dt))

        def sem(name):
            return ctx.enter_context(nc.semaphore(name))

        bank = [ctx.enter_context(nc.psum_tensor(f"bank{i}", [P, 512], F32)) for i in range(8)]

        hid_a = sb("hid", NT * D)
        xT_a = sb("xT", DC * TOK)
        w_a = sb("wslots", 4 * 4096)
        h_a = sb("hgrn", 5 * H * TOK)
        t_a = sb("heads", 2 * H * S + NT * WB)
        m_a = sb("temps", 6400)
        cst = sb("cst", cst_np.shape[1])
        hid = hid_a[:, :].rearrange("p (i n) -> p i n", i=NT)
        xT = xT_a[:, :].rearrange("p (c n) -> p c n", c=DC)
        oT = xT

        def con(name, r=P):
            o, n = at[name]
            return cst[0:r, o:o + n]

        ident, ones, iota = con("ident"), con("ones"), con("iota")
        cosT = con("cos").rearrange("p (i n) -> p i n", i=NT)
        sinT = con("sin").rearrange("p (i n) -> p i n", i=NT)
        smask = con("smask").rearrange("p (b n) -> p b n", b=DB)

        def wslot(s):
            return w_a[:, 4096 * s:4096 * (s + 1)] if s < 4 else h_a[:, 4096 * (s - 4):4096 * (s - 3)]

        def weights(key, chunks):
            return wslot(where[key][0]).rearrange("p (c n) -> p c n", c=chunks)

        kpage = [w_a[:, 512 * s:512 * (s + 1)].rearrange("p (h n) -> p h n", h=H) for s in range(8)]
        vquad = [w_a[:, 4096 + 2048 * v:6144 + 2048 * v].rearrange("p (j h n) -> p j h n", j=4, h=H) for v in range(5)]
        NK, NV = len(kpage), len(vquad)

        hv = h_a[:, :].rearrange("p (k h n) -> p k h n", k=5, h=H)
        f_h, k_h, q_h, i_h, g_h = (hv[:, k] for k in range(5))

        def blk(a, h):
            return a[:, h, 0:S].rearrange("p (b c) -> p b c", c=C)

        qT = t_a[:, 0:2048].rearrange("p (h n) -> p h n", h=H)
        kT = t_a[:, 2048:4096].rearrange("p (h n) -> p h n", h=H)
        vtok = t_a[:, 4096:4096 + NT * WB].rearrange("p (i n) -> p i n", i=NT)
        xn = [m_a[:, 1024 * i:1024 * (i + 1)] for i in range(2)]
        junk = m_a[:, 2048:3072]
        qkt = [m_a[:, 3072 + 512 * i:3584 + 512 * i] for i in range(3)]
        e_p = [[m_a[:, 1024 * i + 512 * c:1024 * i + 512 * (c + 1)] for c in range(2)] for i in range(2)]
        aT = [m_a[:, 2048 + 512 * i:2560 + 512 * i] for i in range(2)]
        od = m_a[:, 3072:5120].rearrange("p (i n) -> p i n", i=PT)
        odsq = m_a[:, 5120:5248]
        NR = 9
        ev = [m_a[:, 512 * i:512 * (i + 1)] for i in range(2)]
        pv_ = [m_a[:, 1024 + 512 * i:1536 + 512 * i] for i in range(2)]
        FQ = 2048
        Fq = m_a[:, FQ:FQ + 512]
        khat = m_a[:, 2560:3072]
        itok = m_a[:, 3072:3584]
        ktok_m = [m_a[:, 3584 + 512 * i:4096 + 512 * i] for i in range(2)]
        sring = [m_a[:, 4608 + 128 * i:4736 + 128 * i] for i in range(NR)]
        tmp = m_a[:, 5760:6272]
        f15 = m_a[:, 6272:6304]
        ktb = [a.rearrange("p (j h n) -> p j h n", j=4, h=H) for a in (w_a[:, 14336:16384], t_a[:, 0:2048])]
        scr = [t_a[:, 2048 + 512 * i:2560 + 512 * i] for i in range(6)]
        ptq = [t_a[:, 5120 + 512 * i:5632 + 512 * i].rearrange("p (j n) -> p j n", j=4) for i in range(2)]
        s0 = [a.rearrange("p (h n) -> p h n", h=H) for a in (ev[0], ev[1], pv_[1])]
        s1 = [a.rearrange("p (h n) -> p h n", h=H) for a in (Fq, tmp, pv_[0])]
        sitok, sktok = m_a[0:NS, 4608:5120], m_a[0:NS, 5120:5632]
        smk = [a[0:NS, :] for a in ktok_m]
        xe = [t_a[:, 1024 * i:1024 * (i + 1)] for i in range(2)]
        xeT = [t_a[:, 2048 + 1024 * i:3072 + 1024 * i].rearrange("p (c n) -> p c n", c=DC) for i in range(2)]
        yt = [t_a[:, 4096 + 1024 * i:5120 + 1024 * i] for i in range(2)]
        silu = [m_a[:, 3072 + 512 * i:3584 + 512 * i] for i in range(2)]
        hgt = m_a[:, 4096:4608]
        hT = [m_a[:, 4608 + 512 * i:5120 + 512 * i].rearrange("p (c n) -> p c n", c=4) for i in range(2)]
        sels = [m_a[:, o:o + NT * P].rearrange("p (i n) -> p i n", i=NT) for o in (5632, 2048)]
        sel = sels[0]
        yg = [h_a[:, 1024 * i:1024 * (i + 1)] for i in range(8)] + [m_a[:, 0:1024], m_a[:, 1024:2048]]

        smalls = sb("smalls", 2304)
        taken = [0]

        def shaped(a, shape):
            names = "abcd"[:len(shape)]
            if len(shape) == 1:
                return a
            return a.rearrange(f"p ({' '.join(names)}) -> p {' '.join(names)}", **dict(zip(names[:-1], shape)))

        def small(name, shape, dt=F32):
            n = int(np.prod(shape))
            a = smalls[:, taken[0]:taken[0] + n]
            taken[0] += n
            return shaped(a if dt == F32 else a.bitcast(dt), shape)

        qTs = small("qTs", (H, NS))
        kTs = small("kTs", (H, NS))
        qz = [small(f"q_padded{i}", (H, 32)) for i in range(2)]
        nw = small("norm_cols", (2 * L, DC))
        hnw = small("hgrn_norm_col", (L,))
        dnw = small("diff_norm_col", (L,))
        lbr = small("lb_raw", (L, H))
        lbe = small("lb_exp", (L, H))
        lb = small("lb", (L, H))
        omlb = small("one_minus_lb", (L, H))
        lbt = small("lb_tmp", (2, H))
        dl = shaped(h_a[:, 0:512], (L, 4, DK))
        dlp = shaped(h_a[:, 512:768], (L, 2, DK))
        dls = small("diff_sum", (L, 2))
        nlam = small("minus_lambda", (L,))
        wr = small("router", (L, DC, NG + NE))
        brt = small("router_bias", (L, NG + NE))
        ptab = small("page_ids", (DB * NPG,), I32)
        ssq = small("ssq", (NT,))
        rt = small("root", (NT,))
        rs = small("rstd", (NT,))
        rope_t = shaped(m_a[:, 4608:4736], (2 * H, ROT))
        rope_u = shaped(m_a[:, 4736:4864], (2 * H, ROT))
        mx = small("row_max", (2, 2))
        rl = shaped(m_a[:, 5248:5256], (4, 2))
        ls = small("row_sum", (2, 2))
        ssq16 = small("od_ssq", (PT, H))
        rt16 = small("od_root", (PT, H))
        scn = [small(f"new_scores{i}", (NS,)) for i in range(2)]
        mx5 = small("sample_maxes", (5,))
        smx = small("sample_max", (1,))
        nmx = small("sample_minus_max", (2,))
        ls5 = small("sample_sums", (2, 5))
        sinv = small("sample_inv", (1,))
        sl = small("sample_sum", (1,))
        on = small("sample_o_rows", (HD,))
        so = small("sample_o", (H, 2, DT))
        sF = shaped(m_a[:, 2560:2688], (H, DB, DT))
        sE = shaped(m_a[:, 2688:2944], (2 * H, DB, DT))
        sP = shaped(m_a[:, 2944:3072], (H, DB, DT))
        sK = shaped(m_a[:, 3072:3200], (H, DB, DT))
        sA = shaped(m_a[:, 3200:3328], (H, DB, DT))
        lg = small("logits", (NT, NG + NE))
        r4 = shaped(m_a[:, 4608:4728], (6, NT, 4))
        r1 = small("route1", (8, NT))
        r16 = small("route16", (NT, 4, 4))
        msk = small("expert_mask", (NT, NE))
        m1 = shaped(m_a[:, 4728:4808], (NT, 4, 4))
        m2 = shaped(m_a[:, 4808:4888], (NT, 4, 4))
        pos = shaped(m_a[:, 4888:4968], (NT, NE))
        psel = small("slot_or_none", (NT, NE))
        tg = small("id_and_gate", (NT, NE, 2))
        rk = small("y_rows_f", (2, NT))
        rki = small("y_rows", (2, NT), U32)
        idx = small("slot_tokens", (NE,), U32)
        gate = small("slot_gates", (NE,))
        cntx = shaped(m_a[:, 5096:5144], (3, NE))
        ohx = small("extra_expert", (MAXX, NE))
        ohx2 = shaped(m_a[:, 4968:5096], (MAXX, NE))
        kx = small("extra_first_slot", (MAXX,))
        exf = small("extra_expert_f", (MAXX,))
        exi = small("extra_expert_i", (MAXX,), I32)
        nxi = small("extra_count", (1,), I32)
        psx = small("extra_slot_of", (NT,))
        tgx = small("extra_id_and_gate", (NT, 2))
        xid = small("extra_tokens", (1,), U32)
        xidf = small("extra_tokens_f", (1,))
        xgt = small("extra_gates", (1,))

        xn_d = nc.dram_tensor("xn_scratch", [TOK, D], F32, kind="Internal").ap()
        y_d = nc.dram_tensor("y_scratch", [YROWS + 1, D], F32, kind="Internal").ap()

        first, par = sem("constants_loaded"), sem("params_loaded")
        xl = [sem(f"x_loaded{i}") for i in range(NT)]
        wl = [sem(f"w_loaded{i}") for i in range(6)]
        kl = [sem(f"k_loaded{i}") for i in range(NK)]
        vl = [sem(f"v_quad_loaded{i}") for i in range(NV)]
        prep_a, prep_v = sem("lb_exps"), sem("prep_steps")
        dv, ac, pl = sem("dve_steps"), sem("act_steps"), sem("pool_steps")
        rt_ok, xn_ok, xt_ps, xt_ok, xn_st = (sem(x) for x in ("root_ready", "xn_ready", "xt_in_psum", "xt_ready", "xn_stored"))
        tp_ps, tp_ok, roped, qk_ps, qk_ok = (sem(x) for x in ("tok_proj_psum", "tok_proj_ready", "roped", "qk_t_psum", "qk_t_ready"))
        st_k = [sem(f"k_stored{i}") for i in range(3)]
        st_v = sem("v_stored")
        fp_ps, fp_ok, fk_ok = sem("feat_proj_psum"), sem("feat_proj_ready"), sem("gates_ready")
        pa_qk, pa_max, pa_exp, pa_comb, pa_at, pa_ate, pa_pv, pa_od = (
            sem(x) for x in ("p_scores", "p_max", "p_exp", "p_mixed", "p_t_psum", "p_t_ready", "p_o_psum", "p_o_ready"))
        od_sq, od_rt, od_n, od_t, od_ok = (sem(x) for x in ("od_sums", "od_roots", "od_normed", "od_t_psum", "od_t_ready"))
        kt_ps, kt_ok, qz_ok, sq_ps, sq_ok, s_neg, s_exp, pt_ps, pt_ok, pv_ps, s_on, so_ok = (
            sem(x) for x in ("page_t_psum", "page_t_ready", "s_queries", "s_scores_psum", "s_scores_ready", "s_minus_max",
                             "s_exp", "s_p_t_psum", "s_p_t_ready", "s_values_psum", "s_o_rows", "s_o_ready"))
        hi_t, hi_ok, hE, hP, hQ, hbc, hacc, hsum, ho_t = (
            sem(x) for x in ("i_t_psum", "i_t_ready", "h_keys", "h_even_prod", "h_odd_prod", "h_band_psum", "h_band_taken",
                             "h_band_added", "h_o_t_psum"))
        hF, hkt, hkt_ok, hU, hS, hO, hO_sb, hclose, s_stored = (
            sem(x) for x in ("h_decay", "h_kt_psum", "h_kt_ready", "h_update_psum", "h_state", "h_inter_psum", "h_inter_rows", "h_closed", "s_stored"))
        sh_t, sh_m, sh_ps, sh_s, sh_bcp, sh_p = (
            sem(x) for x in ("sh_t_psum", "sh_masked", "sh_psum", "sh_state", "sh_band_psum", "sh_prod"))
        sh_in = [sem(f"sh_state_in{i}") for i in range(3)]
        sh_st = [sem(f"sh_stored{i}") for i in range(3)]
        nsq, nps, nrt, o_ok = (sem(x) for x in ("n_squares", "n_sums_psum", "n_roots", "o_ready"))
        wo_ps, wo_add = sem("wo_psum"), sem("wo_added")
        lg_ps, lg_ok, rexp, msk_ok, pos_ps, psel_ok, sel_ok, id_ps, id_ok, rk_ok = (
            sem(x) for x in ("logits_psum", "logits_ready", "route_exps", "masks_ready", "slots_psum", "slots_ready", "sel_ready", "ids_psum", "ids_ready", "rows_ready"))
        xe_in = [sem(f"xe_gathered{i}") for i in range(2)]
        xe_ps, xe_ok, gu_ps, si_ok, hg_ok, ht_ps, ht_ok, y_ps, y_ok = (
            sem(x) for x in ("xe_t_psum", "xe_t_ready", "gate_up_psum", "silu_ready", "h_ready", "h_t_psum", "h_t_ready", "y_psum", "y_ready"))
        y_st = [sem(f"y_stored{i}") for i in range(2)]
        yg_in = [sem(f"y_gathered{i}") for i in range(NT)]
        xw, xg, xv, xp, xa = ([sem(f"extra_{w}{l}") for l in range(L)] for w in ("weights", "gathered", "dve", "pe", "act"))
        passed = sem("extra_waits_passed")
        zero_st = sem("zero_row_stored")
        moe_add, out_ok, out_st = sem("moe_added"), sem("out_ready"), sem("out_stored")
        fw_in = sem("final_w_loaded")

        def turns(b):
            return (3, 5, 7, 9, 11) if b < DB - 1 else (3, 4, 5, 6, 7)

        NPAR = 12
        NQ = DB * NPG // 4
        SLOTS = DB * NPG + 11

        def qn(g):
            return 5 * (g // 4) + g % 4 + 1

        def state_count(l, b):
            per = sum(1 for x in range(DB) if x % 3 == b % 3)
            return 16 * (per * l + b // 3 + 1)

        def vn(g):
            return 5 * (g // 4) + g % 4

        def last_use(key):
            what, l, j = key
            if what == "in":
                return (tp_ps, 15 * l + NT * (j + 1)) if j < 3 else (fp_ps, 32 * l + 8 * (j - 2))
            if what == "out":
                return wo_ps, 10 * l + 2 * (NT - 1) + j + 1
            if what == "down":
                return y_ps, 2 * (NE * l + j) + 2
            return gu_ps, 2 * (NE * l + j) + (1 if what == "gate" else 2)

        def extra_tiles(eng, ready, body):
            eng.wait_ge(rk_ok, ready)
            n = eng.value_load(nxi[0:1, 0:1], min_val=0, max_val=MAXX)
            with eng.If(0 < n):
                with eng.Fori(0, MAXX) as t:
                    with eng.If(t < n):
                        body(t)
                        eng.sem_inc(passed, 1)

        def wwait(eng, key):
            slot, n = where[key]
            eng.wait_ge(wl[slot], 16 * n)

        block = ctx.enter_context(nc.Block())

        @block.sync
        def _(sp):
            with nc.allow_non_contiguous_dma(reason="small parameter columns"):
                def load_x(i):
                    src = t_in["x_prompt"][0, tok(i), :] if i < PT else t_in["x_sample"].rearrange("b t d -> (b t) d")
                    sp.dma_start(hid[0:rows(i), i, :], src).then_inc(xl[i], 16)

                load_x(0)
                sp.dma_start(cst[:, :], t_in["constants"]).then_inc(first, 16)
                sp.dma_start(nw[:, 0:L, :], t_in["attn_norm_w"].rearrange("l (c p) -> p l c", p=P)).then_inc(first, 16)
                for i in range(1, NT):
                    load_x(i)

                def load_w(n):
                    what, l, j, slot = plan[n]
                    cnt = where[(what, l, j)][1]
                    if cnt > 1:
                        before = next(k for k, v in where.items() if v == (slot, cnt - 1))
                        sp.wait_ge(*last_use(before))
                    if what == "in":
                        src = t_in["w_in"][l, :, SPLITS[j] * WB:(SPLITS[j] + 1) * WB]
                    elif what == "out":
                        src = t_in["w_o"][l, :, j * WB:(j + 1) * WB]
                    else:
                        src = t_in["w_" + what][l, j]
                    ch = 4 if what == "down" else DC
                    sp.dma_start(wslot(slot).rearrange("p (c n) -> p c n", c=ch),
                                 src.rearrange("(c p) n -> p c n", p=P)).then_inc(wl[slot], 16)

                load_w(0)
                sp.dma_start(nw[:, L:2 * L, :], t_in["ffn_norm_w"].rearrange("l (c p) -> p l c", p=P)).then_inc(par, 16)
                sp.dma_start(hnw[:, :], t_in["hgrn_norm_w"].rearrange("l p -> p l")).then_inc(par, 16)
                sp.dma_start(dnw[:, :], t_in["diff_norm_w"].rearrange("l p -> p l")).then_inc(par, 16)
                sp.dma_start(lbr[:, :, :], t_in["hgrn_lb"].rearrange("l (h p) -> p l h", p=P)).then_inc(par, 16)
                sp.dma_start(dl[:, :, :, :].rearrange("p a b c -> p (a b c)"),
                             t_in["diff_lambda"].rearrange("(o a) b c -> o (a b c)", o=1).to_broadcast([P, L * 4 * DK])).then_inc(par, 16)
                for l in range(L):
                    sp.dma_start(wr[:, l, :, 0:NG], t_in["w_r1"][l].rearrange("(c p) n -> p c n", p=P)).then_inc(par, 16)
                    sp.dma_start(wr[:, l, :, NG:], t_in["w_r2"][l].rearrange("(c p) n -> p c n", p=P)).then_inc(par, 16)
                sp.dma_start(brt[:, :, 0:NG], t_in["b_r1"].rearrange("(o l) n -> o l n", o=1).to_broadcast([P, L, NG])).then_inc(par, 16)
                sp.dma_start(brt[:, :, NG:], t_in["b_r2"].rearrange("(o l) n -> o l n", o=1).to_broadcast([P, L, NE])).then_inc(par, 16)
                sp.dma_start(ptab[0:1, :], t_in["page_table"].rearrange("(o b) j -> o (b j)", o=1)).then_inc(par, 16)
                for n in range(1, 4):
                    load_w(n)
                sp.wait_ge(par, 16 * NPAR)
                per = len(plan) // L
                for l in range(L):
                    for j in range(4 if l == 0 else 0, 7):
                        if l and j == 1:
                            sp.wait_ge(yg_in[NT - 1], 32 * l)
                        load_w(l * per + j)
                    sp.wait_ge(*last_use(("in", l, 6)))

                    def load_page(p, dst, cache, done):
                        page = sp.value_load(ptab[0:1, p:p + 1], min_val=0, max_val=t_in["cache_k"].shape[1] - 1)
                        sp.dma_start(dst.rearrange("p h n -> p (h n)"),
                                     cache[l, bass.ds(page, 1)].rearrange("o p h n -> (o p) (h n)")).then_inc(done, 16)

                    for g in range(NQ + 1):
                        for p in range(4 * g, min(4 * g + 4, DB * NPG)):
                            if p >= NK:
                                sp.wait_ge(kt_ps, l * DB * NPG + p - NK + 1)
                            load_page(p, kpage[p % NK], t_in["cache_k"], kl[p % NK])
                        if g:
                            v = l * NQ + g - 1
                            if g - 1 >= NV:
                                sp.wait_ge(pv_ps, vn(v - NV) + 1)
                            for j in range(4):
                                load_page(4 * (g - 1) + j, vquad[v % NV][:, j], t_in["cache_v"], vl[v % NV])
                    sp.wait_ge(kt_ps, (l + 1) * DB * NPG)
                    load_w(l * per + 7)
                    sp.wait_ge(pv_ps, (l + 1) * 5 * DB)
                    load_w(l * per + 8)
                    for q in range(3 * NE):
                        if q == 2:
                            sp.wait_ge(o_ok, 6 * (l + 1))
                        load_w(l * per + 9 + q)

                    def extra(t):
                        e = sp.value_load(exi[0:1, bass.ds(t, 1)], min_val=0, max_val=NE - 1)
                        for slot, what, ch in ((2, "gate", DC), (3, "up", DC), (4, "down", 4)):
                            if what == "down":
                                sp.wait_ge(xg[l], t * 16 + 16)
                            sp.dma_start(wslot(slot).rearrange("p (c n) -> p c n", c=ch),
                                         t_in["w_" + what][l, bass.ds(e, 1)].rearrange("o (c p) n -> p (o c) n", p=P)).then_inc(xw[l], 16)
                        sp.wait_ge(xp[l], t * XP["all"] + XP["y"])
                    sp.wait_ge(*last_use(("down", l, NE - 2)))
                    extra_tiles(sp, l + 1, extra)
                sp.wait_ge(moe_add, 10 * L)
                sp.dma_start(xT_a[:, 0:D], t_in["final_norm_w"].rearrange("(o n) -> o n", o=1).to_broadcast([P, D])).then_inc(fw_in, 16)

        @block.tensor
        def _(pe):
            mm, tr = nc.tensor.matmul, nc.tensor.transpose

            def norm_turn(m, i):
                pe.wait_ge(xn_ok, NT * m + i + 1)
                r = rows(i)
                for j in range(2):
                    n = 2 * (NT * m + i) + j
                    if n >= 2:
                        pe.wait_ge(xt_ok, n - 1)
                    for c in range(4):
                        k = 4 * j + c
                        x = tr(bank[j][:, c * P:c * P + r], xn[i % 2][0:r, k * P:(k + 1) * P], ident[0:r, 0:r])
                    x.then_inc(xt_ps, 1)

            def proj_tok(l, n):
                s, i = n // NT, n % NT
                r = rows(i)
                g = 15 * l + n
                if i == 0:
                    wwait(pe, ("in", l, s))
                pe.wait_ge(xt_ok, 10 * 2 * l + 2 * (i + 1))
                if g >= 2:
                    pe.wait_ge(tp_ok, g - 1)
                w = weights(("in", l, s), DC)
                for c in range(DC):
                    x = mm(bank[2 + n % 2][0:r, :], xT[:, c, tok(i)], w[:, c, :], start=(c == 0), stop=(c == DC - 1))
                x.then_inc(tp_ps, 1)

            def turn_qk(l, n):
                i = n % NT
                r = rows(i)
                g = 10 * l + n
                pe.wait_ge(roped, g + 1)
                if g >= 2:
                    pe.wait_ge(qk_ok, g - 1)
                for h in range(H):
                    x = tr(bank[4 + n % 2][:, h * P:h * P + r], qkt[n % 3][0:r, h * P:(h + 1) * P], ident[0:r, 0:r])
                x.then_inc(qk_ps, 1)

            def proj_feat(l, g):
                s, h, half = 3 + g // 8, g // 2 % 4, g % 2
                n = 32 * l + g
                if g % 8 == 0:
                    wwait(pe, ("in", l, s))
                if n >= 2:
                    pe.wait_ge(fp_ok, n - 1)
                w = weights(("in", l, s), DC)
                for c in range(DC):
                    x = mm(bank[6 + g % 2][:, 0:HALF], w[:, c, h * P:(h + 1) * P], xT[:, c, half * HALF:(half + 1) * HALF],
                           start=(c == 0), stop=(c == DC - 1))
                x.then_inc(fp_ps, 1)

            def scores(l, u):
                i, h, U = u // H, u % H, 16 * l + u
                if U >= 2:
                    pe.wait_ge(pa_exp, U - 1)
                for c in range(2):
                    o = bank[c + 2 * (u % 2)]
                    a, z = 64 * c, 64 * (c + 1)
                    q = qT[a:z, h, tok(i)]
                    if i > 0:
                        mm(o[:, 0:i * P], q, kT[a:z, h, 0:i * P], start=True, stop=True)
                    mm(o[:, i * P:(i + 1) * P], q, kT[a:z, h, tok(i)], start=True, stop=False)
                    x = mm(o[:, i * P:(i + 1) * P], ident, con("cmask"), start=False, stop=True)
                x.then_inc(pa_qk, 1)

            def turn_a(l, u):
                i, U = u // H, 16 * l + u
                pe.wait_ge(pa_comb, U + 1)
                if U >= 2:
                    pe.wait_ge(pa_ate, U - 1)
                for j in range(i + 1):
                    x = tr(bank[4 + u % 2][:, j * P:(j + 1) * P], e_p[u % 2][1][:, j * P:(j + 1) * P], ident)
                x.then_inc(pa_at, 1)

            def values(l, u):
                i, h, U = u // H, u % H, 16 * l + u
                pe.wait_ge(pa_ate, U + 1)
                if U >= 2:
                    pe.wait_ge(pa_od, U - 1)
                for j in range(i + 1):
                    x = mm(bank[6 + u % 2][:, 0:HD], aT[u % 2][:, j * P:(j + 1) * P], vtok[:, j, h * HD:(h + 1) * HD],
                           start=(j == 0), stop=(j == i))
                x.then_inc(pa_pv, 1)

            def page_turn(l, s):
                g = l * DB * NPG + s
                pe.wait_ge(kl[s % NK], 16 * (l * (DB * NPG // NK) + s // NK + 1))
                if g >= 2:
                    pe.wait_ge(kt_ok, g - 1)
                for h in range(H):
                    x = tr(bank[s % 2][:, h * P:(h + 1) * P], kpage[s % NK][:, h, :], ident)
                x.then_inc(kt_ps, 1)

            def quad_scores(l, g):
                G_ = l * NQ + g
                Q = qn(G_)
                pe.wait_ge(kt_ok, 4 * G_ + 4)
                pe.wait_ge(qz_ok, G_ // 4 + 1)
                pe.wait_ge(sq_ok, Q)
                for h in range(H):
                    x = mm(bank[2][32 * h:32 * h + 32, :], qz[g // 4 % 2][:, h, :], ktb[g % 2][:, :, h, :], start=True, stop=True)
                x.then_inc(sq_ps, 1)

            def new_scores(l, b):
                B = l * DB + b
                pe.wait_ge(qz_ok, B + 1)
                if B:
                    pe.wait_ge(sq_ok, 5 * B)
                for h in range(H):
                    x = mm(bank[2][32 * h:32 * h + 32, 0:NS], qz[b % 2][:, h, :], kTs[:, h, :], start=True, stop=True)
                x.then_inc(sq_ps, 1)

            def turn_p(l, b, q):
                B = l * DB + b
                pe.wait_ge(s_exp, 5 * B + q + 1)
                if q:
                    pe.wait_ge(pt_ok, 5 * B + q)
                elif B:
                    pe.wait_ge(so_ok, B)
                if q < 4:
                    for j in range(4):
                        x = tr(bank[4][:, j * P:(j + 1) * P], scr[(4 * B + q) % 6][:, j * P:(j + 1) * P], ident)
                else:
                    x = tr(bank[4][0:NS, 0:P], scn[b % 2], ident)
                x.then_inc(pt_ps, 1)

            def quad_values(l, b, q):
                B = l * DB + b
                pe.wait_ge(pt_ok, 5 * B + q + 1)
                if q == 0 and B:
                    pe.wait_ge(s_on, B)
                par = (5 * B + q) % 2
                if q < 4:
                    v = l * NQ + 4 * b + q
                    pe.wait_ge(vl[v % NV], 64 * (v // NV + 1))
                    for j in range(4):
                        for h in range(H):
                            x = mm(bank[5][32 * h:32 * h + 32, 0:HD], ptq[par][:, j, 32 * h:32 * h + 32], vquad[v % NV][:, j, h, :],
                                   start=(q == 0 and j == 0), stop=False)
                else:
                    for h in range(H):
                        x = mm(bank[5][32 * h:32 * h + 32, 0:HD], ptq[par][0:NS, 0, 32 * h:32 * h + 32],
                               vtok[0:NS, PT, h * HD:(h + 1) * HD], start=False, stop=True)
                x.then_inc(pv_ps, 1)

            def turn_o(l, b):
                B = l * DB + b
                pe.wait_ge(s_on, B + 1)
                pe.wait_ge(pt_ok, 5 * B + 5)
                tr(bank[4][:, 0:P], on, ident).then_inc(pt_ps, 1)

            def hgrn(l, item):
                kind, h, n = item
                hh = l * H + h
                if kind == "prep":
                    if hh >= 1:
                        pe.wait_ge(hclose, hh)
                    for i in range(PT):
                        x = tr(bank[6][:, i * P:(i + 1) * P], i_h[:, h, tok(i)], ident)
                    x.then_inc(hi_t, 1)
                elif kind == "band":
                    g = C * hh + n
                    pe.wait_ge(hQ if n % 2 else hP, C // 2 * hh + n // 2 + 1)
                    if n == 1:
                        pe.wait_ge(hi_ok, hh + 1)
                    if g >= 2:
                        pe.wait_ge(hacc, g - 1)
                    mm(bank[7 - n % 2][:, 0:NB * (C - n)], ones, pv_[n % 2][:, 0:NB * (C - n)], start=True, stop=True).then_inc(hbc, 1)
                elif kind == "keys":
                    pe.wait_ge(hacc, C * (hh + 1))
                    pe.wait_ge(hE, C * hh + C)
                    for i in range(PT):
                        x = tr(bank[6][:, i * P:(i + 1) * P], khat[:, i * P:(i + 1) * P], ident)
                    x.then_inc(hkt, 1)
                elif kind == "round":
                    if n == 0:
                        pe.wait_ge(hkt_ok, hh + 1)
                    elif n >= 2:
                        pe.wait_ge(hS, NB * hh + 4 * (n - 1))
                    for k in range(4):
                        b = 4 * n + k
                        rr = slice(32 * (b // 2 % 4), 32 * (b // 2 % 4) + 32)
                        tile_ = b // 8
                        x = mm(bank[3 if n % 2 else 6][:, k * P:(k + 1) * P], ktok_m[b % 2][rr, tile_ * P:(tile_ + 1) * P],
                               itok[rr, tile_ * P:(tile_ + 1) * P], start=True, stop=True)
                        if k % 2:
                            x.then_inc(hU, 1)
                        if k == 1:
                            if n >= 2:
                                inter(l, h, n - 2)
                            pe.wait_ge(hU, 2 * ((NB // 4) * hh + n) + 1)
                elif kind == "close":
                    inter(l, h, NB // 4 - 2)
                    inter(l, h, NB // 4 - 1)
                elif kind == "merge":
                    pe.wait_ge(hS, NB * (hh + 1))
                    for half in range(2):
                        pe.wait_ge(hO_sb, 2 * hh + half + 1)
                        for j in range(4):
                            x = tr(bank[3 if half else 6][:, j * P:(j + 1) * P], ev[half][:, j * P:(j + 1) * P], ident)
                    x.then_inc(ho_t, 1)
                elif kind == "s_turn":
                    sample_turn(l)
                elif kind == "s_batch":
                    sample_batch(l, n)
                elif kind == "norm":
                    feature_sums(l, n)

            def inter(l, h, n):
                hh = l * H + h
                pe.wait_ge(hF, hh + 1)
                if n == 4:
                    pe.wait_ge(hO_sb, 2 * hh + 1)
                for g in range(4):
                    b = 4 * n + g
                    pe.wait_ge(hS, NB * hh + max(b, 1))
                    x = mm(bank[7][32 * g:32 * g + 32, n % 4 * P:(n % 4 + 1) * P], m_a[:, FQ + b * C:FQ + b * C + 32],
                           sring[max(b, 1) % NR], start=True, stop=True)
                x.then_inc(hO, 1)

            def sample_turn(l):
                pe.wait_ge(hclose, (l + 1) * H)
                pe.wait_ge(sh_p, 1 + 2 * l)
                for h in range(H):
                    tr(bank[6][0:NS, h * P:(h + 1) * P], i_h[:, h, S:TOK], ident)
                for h in range(H):
                    x = tr(bank[7][0:NS, h * P:(h + 1) * P], sK[:, h].rearrange("p b t -> p (b t)"), ident)
                x.then_inc(sh_t, 1)
                pe.wait_ge(sh_p, 2 + 2 * l)
                mm(bank[3][:, 0:H * DB * 10], ones, pv_[0][:, 0:H * DB * 10], start=True, stop=True).then_inc(sh_bcp, 1)

            def sample_batch(l, b):
                B = l * DB + b
                pe.wait_ge(sh_m, B + 1)
                if b >= 2:
                    pe.wait_ge(sh_s, B - 1)
                for h in range(H):
                    mm(bank[6 + b % 2][:, h * P:(h + 1) * P], smk[b % 2][:, h * P:(h + 1) * P], sitok[:, h * P:(h + 1) * P],
                       start=True, stop=True)
                pe.wait_ge(sh_in[b % 3], state_count(l, b))
                for h in range(H):
                    x = mm(bank[3][:, (b * H + h) * DT:(b * H + h + 1) * DT], s0[b % 3][:, h, :], sF[:, h, b, :],
                           start=True, stop=True)
                x.then_inc(sh_ps, 1)

            def feature_sums(l, n):
                g = 6 * l + n
                pe.wait_ge(nsq, g + 1)
                if g >= 2:
                    pe.wait_ge(nrt, g - 1)
                w = S if n < 4 else H * NS
                mm(bank[6 + n % 2][:, 0:w], ones, pv_[n % 2][:, 0:w], start=True, stop=True).then_inc(nps, 1)

            def out_proj(l, n):
                i, s = n // 2, n % 2
                r, g = rows(i), 10 * l + n
                if i == 0:
                    wwait(pe, ("out", l, s))
                if g >= 2:
                    pe.wait_ge(wo_add, g - 1)
                w = weights(("out", l, s), DC)
                for c in range(DC):
                    x = mm(bank[2 + n % 2][0:r, :], oT[:, c, tok(i)], w[:, c, :], start=(c == 0), stop=(c == DC - 1))
                x.then_inc(wo_ps, 1)

            def logits(l, i):
                n = NT * l + i
                pe.wait_ge(xt_ok, 10 * (2 * l + 1) + 2 * (i + 1))
                if i >= 2:
                    pe.wait_ge(lg_ok, n - 1 + l)
                for c in range(DC):
                    x = mm(bank[4 + i % 2][0:rows(i), 0:NG + NE], xT[:, c, tok(i)], wr[:, l, c, :], start=(c == 0), stop=(c == DC - 1))
                x.then_inc(lg_ps, 1)

            def slot_ids(l, e):
                E_ = l * NE + e
                pe.wait_ge(sel_ok, E_ + 1)
                if e >= 1:
                    pe.wait_ge(id_ok, E_)
                for i in range(NT):
                    x = mm(bank[7][:, 0:2], sels[e % 2][:, i, :], tg[:, i, e, :], start=(i == 0), stop=(i == NT - 1))
                x.then_inc(id_ps, 1)

            def x_turn(l, e):
                E_ = l * NE + e
                pe.wait_ge(xe_in[e % 2], 16 * (l * (NE // 2) + e // 2 + 1))
                if E_ >= 1:
                    pe.wait_ge(xe_ok, 2 * E_)
                for j in range(2):
                    for c in range(4):
                        k = 4 * j + c
                        x = tr(bank[j][:, c * P:(c + 1) * P], xe[e % 2][:, k * P:(k + 1) * P], ident)
                    x.then_inc(xe_ps, 1)

            def gate_up(l, e):
                E_ = l * NE + e
                pe.wait_ge(xe_ok, 2 * E_ + 2)
                if E_ >= 1:
                    pe.wait_ge(hg_ok, E_)
                for k, what in enumerate(("gate", "up")):
                    wwait(pe, (what, l, e))
                    w = weights((what, l, e), DC)
                    for c in range(DC):
                        x = mm(bank[2 + k][:, :], xeT[e % 2][:, c, :], w[:, c, :], start=(c == 0), stop=(c == DC - 1))
                    x.then_inc(gu_ps, 1)

            def h_turn(l, e):
                E_ = l * NE + e
                pe.wait_ge(hg_ok, E_ + 1)
                if E_ >= 1:
                    pe.wait_ge(ht_ok, E_)
                for c in range(4):
                    x = tr(bank[4][:, c * P:(c + 1) * P], hgt[:, c * P:(c + 1) * P], ident)
                x.then_inc(ht_ps, 1)

            def down(l, e):
                E_ = l * NE + e
                pe.wait_ge(ht_ok, E_ + 1)
                wwait(pe, ("down", l, e))
                w = weights(("down", l, e), 4)
                for n in range(2):
                    if E_ >= 1:
                        pe.wait_ge(y_ok, 2 * E_ - 1 + n)
                    for c in range(4):
                        x = mm(bank[5 + n][:, :], hT[e % 2][:, c, :], w[:, c, n * WB:(n + 1) * WB], start=(c == 0), stop=(c == 3))
                    x.then_inc(y_ps, 1)

            pe.wait_ge(first, 32)
            for l in range(L):
                if l:
                    pe.wait_ge(y_ok, 2 * NE * l)
                for i in range(NT):
                    norm_turn(2 * l, i)
                for n in range(15):
                    proj_tok(l, n)
                    if 1 <= n <= 10:
                        turn_qk(l, n - 1)
                for g in range(32):
                    proj_feat(l, g)
                pe.wait_ge(tp_ok, 15 * (l + 1))
                pe.wait_ge(fp_ok, 32 * (l + 1))
                pe.wait_ge(qk_ok, 10 * (l + 1))
                for v in range(16 + 3):
                    if v < 16:
                        scores(l, v)
                    if 2 <= v < 18:
                        turn_a(l, v - 2)
                    if 3 <= v:
                        values(l, v - 3)
                pe.wait_ge(pa_ate, 16 * (l + 1))
                for i in range(PT):
                    n = PT * l + i
                    pe.wait_ge(od_n, n + 1)
                    if n >= 2:
                        pe.wait_ge(od_ok, n - 1)
                    for h in range(H):
                        x = tr(bank[4 + i % 2][:, h * P:(h + 1) * P], od[:, i, h * P:(h + 1) * P], ident)
                    x.then_inc(od_t, 1)
                pe.wait_ge(od_ok, PT * (l + 1))
                pe.wait_ge(pa_od, 16 * (l + 1))
                pe.wait_ge(pa_exp, 16 * (l + 1))
                for s in range(SLOTS):
                    if s < DB * NPG:
                        page_turn(l, s)
                    if s % 4 == 0 and 1 <= s // 4 <= NQ:
                        quad_scores(l, s // 4 - 1)
                    b, k = s // NPG - 1, s % NPG
                    if k == 2 and b + 1 < DB:
                        new_scores(l, b + 1)
                    if b >= 0:
                        if k in turns(b):
                            turn_p(l, b, turns(b).index(k))
                        if k - 1 in turns(b):
                            quad_values(l, b, turns(b).index(k - 1))
                        if k == turns(b)[4] + 3:
                            turn_o(l, b)
                    if s < len(items):
                        hgrn(l, items[s])
                pe.wait_ge(so_ok, DB * (l + 1))
                feature_sums(l, H + 1)
                pe.wait_ge(o_ok, 6 * (l + 1))
                pe.wait_ge(sh_s, DB * (l + 1))
                for i in range(NT + 2):
                    if i < NT:
                        out_proj(l, 2 * i)
                        out_proj(l, 2 * i + 1)
                    if 1 <= i <= NT:
                        norm_turn(2 * l + 1, i - 1)
                    if i >= 2:
                        logits(l, i - 2)
                pe.wait_ge(msk_ok, l + 1)
                mm(bank[6][:, 0:NE], con("tri"), msk[:, 0, :], start=True, stop=True)
                for j in range(NT):
                    later = msk[:, j, :].unsqueeze(1).to_broadcast([P, NT - j, NE])
                    if j == NT - 1:
                        mm(bank[6][:, NE:NT * NE].rearrange("p (i e) -> p i e", e=NE), con("tri"), msk[:, 1:NT, :],
                           start=False, stop=False)
                    x = mm(bank[6][:, (j + 1) * NE:(NT + 1) * NE].rearrange("p (i e) -> p i e", e=NE), ones, later,
                           start=(j == 0), stop=(j == NT - 1))
                x.then_inc(pos_ps, 1)
                pe.wait_ge(psel_ok, l + 1)
                slot_ids(l, 0)
                slot_ids(l, 1)
                pe.wait_ge(xt_ok, 10 * (2 * l + 2))
                pe.wait_ge(wo_add, 10 * (l + 1))
                x_turn(l, 0)
                for e in range(NE):
                    gate_up(l, e)
                    if e >= 1:
                        down(l, e - 1)
                    if e + 2 < NE:
                        slot_ids(l, e + 2)
                    if e + 1 < NE:
                        x_turn(l, e + 1)
                    h_turn(l, e)
                down(l, NE - 1)

                def extra(t):
                    V_, A_ = t * XV["all"], t * XA["y"]
                    pe.wait_ge(xv[l], V_ + XV["sel"])
                    for i in range(NT):
                        x = mm(bank[7][:, 0:2], sel[:, i, :], tgx[:, i, :], start=(i == 0), stop=(i == NT - 1))
                    x.then_inc(xp[l], 1)
                    pe.wait_ge(xg[l], t * 16 + 16)
                    for k in range(DC):
                        x = tr(bank[k // 4][:, k % 4 * P:(k % 4 + 1) * P], xe[0][:, k * P:(k + 1) * P], ident)
                    x.then_inc(xp[l], 1)
                    pe.wait_ge(xv[l], V_ + XV["x"])
                    pe.wait_ge(xw[l], t * 48 + 48)
                    for k in range(2):
                        w = wslot(2 + k).rearrange("p (c n) -> p c n", c=DC)
                        for c in range(DC):
                            x = mm(bank[2 + k][:, :], xeT[0][:, c, :], w[:, c, :], start=(c == 0), stop=(c == DC - 1))
                    x.then_inc(xp[l], 1)
                    pe.wait_ge(xv[l], V_ + XV["h"])
                    for c in range(4):
                        x = tr(bank[4][:, c * P:(c + 1) * P], hgt[:, c * P:(c + 1) * P], ident)
                    x.then_inc(xp[l], 1)
                    pe.wait_ge(xa[l], A_ + XA["h"])
                    w = wslot(4).rearrange("p (c n) -> p c n", c=4)
                    for n in range(2):
                        for c in range(4):
                            x = mm(bank[5 + n][:, :], hT[0][:, c, :], w[:, c, n * WB:(n + 1) * WB], start=(c == 0), stop=(c == 3))
                    x.then_inc(xp[l], 1)
                    pe.wait_ge(xa[l], A_ + XA["y"])
                    pe.wait_ge(xv[l], V_ + XV["back"])
                    for n in range(2):
                        if n:
                            pe.wait_ge(xv[l], V_ + XV["low"])
                        for i in range(NT):
                            x = mm(bank[i][0:rows(i), :], sel[:, i, 0:rows(i)], yt[0][:, n * WB:(n + 1) * WB], start=True, stop=True)
                        x.then_inc(xp[l], 1)
                    pe.wait_ge(xv[l], V_ + XV["all"])

                pe.wait_ge(y_ok, 2 * NE * (l + 1))
                extra_tiles(pe, l + 1, extra)

        @block.scalar
        def _(act):
            A = nc.scalar.activation
            steps = [0]

            def link(ins):
                steps[0] += 1
                ins.then_inc(ac, 1)
                act.wait_ge(ac, steps[0])

            def norm_roots(m):
                for i in range(NT):
                    r = rows(i)
                    if m == 0:
                        act.wait_ge(xl[i], 16)
                    elif m % 2:
                        act.wait_ge(wo_add, 10 * (m // 2) + 2 * (i + 1))
                    else:
                        act.wait_ge(moe_add, 10 * (m // 2 - 1) + 2 * i + 2)
                    link(A(junk[0:r, :], hid[0:r, i, :], ACT.Square, accum_out=ssq[0:r, i:i + 1]))
                    A(rt[0:r, i:i + 1], ssq[0:r, i:i + 1], ACT.Sqrt, bias=con("eps")[0:r, :], scale=1.0 / D).then_inc(rt_ok, 1)

            def feature_root(l, n):
                g = 6 * l + n
                w = S if n < 4 else H * NS
                act.wait_ge(nps, g + 1)
                if n >= 2:
                    act.wait_ge(o_ok, g - 1)
                A(ev[n % 2][:, 0:w], bank[6 + n % 2][:, 0:w], ACT.Sqrt, bias=con("eps"), scale=1.0 / HD).then_inc(nrt, 1)

            act.wait_ge(first, 32)
            for l in range(L):
                norm_roots(2 * l)
                if l == 0:
                    act.wait_ge(prep_v, 1)
                    A(lbe[:, :, :], lbe[:, :, :], ACT.Exp).then_inc(prep_a, 1)
                    A(dls[:, :, :], dls[:, :, :], ACT.Exp).then_inc(prep_a, 1)
                for n in range(15):
                    s, i, g = n // NT, n % NT, 15 * l + n
                    r = rows(i)
                    act.wait_ge(tp_ps, g + 1)
                    if s < 2:
                        if n >= 3:
                            act.wait_ge(qk_ps, 10 * l + n - 2)
                        if l or n >= 8:
                            per = [sum(1 for x in range(5, 10) if x % 3 == k) for k in range(3)]
                            done = per[n % 3] * l + sum(1 for x in range(5, n) if x % 3 == n % 3)
                            if done:
                                act.wait_ge(st_k[n % 3], 16 * done)
                        dst = qkt[n % 3][0:r, :]
                    else:
                        dst = vtok[0:r, i, :]
                    A(dst, bank[2 + n % 2][0:r, :], ACT.Copy).then_inc(tp_ok, 1)
                for g in range(32):
                    s, h, half = g // 8, g // 2 % 4, g % 2
                    cols = slice(half * HALF, (half + 1) * HALF)
                    act.wait_ge(fp_ps, 32 * l + g + 1)
                    src = bank[6 + g % 2][:, 0:HALF]
                    if s == 0:
                        A(f_h[:, h, cols], src, ACT.Sigmoid)
                        x = A(k_h[:, h, cols], src, ACT.Sigmoid, scale=-1.0)
                    elif s == 1:
                        x = A(i_h[:, h, cols], src, ACT.Copy)
                    elif s == 2:
                        x = A(q_h[:, h, cols], src, ACT.Copy, scale=float(HD) ** -0.5)
                    else:
                        x = A(g_h[:, h, cols], src, ACT.Sigmoid)
                    x.then_inc(fp_ok, 1)
                for v in range(16 + 3):
                    if v < 16:
                        u, U = v, 16 * l + v
                        w = (u // H + 1) * P
                        act.wait_ge(pa_max, U + 1)
                        if v >= 2:
                            act.wait_ge(pa_at, U - 1)
                        for c in range(2):
                            x = A(e_p[u % 2][c][:, 0:w], bank[c + 2 * (u % 2)][:, 0:w], ACT.Exp,
                                  bias=mx[:, u % 2, c:c + 1], accum_out=ls[:, u % 2, c:c + 1])
                        x.then_inc(pa_exp, 1)
                    if 2 <= v < 18:
                        u, U = v - 2, 16 * l + v - 2
                        w = (u // H + 1) * P
                        act.wait_ge(pa_at, U + 1)
                        if v >= 4:
                            act.wait_ge(pa_pv, U - 1)
                        A(aT[u % 2][:, 0:w], bank[4 + u % 2][:, 0:w], ACT.Copy).then_inc(pa_ate, 1)
                act.wait_ge(od_sq, l + 1)
                A(rt16[:, :, :], ssq16[:, :, :], ACT.Sqrt, bias=con("eps"), scale=1.0 / HD).then_inc(od_rt, 1)
                act.wait_ge(od_t, PT * (l + 1))
                for s in range(SLOTS):
                    if s < len(items) and items[s][0] in ("round", "merge"):
                        kind, h, n = items[s]
                        hh = l * H + h
                        if kind == "merge" or n == 6:
                            half = int(kind == "merge")
                            act.wait_ge(hO, NB // 4 * hh + 4 * (half + 1))
                            A(ev[half], bank[7][:, :], ACT.Copy).then_inc(hO_sb, 1)
                    if s < DB * NPG:
                        G_ = l * NQ + s // 4
                        act.wait_ge(kt_ps, l * DB * NPG + s + 1)
                        if G_ >= 2:
                            act.wait_ge(sq_ps, qn(G_ - 2) + 1)
                        A(ktb[s // 4 % 2][:, s % 4].rearrange("p h n -> p (h n)"), bank[s % 2][:, :], ACT.Copy).then_inc(kt_ok, 1)
                    b, k = s // NPG - 1, s % NPG
                    if b >= 0 and 1 <= k < 4:
                        B = l * DB + b
                        act.wait_ge(s_neg, B + 1)
                        for q in range(2 * (k - 1), min(2 * k, 5)):
                            x = scr[(4 * B + q) % 6] if q < 4 else scn[b % 2]
                            A(x, x, ACT.Exp, bias=nmx[:, b % 2:b % 2 + 1], accum_out=ls5[:, b % 2, q:q + 1]).then_inc(s_exp, 1)
                    if b >= 0 and k in turns(b):
                        q = turns(b).index(k)
                        n = 5 * (l * DB + b) + q
                        act.wait_ge(pt_ps, 6 * (l * DB + b) + q + 1)
                        if n >= 2:
                            act.wait_ge(pv_ps, n - 1)
                        if q < 4:
                            A(ptq[n % 2], bank[4][:, :].rearrange("p (j n) -> p j n", j=4), ACT.Copy).then_inc(pt_ok, 1)
                        else:
                            A(ptq[n % 2][0:NS, 0, :], bank[4][0:NS, 0:P], ACT.Copy).then_inc(pt_ok, 1)
                    if s < len(items) and items[s][0] == "norm":
                        feature_root(l, items[s][2])
                feature_root(l, H + 1)
                for b in range(DB - 3, DB):
                    act.wait_ge(sh_st[b % 3], state_count(l, b))
                norm_roots(2 * l + 1)
                act.wait_ge(lg_ok, NT * (l + 1) + l + 1)
                A(r4[:, 0], r4[:, 0], ACT.Exp).then_inc(rexp, 1)
                A(r1[:, 2], r1[:, 2], ACT.Exp).then_inc(rexp, 1)
                for e in range(NE + 1):
                    if e < NE:
                        E_ = l * NE + e
                        act.wait_ge(gu_ps, 2 * E_ + 1)
                        if E_ >= 2:
                            act.wait_ge(hg_ok, E_ - 1)
                        A(silu[e % 2], bank[2][:, :], ACT.Silu).then_inc(si_ok, 1)
                    if e >= 1:
                        E_ = l * NE + e - 1
                        act.wait_ge(y_ps, 2 * E_ + 1)
                        if E_ >= 2:
                            act.wait_ge(y_st[(e - 1) % 2], 16 * (E_ // 2))
                        A(yt[(e - 1) % 2][:, 0:WB], bank[5][:, :], ACT.Copy).then_inc(y_ok, 1)
                        act.wait_ge(y_ps, 2 * E_ + 2)
                        A(yt[(e - 1) % 2][:, WB:D], bank[6][:, :], ACT.Copy).then_inc(y_ok, 1)
                    if e < NE:
                        E_ = l * NE + e
                        act.wait_ge(ht_ps, E_ + 1)
                        A(hT[e % 2].rearrange("p c n -> p (c n)"), bank[4][:, :], ACT.Copy).then_inc(ht_ok, 1)

                def extra(t):
                    P_, A_ = t * XP["all"], t * XA["y"]
                    act.wait_ge(xp[l], P_ + XP["gate_up"])
                    A(silu[0], bank[2][:, :], ACT.Silu).then_inc(xa[l], 1)
                    act.wait_ge(xp[l], P_ + XP["h"])
                    A(hT[0].rearrange("p c n -> p (c n)"), bank[4][:, :], ACT.Copy).then_inc(xa[l], 1)
                    act.wait_ge(xp[l], P_ + XP["y"])
                    for n in range(2):
                        A(yt[0][:, n * WB:(n + 1) * WB], bank[5 + n][:, :], ACT.Copy).then_inc(xa[l], 1)
                for b in range(2):
                    act.wait_ge(y_st[b], 16 * (NE // 2) * (l + 1))
                extra_tiles(act, l + 1, extra)
            norm_roots(2 * L)

        @block.vector
        def _(dve):
            V = nc.vector
            made = {}

            def link(ins, signal=dv):
                made[signal.name] = made.get(signal.name, 0) + 1
                ins.then_inc(signal, 1)
                dve.wait_ge(signal, made[signal.name])

            def tell(ins, signal):
                made[signal.name] = made.get(signal.name, 0) + 1
                ins.then_inc(signal, 1)

            def norm_tile(m, i):
                r = rows(i)
                dve.wait_ge(rt_ok, NT * m + i + 1)
                link(V.reciprocal(rs[0:r, i:i + 1], rt[0:r, i:i + 1]))
                if m < 2 * L:
                    if i >= 2:
                        dve.wait_ge(xt_ps, 2 * (NT * m + i - 2) + 2)
                        if m % 2:
                            dve.wait_ge(xn_st, 16 * (NT * (m // 2) + i - 1))
                    link(V.tensor_scalar(xn[i % 2][0:r, :], hid[0:r, i, :], rs[0:r, i:i + 1], None, ALU.mult), xn_ok)

            def norm_out(m, i):
                r = rows(i)
                wcol = (m // 2) if m % 2 == 0 else L + m // 2
                for j in range(2):
                    dve.wait_ge(xt_ps, 2 * (NT * m + i) + j + 1)
                    link(V.tensor_tensor(xT[:, 4 * j:4 * j + 4, tok(i)], bank[j][:, :].rearrange("p (c n) -> p c n", c=4)[:, :, 0:r],
                                    nw[:, wcol, 4 * j:4 * j + 4].unsqueeze(2).to_broadcast([P, 4, r]), ALU.mult), xt_ok)

            def norm(m):
                for i in range(NT):
                    norm_tile(m, i)
                    if i >= 1:
                        norm_out(m, i - 1)
                norm_out(m, NT - 1)

            for i in range(2):
                V.memset(qz[i], 0.0)
            V.memset(lg[:, :, :].rearrange("p a b -> p (a b)"), 0.0)
            dve.wait_ge(first, 32)
            norm(0)
            dve.wait_ge(par, 16 * NPAR)
            link(V.tensor_tensor(lbt[:, 0], lbr[:, 0], lbr[:, 1], ALU.max))
            for l in range(L):
                link(V.tensor_tensor(lbe[:, l], lbr[:, l], lbt[:, 0], ALU.subtract))
                link(V.tensor_tensor(dlp[:, l], dl[:, l, 0:4:2, :], dl[:, l, 1:4:2, :], ALU.mult))
                link(V.tensor_reduce(dls[:, l, :], dlp[:, l], AX, ALU.add))
            link(V.tensor_copy(lbt[:, 1], lbt[:, 0]), prep_v)
            dve.wait_ge(prep_a, 2)
            link(V.tensor_tensor(lbt[:, 0], lbe[:, 0], lbe[:, 1], ALU.add))
            link(V.reciprocal(lbt[:, 0], lbt[:, 0]))
            for l in range(L):
                link(V.tensor_tensor(lbe[:, l], lbe[:, l], lbt[:, 0], ALU.mult))
            link(V.tensor_tensor(lb[:, 0], lbe[:, 0], lbe[:, 0], ALU.subtract))
            link(V.tensor_tensor(lb[:, 1], lbe[:, 0], lbe[:, 1], ALU.add))
            link(V.tensor_tensor(lb[:, 1], lb[:, 1], lbe[:, 0], ALU.subtract))
            for l in range(L):
                lam_init = 0.8 - 0.6 * math.exp(-0.3 * l)
                link(V.tensor_scalar(omlb[:, l], lb[:, l], -1.0, 1.0, ALU.mult, ALU.add))
                link(V.tensor_tensor(nlam[:, l:l + 1], dls[:, l, 1:2], dls[:, l, 0:1], ALU.subtract))
                link(V.tensor_scalar(nlam[:, l:l + 1], nlam[:, l:l + 1], lam_init, None, ALU.subtract))
                link(V.tensor_scalar(dnw[:, l:l + 1], dnw[:, l:l + 1], 1.0 - lam_init, None, ALU.mult))

            def rope(l, n):
                i = n % NT
                r = rows(i)
                dve.wait_ge(tp_ok, 15 * l + n + 1)
                x = qkt[n % 3][0:r, :].rearrange("p (g n) -> p g n", n=DK)
                hr = ROT // 2
                cb = cosT[0:r, i, :].unsqueeze(1).to_broadcast([r, 2 * H, ROT])
                V.tensor_tensor(rope_t[0:r], x[:, :, 0:ROT], cb, ALU.mult)
                V.tensor_tensor(rope_u[0:r, :, 0:hr], x[:, :, hr:ROT], sinT[0:r, i, 0:hr].unsqueeze(1).to_broadcast([r, 2 * H, hr]), ALU.mult)
                link(V.tensor_tensor(rope_u[0:r, :, hr:ROT], x[:, :, 0:hr], sinT[0:r, i, hr:ROT].unsqueeze(1).to_broadcast([r, 2 * H, hr]), ALU.mult))
                link(V.tensor_tensor(x[:, :, 0:ROT], rope_t[0:r], rope_u[0:r], ALU.add), roped)

            def qk_out(l, n):
                i = n % NT
                r = rows(i)
                dve.wait_ge(qk_ps, 10 * l + n + 1)
                src = bank[4 + n % 2][:, :].rearrange("p (h n) -> p h n", h=H)[:, :, 0:r]
                if n < NT:
                    dst = qT[:, :, tok(i)] if i < PT else qTs[:, :, :]
                    link(V.tensor_scalar(dst, src, DK ** -0.5, None, ALU.mult), qk_ok)
                else:
                    dst = kT[:, :, tok(i)] if i < PT else kTs[:, :, :]
                    link(V.tensor_copy(dst, src), qk_ok)

            def hgrn(l, item):
                kind, h, n = item
                hh = l * H + h
                E0 = blk(k_h, h)
                if kind == "prep":
                    dve.wait_ge(hi_t, hh + 1)
                    link(V.tensor_copy(itok, bank[6][:, :]), hi_ok)
                    band_prod(l, h, 0)
                elif kind == "band":
                    if n % 2 and n + 1 < C:
                        band_prod(l, h, n + 1)
                    w = C - n
                    dve.wait_ge(hbc, C * hh + n + 1)
                    src = bank[7 - n % 2][:, 0:NB * w].rearrange("p (b c) -> p b c", c=w)
                    o = oT[:, h, 0:S].rearrange("p (b c) -> p b c", c=C)
                    if n == 0:
                        tell(V.tensor_tensor(o, src, blk(i_h, h), ALU.mult), hacc)
                    else:
                        if (C - 1) * hh + n - 1:
                            dve.wait_ge(hsum, (C - 1) * hh + n - 1)
                        t = tmp[:, 0:NB * w].rearrange("p (b c) -> p b c", c=w)
                        tell(V.tensor_tensor(t, src, blk(i_h, h)[:, :, 0:w], ALU.mult), hacc)
                        dve.wait_ge(hacc, C * hh + n + 1)
                        tell(V.tensor_tensor(o[:, :, n:C], o[:, :, n:C], t, ALU.add), hsum)
                elif kind == "keys":
                    dve.wait_ge(hkt, hh + 1)
                    V.tensor_scalar(ktok_m[0], bank[6][:, :], con("even"), None, ALU.mult)
                    link(V.tensor_scalar(ktok_m[1], bank[6][:, :], con("odd"), None, ALU.mult), hkt_ok)
                elif kind == "round":
                    dve.wait_ge(hU, 2 * ((NB // 4) * hh + n + 1))
                    if n == 0:
                        dve.wait_ge(hF, hh + 1)
                        if hh:
                            dve.wait_ge(s_stored, 16 * hh)
                    elif n >= 2:
                        dve.wait_ge(hO, (NB // 4) * hh + n - 1)
                    for k in range(4):
                        b = 4 * n + k
                        u = bank[3 if n % 2 else 6][:, k * P:(k + 1) * P]
                        if b == 0:
                            x = V.tensor_copy(sring[1], u)
                        else:
                            x = V.scalar_tensor_tensor(sring[(b + 1) % NR], sring[b % NR], f15[:, b:b + 1], u, ALU.mult, ALU.add)
                        link(x, hS)
                        dve.wait_ge(hS, NB * hh + b + 1)
                elif kind == "merge":
                    dve.wait_ge(ho_t, hh + 1)
                    dve.wait_ge(hsum, (C - 1) * (hh + 1))
                    o = oT[:, h, 0:S].rearrange("p (b c) -> p b c", c=C)
                    first_, rest = (bank[k][:, :].rearrange("p (b c) -> p b c", c=32)[:, :, 0:C] for k in (6, 3))
                    V.tensor_tensor(o[:, 1:NB // 2], o[:, 1:NB // 2], first_[:, 1:NB // 2], ALU.add)
                    link(V.tensor_tensor(o[:, NB // 2:NB], o[:, NB // 2:NB], rest, ALU.add), hclose)
                elif kind == "s_keys":
                    sample_keys(l)
                elif kind == "s_turn":
                    sample_turned(l)
                elif kind == "s_batch":
                    sample_batch(l, n)
                elif kind == "norm":
                    feature_norm(l, n)

            def band_prod(l, h, n):
                hh = l * H + h
                g = C * hh + n
                dve.wait_ge(hE, g + 1)
                if n >= 2:
                    dve.wait_ge(hbc, g - 1)
                w = C - n
                e = blk(k_h, h) if n == 0 else ev[0].rearrange("p (b c) -> p b c", c=C)[:, :, n:C]
                tell(V.tensor_tensor(pv_[0][:, 0:NB * w].rearrange("p (b c) -> p b c", c=w), e, blk(q_h, h)[:, :, n:C], ALU.mult), hP)

            def queries(l, b):
                if b >= 2:
                    dve.wait_ge(sq_ps, 5 * (l * DB + b - 1))
                for c in range(2):
                    a, z = 64 * c, 64 * (c + 1)
                    x = V.tensor_copy(qz[b % 2][a:z, :, DT * c:DT * (c + 1)], qTs[a:z, :, b * DT:(b + 1) * DT])
                link(x, qz_ok)

            def scores_out(l, g):
                G_ = l * NQ + g
                dve.wait_ge(sq_ps, qn(G_) + 1)
                if G_ >= 6:
                    dve.wait_ge(pt_ps, 6 * ((G_ - 6) // 4) + (G_ - 6) % 4 + 1)
                tell(V.tensor_scalar(scr[G_ % 6], bank[2][:, :], 1.0, None, ALU.mult, ALU.max,
                                     accum_out=mx5[:, g % 4:g % 4 + 1]), sq_ok)

            def new_out(l, b):
                B = l * DB + b
                dve.wait_ge(sq_ps, 5 * B + 1)
                if b >= 2:
                    dve.wait_ge(pt_ps, 6 * (B - 2) + 5)
                link(V.tensor_tensor(scn[b % 2], bank[2][:, 0:NS], smask[:, b, :], ALU.add), sq_ok)
                link(V.tensor_reduce(mx5[:, 4:5], scn[b % 2], AX, ALU.max))

            def max_out(l, b):
                dve.wait_ge(sq_ok, 5 * (l * DB + b) + 5)
                link(V.tensor_reduce(smx, mx5, AX, ALU.max))
                link(V.tensor_scalar(nmx[:, b % 2:b % 2 + 1], smx, -1.0, None, ALU.mult), s_neg)

            def o_rows(l, b):
                B = l * DB + b
                dve.wait_ge(s_exp, 5 * B + 5)
                link(V.tensor_reduce(sl, ls5[:, b % 2, :], AX, ALU.add))
                link(V.reciprocal(sinv, sl))
                dve.wait_ge(pv_ps, 5 * B + 5)
                link(V.tensor_scalar(on, bank[5][:, 0:HD], sinv, None, ALU.mult), s_on)

            def o_out(l, b):
                B = l * DB + b
                dve.wait_ge(pt_ps, 6 * B + 6)
                link(V.tensor_copy(so.rearrange("p h c t -> p h (c t)"), bank[4][:, 0:P].rearrange("p (h r) -> p h r", h=H)[:, :, 0:2 * DT]))
                link(V.scalar_tensor_tensor(oT[:, H:2 * H, S + b * DT:S + (b + 1) * DT], so[:, :, 1, :], nlam[:, l:l + 1], so[:, :, 0, :],
                                            ALU.mult, ALU.add), so_ok)

            def sample_keys(l):
                sv = [a[:, :, S:TOK].rearrange("p h (b t) -> p h b t", t=DT) for a in (f_h, k_h, q_h, i_h)]
                f, k, q, i_ = sv
                link(V.tensor_copy(sF[:, :, :, 0], f[:, :, :, 0]))
                for t in range(1, DT):
                    link(V.tensor_tensor(sF[:, :, :, t], sF[:, :, :, t - 1], f[:, :, :, t], ALU.mult))
                at_ = 0
                for d in range(DT):
                    src = k if d == 0 else sE[:, H * (d % 2):H * (d % 2) + H]
                    if d:
                        prev = k if d == 1 else sE[:, H * ((d - 1) % 2):H * ((d - 1) % 2) + H]
                        link(V.tensor_tensor(src[:, :, :, d:DT], f[:, :, :, d:DT], prev[:, :, :, d - 1:DT - 1], ALU.mult))
                    V.tensor_copy(sK[:, :, :, DT - 1 - d], src[:, :, :, DT - 1])
                    w = DT - d
                    dst = pv_[0][:, at_:at_ + H * DB * w].rearrange("p (h b t) -> p h b t", h=H, t=w)
                    x = V.tensor_tensor(dst, src[:, :, :, d:DT], q[:, :, :, d:DT], ALU.mult)
                    if d < DT - 1:
                        link(x)
                    at_ += H * DB * w
                link(x, sh_p)
                dve.wait_ge(sh_p, 2 * l + 1)
                link(V.tensor_copy(f15.rearrange("p (h b) -> p h b", h=H), sF[:, :, :, DT - 1]))
                link(V.tensor_tensor(sF[:, :, :, :], sF[:, :, :, :], q, ALU.mult), sh_p)

            def sample_turned(l):
                i_ = i_h[:, :, S:TOK].rearrange("p h (b t) -> p h b t", t=DT)
                dve.wait_ge(sh_t, l + 1)
                dve.wait_ge(s_stored, 16 * H * (l + 1))
                V.tensor_copy(sitok, bank[6][0:NS, :])
                link(V.tensor_copy(sktok, bank[7][0:NS, :]))
                dve.wait_ge(sh_bcp, l + 1)
                at_ = 0
                for d in range(DT):
                    w = DT - d
                    src = bank[3][:, at_:at_ + H * DB * w].rearrange("p (h b t) -> p h b t", h=H, t=w)
                    if d == 0:
                        link(V.tensor_tensor(sA[:, :, :, :], src, i_, ALU.mult))
                    else:
                        link(V.tensor_tensor(sP[:, :, :, 0:w], src, i_[:, :, :, 0:w], ALU.mult))
                        link(V.tensor_tensor(sA[:, :, :, d:DT], sA[:, :, :, d:DT], sP[:, :, :, 0:w], ALU.add))
                    at_ += H * DB * w

            def sample_batch(l, b):
                B = l * DB + b
                if b >= 2:
                    dve.wait_ge(sh_ps, B - 1)
                if b >= 3:
                    dve.wait_ge(sh_st[b % 3], state_count(l, b - 3))
                link(V.tensor_scalar(smk[b % 2], sktok, con("batch", NS)[:, b:b + 1], None, ALU.mult), sh_m)
                dve.wait_ge(sh_ps, B + 1)
                for h in range(H):
                    x = V.scalar_tensor_tensor(s1[b % 3][:, h, :], s0[b % 3][:, h, :], f15[:, h * DB + b:h * DB + b + 1],
                                               bank[6 + b % 2][:, h * P:(h + 1) * P], ALU.mult, ALU.add)
                link(x, sh_s)
                if b == DB - 1:
                    o = oT[:, 0:H, S:TOK].rearrange("p h (b t) -> p h b t", t=DT)
                    link(V.tensor_tensor(o, sA[:, :, :, :], bank[3][:, 0:DB * H * DT].rearrange("p (b h t) -> p h b t", b=DB, h=H), ALU.add))
                    dve.wait_ge(sh_st[2], state_count(l, 5))
                    square(l, 0)

            def parts(n):
                if n < 4:
                    return oT[:, n, 0:S], g_h[:, n, 0:S]
                if n == 4:
                    return oT[:, 0:H, S:TOK], g_h[:, :, S:TOK]
                return oT[:, H:2 * H, S:TOK], None

            def flat(a, n):
                w = S if n < 4 else H * NS
                return a[:, 0:w] if n < 4 else a[:, 0:w].rearrange("p (h n) -> p h n", h=H)

            def square(l, n):
                g = 6 * l + n
                o, _ = parts(n)
                if n >= 2:
                    dve.wait_ge(nps, g - 1)
                link(V.tensor_tensor(flat(pv_[n % 2], n), o, o, ALU.mult), nsq)

            def feature_norm(l, n):
                g = 6 * l + n
                o, gt = parts(n)
                if n < H:
                    square(l, n + 1)
                dve.wait_ge(nrt, g + 1)
                e = flat(ev[n % 2], n)
                link(V.reciprocal(e, e))
                if n < 5:
                    link(V.scalar_tensor_tensor(o, o, hnw[:, l:l + 1], e, ALU.mult, ALU.mult))
                    link(V.tensor_tensor(o, o, gt, ALU.mult), o_ok)
                else:
                    link(V.scalar_tensor_tensor(o, o, dnw[:, l:l + 1], e, ALU.mult, ALU.mult), o_ok)

            def first_of(dst, x, m, t):
                b = lambda a: a.unsqueeze(2).to_broadcast([P, NT, 4])
                link(V.tensor_reduce(m, x, AX, ALU.max))
                link(V.tensor_tensor(dst, x, b(m), ALU.is_equal))
                link(V.tensor_tensor(dst, dst, con("prio").unsqueeze(1).to_broadcast([P, NT, 4]), ALU.mult))
                link(V.tensor_reduce(t, dst, AX, ALU.max))
                link(V.tensor_tensor(dst, dst, b(t), ALU.is_equal))

            def logits_out(l, i):
                r = rows(i)
                dve.wait_ge(lg_ps, NT * l + i + 1)
                link(V.tensor_tensor(lg[0:r, i, :], bank[4 + i % 2][0:r, 0:NG + NE], brt[0:r, l, :], ALU.add), lg_ok)

            def route(l):
                b = lambda a: a.unsqueeze(2).to_broadcast([P, NT, 4])
                lg1 = lg[:, :, 0:NG]
                lg2 = lg[:, :, NG:].rearrange("p i (g j) -> p i g j", g=NG)
                grp, o1, o2, lgg = r4[:, 1], r4[:, 2], r4[:, 3], r4[:, 4]
                first_of(grp, lg1, r1[:, 0], r1[:, 1])
                link(V.tensor_tensor(r4[:, 0], lg1, b(r1[:, 0]), ALU.subtract))
                of_group = grp.unsqueeze(3).to_broadcast([P, NT, 4, 4])
                link(V.tensor_tensor(r16[:, :, :, :], lg2, of_group, ALU.mult))
                link(V.tensor_reduce(lgg, r16.rearrange("p i g j -> p i j g"), AX, ALU.add))
                link(V.tensor_tensor(grp, grp, b(con("valid")), ALU.mult))
                first_of(o1, lgg, r1[:, 3], r1[:, 1])
                link(V.scalar_tensor_tensor(r4[:, 5], o1, NEG, lgg, ALU.mult, ALU.add))
                first_of(o2, r4[:, 5], r1[:, 4], r1[:, 1])
                link(V.tensor_tensor(r1[:, 2], r1[:, 4], r1[:, 3], ALU.subtract))
                link(V.tensor_copy(r1[:, 5], r1[:, 4]), lg_ok)
                for m, o in ((m1, o1), (m2, o2)):
                    link(V.tensor_tensor(m, of_group, o.unsqueeze(2).to_broadcast([P, NT, 4, 4]), ALU.mult))
                f1, f2 = (m.rearrange("p i g j -> p i (g j)") for m in (m1, m2))
                link(V.tensor_tensor(msk[:, :, :], f1, f2, ALU.add), msk_ok)
                dve.wait_ge(rexp, 2 * l + 2)
                link(V.tensor_reduce(r1[:, 0], r4[:, 0], AX, ALU.add))
                link(V.tensor_scalar(r1[:, 5], r1[:, 2], 1.0, None, ALU.add))
                link(V.tensor_tensor(r1[:, 0], r1[:, 0], r1[:, 5], ALU.mult))
                link(V.reciprocal(r1[:, 6], r1[:, 0]))
                link(V.tensor_tensor(r1[:, 7], r1[:, 6], r1[:, 2], ALU.mult))
                b16 = lambda a: a.unsqueeze(2).to_broadcast([P, NT, NE])
                t16 = r16.rearrange("p i g j -> p i (g j)")
                link(V.tensor_tensor(t16, f1, b16(r1[:, 6]), ALU.mult))
                link(V.tensor_tensor(psel[:, :, :], f2, b16(r1[:, 7]), ALU.mult))
                V.tensor_copy(tg[:, :, :, 0], b16(con("tokid")))
                link(V.tensor_tensor(tg[:, :, :, 1], t16, psel[:, :, :], ALU.add))
                dve.wait_ge(pos_ps, l + 1)
                link(V.tensor_copy(pos.rearrange("p i e -> p (i e)"), bank[6][:, 0:NT * NE]))
                link(V.scalar_tensor_tensor(psel[:, :, :], pos[:, :, :], 1.0, msk[:, :, :], ALU.add, ALU.mult))
                link(V.tensor_scalar(psel[:, :, :], psel[:, :, :], 1.0, None, ALU.subtract))
                link(V.tensor_copy(r1[:, 0], r1[:, 1]), psel_ok)

            def extra_plan(l):
                cnt = bank[6][:, NT * NE:(NT + 1) * NE]
                link(V.tensor_scalar(cntx[:, 0], cnt, float(P), None, ALU.is_gt))
                for k in range(2, NT):
                    link(V.scalar_tensor_tensor(cntx[:, 0], cnt, float(P * k), cntx[:, 0], ALU.is_gt, ALU.add))
                link(V.tensor_tensor_scan(cntx[:, 1], ones[:, 0:NE], cntx[:, 0], 0.0, ALU.mult, ALU.add))
                link(V.tensor_tensor(cntx[:, 2], cntx[:, 1], cntx[:, 0], ALU.subtract))
                it = iota[:, 0:MAXX].unsqueeze(2).to_broadcast([P, MAXX, NE])
                be = lambda a: a.unsqueeze(1).to_broadcast([P, MAXX, NE])
                link(V.tensor_tensor(ohx[:, :, :], it, be(cntx[:, 2]), ALU.is_ge))
                link(V.tensor_tensor(ohx2[:, :, :], it, be(cntx[:, 1]), ALU.is_lt))
                link(V.tensor_tensor(ohx[:, :, :], ohx[:, :, :], ohx2[:, :, :], ALU.mult))
                link(V.tensor_tensor(ohx2[:, :, :], ohx[:, :, :], be(cntx[:, 2]), ALU.mult))
                link(V.tensor_reduce(kx[:, :], ohx2[:, :, :], AX, ALU.add))
                link(V.tensor_tensor(kx[:, :], iota[:, 0:MAXX], kx[:, :], ALU.subtract))
                link(V.tensor_scalar(kx[:, :], kx[:, :], 1.0, float(P), ALU.add, ALU.mult))
                link(V.tensor_tensor(ohx2[:, :, :], ohx[:, :, :], be(iota[:, 0:NE]), ALU.mult))
                link(V.tensor_reduce(exf[:, :], ohx2[:, :, :], AX, ALU.add))
                link(V.tensor_copy(exi[:, :], exf[:, :]))
                link(V.tensor_copy(nxi[:, :], cntx[:, 1, NE - 1:NE]))

            def result_rows(l):
                f1, f2 = (m.rearrange("p i g j -> p i (g j)") for m in (m1, m2))
                t16 = r16.rearrange("p i g j -> p i (g j)")
                for k, f in enumerate((f1, f2)):
                    link(V.tensor_tensor(t16, f, pos[:, :, :], ALU.mult))
                    link(V.tensor_reduce(r1[:, 1], t16, AX, ALU.add))
                    link(V.tensor_tensor(t16, f, con("ebase").unsqueeze(1).to_broadcast([P, NT, NE]), ALU.mult))
                    link(V.tensor_reduce(rk[:, k], t16, AX, ALU.add))
                    link(V.tensor_tensor(rk[:, k], rk[:, k], r1[:, 1], ALU.add))
                    link(V.tensor_scalar(r1[:, 1], r1[:, 1], float(P), None, ALU.is_lt))
                    link(V.tensor_scalar(rk[:, k], rk[:, k], float(YROWS), None, ALU.subtract))
                    link(V.tensor_tensor(rk[:, k], rk[:, k], r1[:, 1], ALU.mult))
                    link(V.tensor_scalar(rk[:, k], rk[:, k], float(YROWS), None, ALU.add))
                link(V.tensor_copy(rki[:, :, :], rk[:, :, :]), rk_ok)

            def x_out(l, e):
                E_ = l * NE + e
                for j in range(2):
                    dve.wait_ge(xe_ps, 2 * E_ + j + 1)
                    link(V.tensor_tensor(xeT[e % 2][:, 4 * j:4 * j + 4, :], bank[j][:, :].rearrange("p (c n) -> p c n", c=4),
                                         nw[:, L + l, 4 * j:4 * j + 4].unsqueeze(2).to_broadcast([P, 4, P]), ALU.mult), xe_ok)

            def sel_build(l, e):
                E_ = l * NE + e
                if E_ >= 2:
                    dve.wait_ge(id_ps, E_ - 1)
                link(V.tensor_tensor(sels[e % 2], iota.unsqueeze(1).to_broadcast([P, NT, P]), psel[:, :, e].unsqueeze(2).to_broadcast([P, NT, P]),
                                ALU.is_equal), sel_ok)

            def ids_out(l, e):
                E_ = l * NE + e
                dve.wait_ge(id_ps, E_ + 1)
                V.tensor_copy(idx[:, e:e + 1], bank[7][:, 0:1])
                link(V.tensor_copy(gate[:, e:e + 1], bank[7][:, 1:2]), id_ok)

            for l in range(L):
                if l:
                    norm(2 * l)
                for n in range(15):
                    if n < 10:
                        rope(l, n)
                    if 1 <= n <= 10:
                        qk_out(l, n - 1)
                dve.wait_ge(fp_ok, 32 * l + 8)
                for h in range(H):
                    link(V.tensor_scalar(f_h[:, h, :], f_h[:, h, :], omlb[:, l, h:h + 1], lb[:, l, h:h + 1], ALU.mult, ALU.add))
                    V.tensor_scalar(k_h[:, h, :], k_h[:, h, :], omlb[:, l, h:h + 1], None, ALU.mult)
                    link(V.tensor_scalar(f_h[:, h, :], f_h[:, h, :], F_MIN, None, ALU.max), fk_ok)
                dve.wait_ge(fk_ok, H * (l + 1))
                for v in range(16 + 3):
                    if v < 16:
                        u, U = v, 16 * l + v
                        w = (u // H + 1) * P
                        dve.wait_ge(pa_qk, U + 1)
                        for c in range(2):
                            x = V.tensor_reduce(mx[:, u % 2, c:c + 1], bank[c + 2 * (u % 2)][:, 0:w], AX, ALU.max)
                        link(x)
                        link(V.tensor_scalar(mx[:, u % 2, :], mx[:, u % 2, :], -1.0, None, ALU.mult), pa_max)
                    if 1 <= v < 17:
                        u, U = v - 1, 16 * l + v - 1
                        w = (u // H + 1) * P
                        e0, e1 = (e_p[u % 2][c][:, 0:w] for c in range(2))
                        dve.wait_ge(pa_exp, U + 1)
                        r_ = rl[:, u % 4, :]
                        link(V.reciprocal(r_, ls[:, u % 2, :]))
                        link(V.scalar_tensor_tensor(r_[:, 1:2], r_[:, 1:2], nlam[:, l:l + 1], ls[:, u % 2, 0:1], ALU.mult, ALU.mult))
                        link(V.scalar_tensor_tensor(e1, e1, r_[:, 1:2], e0, ALU.mult, ALU.add), pa_comb)
                    if 3 <= v:
                        u, U = v - 3, 16 * l + v - 3
                        i, h = u // H, u % H
                        dve.wait_ge(pa_pv, U + 1)
                        if v == 3:
                            for k in range(3):
                                dve.wait_ge(st_k[k], 16 * (l + 1) * sum(1 for x_ in range(5, 10) if x_ % 3 == k))
                        link(V.tensor_scalar(od[:, i, h * HD:(h + 1) * HD], bank[6 + u % 2][:, 0:HD], rl[:, u % 4, 0:1], None, ALU.mult), pa_od)
                        dve.wait_ge(pa_od, U + 1)
                        o = od[:, i, h * HD:(h + 1) * HD]
                        x = V.tensor_tensor_reduce(odsq, o, o, 1.0, 0.0, ALU.mult, ALU.add, ssq16[:, i, h:h + 1])
                link(x, od_sq)
                dve.wait_ge(od_rt, l + 1)
                link(V.reciprocal(rt16[:, :, :], rt16[:, :, :]))
                for i in range(PT):
                    o = od[:, i, :].rearrange("p (h n) -> p h n", h=H)
                    link(V.tensor_tensor(o, o, rt16[:, i, :].unsqueeze(2).to_broadcast([P, H, HD]), ALU.mult), od_n)
                for i in range(PT):
                    dve.wait_ge(od_t, PT * l + i + 1)
                    link(V.tensor_scalar(oT[:, H:2 * H, tok(i)], bank[4 + i % 2][:, :].rearrange("p (h n) -> p h n", h=H),
                                    dnw[:, l:l + 1], None, ALU.mult), od_ok)
                queries(l, 0)
                dve.wait_ge(st_v, 16 * NT * (l + 1))
                for s in range(SLOTS):
                    if s % 4 == 0 and 1 <= s // 4 <= NQ:
                        scores_out(l, s // 4 - 1)
                        if s % NPG == 0:
                            max_out(l, s // NPG - 1)
                    b, k = s // NPG - 1, s % NPG
                    if k == 2 and b + 1 < DB:
                        new_out(l, b + 1)
                    if k == 8 and b + 2 < DB:
                        queries(l, b + 2)
                    if b >= 0:
                        if k == turns(b)[4] + 2:
                            o_rows(l, b)
                        if k == turns(b)[4] + 3:
                            o_out(l, b)
                    if s < len(items):
                        hgrn(l, items[s])
                square(l, H + 1)
                feature_norm(l, H + 1)
                for i in range(NT + 2):
                    if i < NT:
                        for k in range(2):
                            r = rows(i)
                            dve.wait_ge(wo_ps, 10 * l + 2 * i + k + 1)
                            hh_ = hid[0:r, i, k * WB:(k + 1) * WB]
                            link(V.tensor_tensor(hh_, hh_, bank[2 + k][0:r, :], ALU.add), wo_add)
                        norm_tile(2 * l + 1, i)
                    if 1 <= i <= NT:
                        norm_out(2 * l + 1, i - 1)
                    if i >= 2:
                        logits_out(l, i - 2)
                route(l)
                for e in range(2):
                    sel_build(l, e)
                for e in range(2):
                    ids_out(l, e)
                extra_plan(l)
                x_out(l, 0)
                result_rows(l)
                for e in range(NE):
                    if e + 2 < NE:
                        sel_build(l, e + 2)
                    E_ = l * NE + e
                    dve.wait_ge(si_ok, E_ + 1)
                    dve.wait_ge(gu_ps, 2 * E_ + 2)
                    if E_ >= 1:
                        dve.wait_ge(ht_ps, E_)
                    link(V.scalar_tensor_tensor(hgt, silu[e % 2], gate[:, e:e + 1], bank[3][:, :], ALU.mult, ALU.mult), hg_ok)
                    if e + 2 < NE:
                        ids_out(l, e + 2)
                    if e + 1 < NE:
                        x_out(l, e + 1)

                def extra(t):
                    P_, A_, V_ = t * XP["all"], t * XA["y"], t * XV["all"]
                    k = [0]

                    def step(ins):
                        k[0] += 1
                        ins.then_inc(xv[l], 1)
                        dve.wait_ge(xv[l], V_ + k[0])

                    t16 = r16.rearrange("p i g j -> p i (g j)")
                    oh = ohx[:, bass.ds(t, 1), :].to_broadcast([P, NT, NE])
                    step(V.tensor_tensor(t16, psel[:, :, :], oh, ALU.mult))
                    step(V.tensor_reduce(psx[:, :], t16, AX, ALU.add))
                    step(V.tensor_tensor(t16, tg[:, :, :, 1], oh, ALU.mult))
                    step(V.tensor_reduce(tgx[:, :, 1], t16, AX, ALU.add))
                    step(V.tensor_copy(tgx[:, :, 0], con("tokid")))
                    step(V.tensor_tensor(psx[:, :], psx[:, :], kx[:, bass.ds(t, 1)].to_broadcast([P, NT]), ALU.subtract))
                    step(V.tensor_tensor(sel, iota.unsqueeze(1).to_broadcast([P, NT, P]), psx[:, :].unsqueeze(2).to_broadcast([P, NT, P]), ALU.is_equal))
                    assert k[0] == XV["sel"]
                    dve.wait_ge(xp[l], P_ + XP["ids"])
                    step(V.tensor_copy(xid[:, :], bank[7][:, 0:1]))
                    step(V.tensor_copy(xidf[:, :], bank[7][:, 0:1]))
                    step(V.tensor_copy(xgt[:, :], bank[7][:, 1:2]))
                    assert k[0] == XV["ids"]
                    dve.wait_ge(xp[l], P_ + XP["x"])
                    for j in range(2):
                        step(V.tensor_tensor(xeT[0][:, 4 * j:4 * j + 4, :], bank[j][:, :].rearrange("p (c n) -> p c n", c=4),
                                             nw[:, L + l, 4 * j:4 * j + 4].unsqueeze(2).to_broadcast([P, 4, P]), ALU.mult))
                    assert k[0] == XV["x"]
                    dve.wait_ge(xa[l], A_ + XA["silu"])
                    step(V.scalar_tensor_tensor(hgt, silu[0], xgt[:, 0:1], bank[3][:, :], ALU.mult, ALU.mult))
                    assert k[0] == XV["h"]
                    for i in range(NT):
                        step(V.tensor_scalar(sel[:, i, :], iota, float(P * i), xidf[:, 0:1], ALU.add, ALU.is_equal))
                    assert k[0] == XV["back"]
                    for n in range(2):
                        dve.wait_ge(xp[l], P_ + XP["all"] - 1 + n)
                        for i in range(NT):
                            hh_ = hid[0:rows(i), i, n * WB:(n + 1) * WB]
                            step(V.tensor_tensor(hh_, hh_, bank[i][0:rows(i), :], ALU.add))
                    assert k[0] == XV["all"]
                extra_tiles(dve, l + 1, extra)

                for i in range(NT):
                    r = rows(i)
                    dve.wait_ge(yg_in[i], 32 * (l + 1))
                    for k in range(2):
                        link(V.tensor_tensor(hid[0:r, i, :], hid[0:r, i, :], yg[2 * i + k][0:r, :], ALU.add), moe_add)
            dve.wait_ge(fw_in, 16)
            for i in range(NT):
                r = rows(i)
                norm_tile(2 * L, i)
                link(V.scalar_tensor_tensor(hid[0:r, i, :], hid[0:r, i, :], rs[0:r, i:i + 1], xT_a[0:r, 0:D], ALU.mult, ALU.mult), out_ok)

        @block.gpsimd
        def _(pool):
            G = nc.gpsimd
            made = {}

            def link(ins, signal=pl):
                made[signal.name] = made.get(signal.name, 0) + 1
                ins.then_inc(signal, 1)
                pool.wait_ge(signal, made[signal.name])

            def hgrn(l, h):
                hh = l * H + h
                f, k, q = blk(f_h, h), blk(k_h, h), blk(q_h, h)
                kh = khat.rearrange("p (b c) -> p b c", c=C)
                Fb = Fq.rearrange("p (b c) -> p b c", c=C)
                if hh:
                    pool.wait_ge(hclose, hh)
                else:
                    pool.wait_ge(od_ok, PT)
                for d in range(C):
                    g = C * hh + d
                    src = k if d == 0 else ev[d % 2].rearrange("p (b c) -> p b c", c=C)
                    if d:
                        prev = k if d == 1 else ev[(d - 1) % 2].rearrange("p (b c) -> p b c", c=C)
                        if d >= 3:
                            pool.wait_ge(hQ if d % 2 else hP, C // 2 * hh + d // 2)
                        link(G.tensor_tensor(src[:, :, d:C], f[:, :, d:C], prev[:, :, d - 1:C - 1], ALU.mult))
                    link(G.tensor_copy(kh[:, :, C - 1 - d], src[:, :, C - 1]), hE)
                    if d % 2:
                        if d >= 3:
                            pool.wait_ge(hbc, g - 1)
                        w = C - d
                        link(G.tensor_tensor(pv_[1][:, 0:NB * w].rearrange("p (b c) -> p b c", c=w), src[:, :, d:C], q[:, :, d:C], ALU.mult), hQ)
                link(G.tensor_copy(Fb[:, :, 0], f[:, :, 0]))
                for t in range(1, C):
                    link(G.tensor_tensor(Fb[:, :, t], Fb[:, :, t - 1], f[:, :, t], ALU.mult))
                link(G.tensor_copy(f15, Fb[:, :, C - 1]))
                link(G.tensor_tensor(Fb, Fb, q, ALU.mult), hF)
                pool.wait_ge(hS, NB * (hh + 1))
                G.dma_start(t_out["s_prompt"][l, 0, h], sring[NB % NR]).then_inc(s_stored, 16)

            def y_store(l, e):
                E_ = l * NE + e
                pool.wait_ge(y_ok, 2 * E_ + 2)
                G.dma_start(y_d[e * P:(e + 1) * P, :], yt[e % 2]).then_inc(y_st[e % 2], 16)

            pool.wait_ge(par, 16 * NPAR)
            G.dma_start(y_d[YROWS, :].rearrange("(p n) -> p n", n=8), con("zero")).then_inc(zero_st, 16)
            for l in range(L):
                for n in range(5, 10):
                    i = n % NT
                    r = rows(i)
                    pool.wait_ge(roped, 10 * l + n + 1)
                    dst = (t_out["k_prompt"][l, 0, tok(i)] if i < PT else t_out["k_sample"][l].rearrange("b t h n -> (b t) h n"))
                    G.dma_start(dst.rearrange("t h n -> t (h n)"), qkt[n % 3][0:r, :]).then_inc(st_k[n % 3], 16)
                for i in range(NT):
                    r = rows(i)
                    pool.wait_ge(tp_ok, 15 * l + 10 + i + 1)
                    dst = (t_out["v_prompt"][l, 0, tok(i)] if i < PT else t_out["v_sample"][l].rearrange("b t h n -> (b t) h n"))
                    G.dma_start(dst.rearrange("t h n -> t (h n)"), vtok[0:r, i, :]).then_inc(st_v, 16)
                if l:
                    pool.wait_ge(od_ok, PT * (l + 1))
                for h in range(H):
                    hgrn(l, h)
                pool.wait_ge(hclose, H * (l + 1))
                for b in range(DB):
                    B = l * DB + b
                    if b >= 3:
                        pool.wait_ge(sh_s, B - 2)
                    G.dma_start(s0[b % 3], t_in["state_hgrn"][l, b].rearrange("h k v -> k h v")).then_inc(sh_in[b % 3], 16)
                    if b >= 1:
                        pool.wait_ge(sh_s, B)
                        G.dma_start(t_out["s_sample"][l, b - 1].rearrange("h k v -> k h v"), s1[(b - 1) % 3]).then_inc(sh_st[(b - 1) % 3], 16)
                pool.wait_ge(sh_s, (l + 1) * DB)
                G.dma_start(t_out["s_sample"][l, DB - 1].rearrange("h k v -> k h v"), s1[(DB - 1) % 3]).then_inc(sh_st[(DB - 1) % 3], 16)
                for i in range(NT):
                    r = rows(i)
                    pool.wait_ge(xn_ok, NT * (2 * l + 1) + i + 1)
                    if i:
                        pool.wait_ge(xn_st, 16 * (NT * l + i))
                    G.dma_start(xn_d[tok(i), :], xn[i % 2][0:r, :]).then_inc(xn_st, 16)
                pool.wait_ge(xn_st, 16 * NT * (l + 1))
                pool.wait_ge(st_v, 16 * NT * (l + 1))
                for b in range(DB - 3, DB):
                    pool.wait_ge(sh_st[b % 3], state_count(l, b))
                for e in range(NE):
                    E_ = l * NE + e
                    pool.wait_ge(id_ok, E_ + 1)
                    if e >= 2:
                        pool.wait_ge(xe_ps, 2 * (E_ - 1))
                    G.indirect_dma_start(out=xe[e % 2], out_offset=None, in_=xn_d,
                                         in_offset=bass.IndirectOffsetOnAxis(ap=idx[:, e:e + 1], axis=0)).then_inc(xe_in[e % 2], 16)
                    if e >= 2:
                        y_store(l, e - 2)
                for e in range(NE - 2, NE):
                    y_store(l, e)

                def extra(t):
                    pool.wait_ge(xv[l], t * XV["all"] + XV["ids"])
                    pool.sem_inc(passed, 1)
                    G.indirect_dma_start(out=xe[0], out_offset=None, in_=xn_d,
                                         in_offset=bass.IndirectOffsetOnAxis(ap=xid[:, 0:1], axis=0)).then_inc(xg[l], 16)
                    pool.wait_ge(xv[l], t * XV["all"] + XV["all"])
                extra_tiles(pool, l + 1, extra)
                for b in range(2):
                    pool.wait_ge(y_st[b], 16 * (NE // 2) * (l + 1))
                pool.wait_ge(zero_st, 16)
                for q in range(2 * NT):
                    i, k = q // 2, q % 2
                    r = rows(i)
                    G.indirect_dma_start(out=yg[q][0:r, :], out_offset=None, in_=y_d,
                                         in_offset=bass.IndirectOffsetOnAxis(ap=rki[0:r, k, i:i + 1], axis=0)).then_inc(yg_in[i], 16)
            for i in range(NT):
                r = rows(i)
                pool.wait_ge(out_ok, i + 1)
                dst = t_out["y_prompt"][0, tok(i), :] if i < PT else t_out["y_sample"].rearrange("b t d -> (b t) d")
                G.dma_start(dst, hid[0:r, i, :]).then_inc(out_st, 16)
            pool.wait_ge(out_st, 16 * NT)
            pool.wait_ge(st_v, 16 * NT * L)
            pool.wait_ge(s_stored, 16 * H * L)
            for k in range(3):
                pool.wait_ge(st_k[k], 16 * L * sum(1 for x in range(5, 10) if x % 3 == k))
            for b in range(DB - 3, DB):
                pool.wait_ge(sh_st[b % 3], state_count(L - 1, b))


_INS = ["x_prompt", "x_sample", "cache_k", "cache_v", "state_hgrn", "page_table", "attn_norm_w", "w_in", "hgrn_lb",
        "hgrn_norm_w", "diff_lambda", "diff_norm_w", "w_o", "ffn_norm_w", "w_r1", "b_r1", "w_r2", "b_r2",
        "w_gate", "w_up", "w_down", "final_norm_w"]
_OUTS = {"y_prompt": (1, S, D), "y_sample": (DB, DT, D), "k_prompt": (L, 1, S, H, HD), "v_prompt": (L, 1, S, H, HD),
         "s_prompt": (L, 1, H, HD, HD), "k_sample": (L, DB, DT, H, HD), "v_sample": (L, DB, DT, H, HD),
         "s_sample": (L, DB, H, HD, HD)}


def kernel(**inputs):
    import concourse.bacc as bacc
    from concourse.bass_utils import run_bass_kernel_spmd

    nc = bacc.Bacc("TRN2", target_bir_lowering=False, num_devices=1)
    arrays, t_in, t_out = {}, {}, {}
    for name in _INS:
        a = np.ascontiguousarray(inputs[name])
        arrays[f"in_{name}"] = a
        t_in[name] = nc.dram_tensor(f"in_{name}", a.shape, mybir.dt.from_np(a.dtype), kind="ExternalInput").ap()
    c = constants()[0]
    arrays["in_constants"] = c
    t_in["constants"] = nc.dram_tensor("in_constants", c.shape, F32, kind="ExternalInput").ap()
    for name, shape in _OUTS.items():
        t_out[name] = nc.dram_tensor(f"out_{name}", shape, F32, kind="ExternalOutput").ap()
    build(nc, t_in, t_out)
    r = run_bass_kernel_spmd(nc, [arrays], core_ids=[0])
    return tuple(r.results[0][f"out_{name}"] for name in _OUTS)
```
